# Optimizing a Trainium2 kernel written in Bass

```python
import math
import jax, jax.numpy as jnp
from jax import lax
import numpy as np

D_MODEL = 1024
BATCH = 1
SEQ = 256
DEPTH = 2

M_HEADS = 4
M_QK_DIM = 128
M_V_DIM = 256
M_QK_WIDTH = M_HEADS * M_QK_DIM
M_V_WIDTH = M_HEADS * M_V_DIM
M_CHUNK = 64
CONV_K = 4
A_Q_HEADS = 16
A_KV_HEADS = 4
A_HEAD_DIM = 64
A_GROUP = A_Q_HEADS // A_KV_HEADS
A_Q_WIDTH = A_Q_HEADS * A_HEAD_DIM
A_KV_WIDTH = A_KV_HEADS * A_HEAD_DIM
WINDOW = 128
N_BUCKETS = 32
MAX_DISTANCE = 128
D_FF = 4 * D_MODEL
EPS = 1e-6

IN_SIZES = (2 * M_QK_WIDTH, M_V_WIDTH, M_V_WIDTH, M_HEADS, M_HEADS,
            A_Q_WIDTH, A_KV_WIDTH, A_KV_WIDTH, D_MODEL, D_MODEL)
N_IN = sum(IN_SIZES)


def rmsnorm(x, g):
    xf = x.astype(jnp.float32)
    y = xf * lax.rsqrt(jnp.mean(xf * xf, axis=-1, keepdims=True) + EPS)
    return (y * g.astype(jnp.float32)).astype(x.dtype)

def t5_bucket(n):
    max_exact = N_BUCKETS // 2
    n = np.maximum(n, 0)
    large = max_exact + (np.log(np.maximum(n, 1) / max_exact)
                         / np.log(MAX_DISTANCE / max_exact)
                         * (N_BUCKETS - max_exact)).astype(np.int32)
    large = np.minimum(large, N_BUCKETS - 1)
    return np.where(n < max_exact, n, large).astype(np.int32)

def causal_conv(x, w, b):
    S = x.shape[1]
    xp = jnp.pad(x, ((0, 0), (CONV_K - 1, 0), (0, 0)))
    y = b
    for j in range(CONV_K):
        y = y + xp[:, j:j + S] * w[j]
    return y

def mlstm_chunkwise(q, k, v, ig, logf):
    B, S, H, dk = q.shape
    dv = v.shape[-1]
    L = M_CHUNK
    NC = S // L

    def chunks4(t):
        return t.reshape(B, NC, L, H, t.shape[-1]).transpose(1, 0, 3, 2, 4)

    def chunks3(t):
        return t.reshape(B, NC, L, H).transpose(1, 0, 3, 2)

    tril = jnp.tril(jnp.ones((L, L), dtype=bool))

    def step(carry, xs):
        C, n, m = carry
        qc, kc, vc, ic, fc = xs
        b = jnp.cumsum(fc, axis=-1)
        dmat = jnp.where(tril, b[..., :, None] - b[..., None, :] + ic[..., None, :], -jnp.inf)
        m_inter = b + m[..., None]
        m_comb = jnp.maximum(m_inter, jnp.max(dmat, axis=-1))
        w_intra = jnp.exp(dmat - m_comb[..., None])
        w_inter = jnp.exp(m_inter - m_comb)
        s = jnp.einsum('bhld,bhsd->bhls', qc, kc) * w_intra
        num = (jnp.einsum('bhls,bhsv->bhlv', s, vc)
               + w_inter[..., None] * jnp.einsum('bhld,bhdv->bhlv', qc, C))
        den = jnp.sum(s, axis=-1) + w_inter * jnp.einsum('bhld,bhd->bhl', qc, n)
        h = num / jnp.maximum(jnp.abs(den), jnp.exp(-m_comb))[..., None]
        bL = b[..., -1]
        g = bL[..., None] - b + ic
        m_new = jnp.maximum(bL + m, jnp.max(g, axis=-1))
        decay = jnp.exp(bL + m - m_new)
        wk = jnp.exp(g - m_new[..., None])
        C_new = decay[..., None, None] * C + jnp.einsum('bhl,bhld,bhlv->bhdv', wk, kc, vc)
        n_new = decay[..., None] * n + jnp.einsum('bhl,bhld->bhd', wk, kc)
        return (C_new, n_new, m_new), h

    init = (jnp.zeros((B, H, dk, dv), jnp.float32),
            jnp.zeros((B, H, dk), jnp.float32),
            jnp.zeros((B, H), jnp.float32))
    _, hs = lax.scan(step, init, (chunks4(q), chunks4(k), chunks4(v), chunks3(ig), chunks3(logf)))
    return hs.transpose(1, 0, 3, 2, 4).reshape(B, S, H, dv)

def sliding_window_attention(q, k, v, sinks, rel_bias):
    B, S = q.shape[:2]
    W = WINDOW
    NB = S // W
    qb = q.astype(jnp.float32).reshape(B, NB, W, A_KV_HEADS, A_GROUP, A_HEAD_DIM)
    kb = k.astype(jnp.float32).reshape(B, NB, W, A_KV_HEADS, A_HEAD_DIM)
    vb = v.astype(jnp.float32).reshape(B, NB, W, A_KV_HEADS, A_HEAD_DIM)

    def with_prev(t):
        prev = jnp.concatenate([jnp.zeros_like(t[:, :1]), t[:, :-1]], axis=1)
        return jnp.concatenate([prev, t], axis=2)

    k_ctx, v_ctx = with_prev(kb), with_prev(vb)
    scores = jnp.einsum('bnqhgd,bnkhd->bnhgqk', qb, k_ctx) * (A_HEAD_DIM ** -0.5)

    dist = np.arange(W)[:, None] + W - np.arange(2 * W)[None, :]
    bias = rel_bias.astype(jnp.float32)[t5_bucket(dist)]
    bias = bias.transpose(2, 0, 1).reshape(A_KV_HEADS, A_GROUP, W, 2 * W)
    valid_rel = jnp.asarray((dist >= 0) & (dist < W))
    kpos = jnp.arange(NB)[:, None, None] * W - W + jnp.arange(2 * W)[None, None, :]
    valid = valid_rel[None] & (kpos >= 0)
    logits = jnp.where(valid[None, :, None, None], scores + bias, -jnp.inf)

    sink = sinks.astype(jnp.float32).reshape(A_KV_HEADS, A_GROUP, 1)
    m = jnp.maximum(jnp.max(logits, axis=-1), sink)
    p = jnp.exp(logits - m[..., None])
    denom = jnp.sum(p, axis=-1) + jnp.exp(sink - m)
    out = jnp.einsum('bnhgqk,bnkhd->bnqhgd', p / denom[..., None], v_ctx)
    return out.reshape(B, S, A_Q_WIDTH).astype(q.dtype)

def mixer_block(h, w_in, conv_w, conv_b, b_igate, b_fgate, mlstm_norm_g, sinks,
                rel_bias, w_branch_m, w_branch_a, w_out):
    B, S, _ = h.shape
    proj = h @ w_in
    offsets = [int(o) for o in np.cumsum(IN_SIZES)[:-1]]
    mqk, mv, mo, mi, mf, aq, ak, av, ga, gb = jnp.split(proj, offsets, axis=-1)

    mqk = jax.nn.silu(causal_conv(mqk, conv_w, conv_b))
    mq, mk = jnp.split(mqk.astype(jnp.float32), 2, axis=-1)
    mq = mq.reshape(B, S, M_HEADS, M_QK_DIM) * (M_QK_DIM ** -0.5)
    mk = mk.reshape(B, S, M_HEADS, M_QK_DIM)
    mvf = mv.astype(jnp.float32).reshape(B, S, M_HEADS, M_V_DIM)
    ig = mi.astype(jnp.float32) + b_igate.astype(jnp.float32)
    logf = jax.nn.log_sigmoid(mf.astype(jnp.float32) + b_fgate.astype(jnp.float32))
    hm = mlstm_chunkwise(mq, mk, mvf, ig, logf)
    hm = hm * lax.rsqrt(jnp.mean(hm * hm, axis=-1, keepdims=True) + EPS)
    hm = hm * mlstm_norm_g.astype(jnp.float32).reshape(M_HEADS, M_V_DIM)
    hm = (hm.reshape(B, S, M_V_WIDTH) * jax.nn.sigmoid(mo.astype(jnp.float32))).astype(h.dtype)

    ha = sliding_window_attention(aq.reshape(B, S, A_Q_HEADS, A_HEAD_DIM),
                                  ak.reshape(B, S, A_KV_HEADS, A_HEAD_DIM),
                                  av.reshape(B, S, A_KV_HEADS, A_HEAD_DIM),
                                  sinks, rel_bias)

    y = jax.nn.sigmoid(ga) * (hm @ w_branch_m) + jax.nn.sigmoid(gb) * (ha @ w_branch_a)
    return y @ w_out

def sqrelu_mlp(h, w_up, w_down):
    return jnp.square(jax.nn.relu(h @ w_up)) @ w_down

def first_inputs(seed: int = 0) -> dict:
    key = jax.random.key(seed)
    ks = jax.random.split(key, 20)
    f32 = jnp.float32
    nrm = lambda k, shape, s: jax.random.normal(k, shape, f32) * s
    return {
        "x": nrm(ks[0], (BATCH, SEQ, D_MODEL), 1.0),
        "norm_mix_g": 1.0 + nrm(ks[1], (DEPTH, D_MODEL), 0.05),
        "w_in": nrm(ks[2], (DEPTH, D_MODEL, N_IN), D_MODEL ** -0.5),
        "conv_w": nrm(ks[3], (DEPTH, CONV_K, 2 * M_QK_WIDTH), CONV_K ** -0.5),
        "conv_b": nrm(ks[4], (DEPTH, 2 * M_QK_WIDTH), 0.02),
        "b_igate": nrm(ks[5], (DEPTH, M_HEADS), 0.1),
        "b_fgate": jnp.linspace(3.0, 6.0, M_HEADS, dtype=f32)[None] + nrm(ks[6], (DEPTH, M_HEADS), 0.1),
        "mlstm_norm_g": 1.0 + nrm(ks[7], (DEPTH, M_V_WIDTH), 0.05),
        "attn_sinks": nrm(ks[8], (DEPTH, A_Q_HEADS), 0.5),
        "rel_bias": nrm(ks[9], (N_BUCKETS, A_Q_HEADS), 0.5),
        "w_branch_m": nrm(ks[10], (DEPTH, M_V_WIDTH, D_MODEL), M_V_WIDTH ** -0.5),
        "w_branch_a": nrm(ks[11], (DEPTH, A_Q_WIDTH, D_MODEL), A_Q_WIDTH ** -0.5),
        "w_out": nrm(ks[12], (DEPTH, D_MODEL, D_MODEL), D_MODEL ** -0.5),
        "norm_mlp_g": 1.0 + nrm(ks[13], (DEPTH, D_MODEL), 0.05),
        "w_up": nrm(ks[14], (DEPTH, D_MODEL, D_FF), D_MODEL ** -0.5),
        "w_down": nrm(ks[15], (DEPTH, D_FF, D_MODEL), D_FF ** -0.5),
        "final_norm_g": 1.0 + nrm(ks[16], (D_MODEL,), 0.05),
    }

def first_block(x, norm_mix_g, w_in, conv_w, conv_b, b_igate, b_fgate, mlstm_norm_g,
              attn_sinks, rel_bias, w_branch_m, w_branch_a, w_out, norm_mlp_g,
              w_up, w_down, final_norm_g):
    for l in range(DEPTH):
        h = rmsnorm(x, norm_mix_g[l])
        x = x + mixer_block(h, w_in[l], conv_w[l], conv_b[l], b_igate[l], b_fgate[l],
                            mlstm_norm_g[l], attn_sinks[l], rel_bias,
                            w_branch_m[l], w_branch_a[l], w_out[l])
        h = rmsnorm(x, norm_mlp_g[l])
        x = x + sqrelu_mlp(h, w_up[l], w_down[l])
    return rmsnorm(x, final_norm_g)


DEPTH_2 = 1

HEAD_DIM = 64
N_HEADS_MOBA = 8
N_HEADS_SB = 8
W_MOBA = N_HEADS_MOBA * HEAD_DIM
W_SB = N_HEADS_SB * HEAD_DIM
MOBA_BLOCK = 256
MOBA_TOPK = 3
Q_CHUNK = 128
PEER_HEADS = 8
PEER_NKEYS = 128
PEER_N_EXPERTS = PEER_NKEYS * PEER_NKEYS
PEER_QDIM = 256
PEER_HALF = PEER_QDIM // 2
PEER_TOPK = 16
PEER_TOK_CHUNK = 128
RMS_EPS = 1e-6
IN_SPLITS = [W_MOBA, W_MOBA, W_MOBA, W_SB, W_SB, W_SB, D_MODEL, D_MODEL]
IN_WIDTH = sum(IN_SPLITS)


def rmsnorm_2(x, g):
    xf = x.astype(jnp.float32)
    y = xf * lax.rsqrt(jnp.mean(xf * xf, axis=-1, keepdims=True) + RMS_EPS)
    return (y * g.astype(jnp.float32)).astype(x.dtype)

def alibi_slopes(n_heads):
    return jnp.exp2(-8.0 * jnp.arange(1, n_heads + 1, dtype=jnp.float32) / n_heads)

def _heads(t, n):
    b, s, _ = t.shape
    return t.reshape(b, s, n, HEAD_DIM).transpose(0, 2, 1, 3)

def _merge(t):
    b, h, s, dh = t.shape
    return t.transpose(0, 2, 1, 3).reshape(b, s, h * dh)

def moba_attention(q, k, v):
    B, H, S, dh = q.shape
    nb = -(-S // MOBA_BLOCK)
    pad = nb * MOBA_BLOCK - S
    kp = jnp.pad(k, ((0, 0), (0, 0), (0, pad), (0, 0)))
    vp = jnp.pad(v, ((0, 0), (0, 0), (0, pad), (0, 0)))
    kb = kp.reshape(B, H, nb, MOBA_BLOCK, dh)
    vb = vp.reshape(B, H, nb, MOBA_BLOCK, dh)
    kmean = jnp.mean(kb.astype(jnp.float32), axis=3)
    ksel = min(MOBA_TOPK, nb)
    scale = dh ** -0.5
    slope = alibi_slopes(H).reshape(1, H, 1, 1)
    slope5 = slope[..., None]
    bidx = jnp.arange(B)[:, None, None, None]
    hidx = jnp.arange(H)[None, :, None, None]
    n_chunks = S // Q_CHUNK
    qc = q.reshape(B, H, n_chunks, Q_CHUNK, dh).transpose(2, 0, 1, 3, 4)

    def chunk(args):
        q_blk, c = args
        qf = q_blk.astype(jnp.float32)
        t = c * Q_CHUNK + jnp.arange(Q_CHUNK)
        own = (c * Q_CHUNK) // MOBA_BLOCK
        bs = jnp.einsum('bhqd,bhnd->bhqn', qf, kmean)
        bs = jnp.where(jnp.arange(nb) < own, bs, -jnp.inf)
        _, top_i = lax.top_k(bs, ksel)
        valid = top_i < own
        k_sel = kb[bidx, hidx, top_i].astype(jnp.float32)
        v_sel = vb[bidx, hidx, top_i].astype(jnp.float32)
        s_pos = top_i[..., None] * MOBA_BLOCK + jnp.arange(MOBA_BLOCK)
        dist_sel = (t[:, None, None] - s_pos).astype(jnp.float32)
        sc_sel = jnp.einsum('bhqd,bhqnkd->bhqnk', qf, k_sel) * scale - slope5 * dist_sel
        sc_sel = jnp.where(valid[..., None], sc_sel, -jnp.inf).reshape(B, H, Q_CHUNK, ksel * MOBA_BLOCK)
        k_own = lax.dynamic_slice_in_dim(kp, own * MOBA_BLOCK, MOBA_BLOCK, axis=2).astype(jnp.float32)
        v_own = lax.dynamic_slice_in_dim(vp, own * MOBA_BLOCK, MOBA_BLOCK, axis=2).astype(jnp.float32)
        s_own = own * MOBA_BLOCK + jnp.arange(MOBA_BLOCK)
        dist_own = (t[:, None] - s_own[None, :]).astype(jnp.float32)
        sc_own = jnp.einsum('bhqd,bhkd->bhqk', qf, k_own) * scale - slope * dist_own
        sc_own = jnp.where(s_own[None, :] <= t[:, None], sc_own, -jnp.inf)
        p = jax.nn.softmax(jnp.concatenate([sc_sel, sc_own], axis=-1), axis=-1)
        p_sel = p[..., :ksel * MOBA_BLOCK].reshape(B, H, Q_CHUNK, ksel, MOBA_BLOCK)
        p_own = p[..., ksel * MOBA_BLOCK:]
        o = (jnp.einsum('bhqnk,bhqnkd->bhqd', p_sel, v_sel)
             + jnp.einsum('bhqk,bhkd->bhqd', p_own, v_own))
        return o.astype(q.dtype)

    out = lax.map(chunk, (qc, jnp.arange(n_chunks)))
    return out.transpose(1, 2, 0, 3, 4).reshape(B, H, S, dh)

def stick_breaking_attention(q, k, v):
    B, H, S, dh = q.shape
    scale = dh ** -0.5
    kf = k.astype(jnp.float32)
    vf = v.astype(jnp.float32)
    s_idx = jnp.arange(S)
    n_chunks = S // Q_CHUNK
    qc = q.reshape(B, H, n_chunks, Q_CHUNK, dh).transpose(2, 0, 1, 3, 4)

    def chunk(args):
        q_blk, c = args
        t = c * Q_CHUNK + jnp.arange(Q_CHUNK)
        z = jnp.einsum('bhqd,bhkd->bhqk', q_blk.astype(jnp.float32), kf) * scale
        strict = s_idx[None, :] < t[:, None]
        log_1m = jnp.where(strict, jax.nn.log_sigmoid(-z), 0.0)
        suffix = lax.cumsum(log_1m, axis=3, reverse=True) - log_1m
        w = jnp.where(strict, jnp.exp(jax.nn.log_sigmoid(z) + suffix), 0.0)
        return jnp.einsum('bhqk,bhkd->bhqd', w, vf).astype(q.dtype)

    out = lax.map(chunk, (qc, jnp.arange(n_chunks)))
    return out.transpose(1, 2, 0, 3, 4).reshape(B, H, S, dh)

def peer_ffn(x, w_q, sub_keys, expert_u, expert_v):
    B, S, D = x.shape
    T = B * S
    xt = x.reshape(T // PEER_TOK_CHUNK, PEER_TOK_CHUNK, D)
    skf = sub_keys.astype(jnp.float32)

    def chunk(x_blk):
        tc = x_blk.shape[0]
        qh = (x_blk @ w_q).astype(jnp.float32).reshape(tc, PEER_HEADS, 2, PEER_HALF)
        scores = jnp.einsum('thpc,hpnc->thpn', qh, skf)
        s_top, i_top = lax.top_k(scores, PEER_TOPK)
        cand = s_top[:, :, 0, :, None] + s_top[:, :, 1, None, :]
        cand_idx = i_top[:, :, 0, :, None] * PEER_NKEYS + i_top[:, :, 1, None, :]
        c_s, c_pos = lax.top_k(cand.reshape(tc, PEER_HEADS, PEER_TOPK * PEER_TOPK), PEER_TOPK)
        e_idx = jnp.take_along_axis(cand_idx.reshape(tc, PEER_HEADS, PEER_TOPK * PEER_TOPK), c_pos, axis=-1)
        g = jax.nn.softmax(c_s, axis=-1)
        u = expert_u[e_idx].astype(jnp.float32)
        v = expert_v[e_idx].astype(jnp.float32)
        a = jax.nn.gelu(jnp.einsum('td,thkd->thk', x_blk.astype(jnp.float32), u), approximate=False)
        return jnp.einsum('thk,thkd->td', g * a, v).astype(x.dtype)

    return lax.map(chunk, xt).reshape(B, S, D)

def second_inputs(seed: int = 0) -> dict:
    key = jax.random.key(seed)
    ks = jax.random.split(key, 12)
    f32 = jnp.float32
    x = jax.random.normal(ks[0], (BATCH, SEQ, D_MODEL), f32)
    norm1_g = 1.0 + 0.01 * jax.random.normal(ks[1], (DEPTH_2, D_MODEL), f32)
    w_in = jax.random.normal(ks[2], (DEPTH_2, D_MODEL, IN_WIDTH), f32) * D_MODEL ** -0.5
    w_out_moba = jax.random.normal(ks[3], (DEPTH_2, W_MOBA, D_MODEL), f32) * W_MOBA ** -0.5
    w_out_sb = jax.random.normal(ks[4], (DEPTH_2, W_SB, D_MODEL), f32) * W_SB ** -0.5
    w_mix_out = jax.random.normal(ks[5], (DEPTH_2, D_MODEL, D_MODEL), f32) * D_MODEL ** -0.5
    norm2_g = 1.0 + 0.01 * jax.random.normal(ks[6], (DEPTH_2, D_MODEL), f32)
    peer_w_q = jax.random.normal(ks[7], (DEPTH_2, D_MODEL, PEER_HEADS * PEER_QDIM), f32) * D_MODEL ** -0.5
    peer_sub_keys = jax.random.normal(ks[8], (DEPTH_2, PEER_HEADS, 2, PEER_NKEYS, PEER_HALF), f32) * PEER_HALF ** -0.5
    peer_u = jax.random.normal(ks[9], (DEPTH_2, PEER_N_EXPERTS, D_MODEL), f32) * D_MODEL ** -0.5
    peer_v = jax.random.normal(ks[10], (DEPTH_2, PEER_N_EXPERTS, D_MODEL), f32) * PEER_HEADS ** -0.5
    final_norm_g = 1.0 + 0.01 * jax.random.normal(ks[11], (D_MODEL,), f32)
    return {"x": x, "norm1_g": norm1_g, "w_in": w_in, "w_out_moba": w_out_moba,
            "w_out_sb": w_out_sb, "w_mix_out": w_mix_out, "norm2_g": norm2_g,
            "peer_w_q": peer_w_q, "peer_sub_keys": peer_sub_keys, "peer_u": peer_u,
            "peer_v": peer_v, "final_norm_g": final_norm_g}

def second_block(x, norm1_g, w_in, w_out_moba, w_out_sb, w_mix_out, norm2_g,
              peer_w_q, peer_sub_keys, peer_u, peer_v, final_norm_g):
    split_at = [int(i) for i in np.cumsum(IN_SPLITS)[:-1]]
    h = x
    for l in range(DEPTH_2):
        xn = rmsnorm_2(h, norm1_g[l])
        proj = xn @ w_in[l]
        q_a, k_a, v_a, q_b, k_b, v_b, gate_a, gate_b = jnp.split(proj, split_at, axis=-1)
        y_a = _merge(moba_attention(_heads(q_a, N_HEADS_MOBA), _heads(k_a, N_HEADS_MOBA),
                                    _heads(v_a, N_HEADS_MOBA))) @ w_out_moba[l]
        y_b = _merge(stick_breaking_attention(_heads(q_b, N_HEADS_SB), _heads(k_b, N_HEADS_SB),
                                              _heads(v_b, N_HEADS_SB))) @ w_out_sb[l]
        mixed = jax.nn.sigmoid(gate_a) * y_a + jax.nn.sigmoid(gate_b) * y_b
        h = h + mixed @ w_mix_out[l]
        h = h + peer_ffn(rmsnorm_2(h, norm2_g[l]), peer_w_q[l], peer_sub_keys[l], peer_u[l], peer_v[l])
    return rmsnorm_2(h, final_norm_g)


def setup_inputs(seed=0):
    out = dict(first_inputs(seed))
    for name, value in second_inputs(seed + 1).items():
        if name != "x":
            out[name + "_2"] = value
    return out


def reference(
    x, norm_mix_g, w_in, conv_w, conv_b, b_igate, b_fgate, mlstm_norm_g, attn_sinks, rel_bias,
    w_branch_m, w_branch_a, w_out, norm_mlp_g, w_up, w_down, final_norm_g, norm1_g_2, w_in_2,
    w_out_moba_2, w_out_sb_2, w_mix_out_2, norm2_g_2, peer_w_q_2, peer_sub_keys_2, peer_u_2,
    peer_v_2, final_norm_g_2,
):
    x = first_block(
        x, norm_mix_g, w_in, conv_w, conv_b, b_igate, b_fgate, mlstm_norm_g, attn_sinks,
        rel_bias, w_branch_m, w_branch_a, w_out, norm_mlp_g, w_up, w_down, final_norm_g,
    )
    return second_block(
        x, norm1_g_2, w_in_2, w_out_moba_2, w_out_sb_2, w_mix_out_2, norm2_g_2, peer_w_q_2,
        peer_sub_keys_2, peer_u_2, peer_v_2, final_norm_g_2,
    )


_drawn_inputs = setup_inputs


def setup_inputs(seed=0):
    import zlib

    import numpy as np

    out = dict(_drawn_inputs(seed))
    spreads = {}
    factors = {'conv_b': 3.53,
     'b_igate': 64.0,
     'attn_sinks': 3.911,
     'norm1_g_2': 3.935,
     'norm2_g_2': 17.102,
     'final_norm_g_2': 27.971}
    for name, (base, spread) in spreads.items():
        noise = np.random.default_rng([zlib.crc32(name.encode()), seed]).standard_normal(out[name].shape)
        drawn = base * np.exp(spread * noise) if base else spread * noise
        out[name] = __import__('jax').numpy.asarray(drawn.astype(out[name].dtype))
    for name, factor in factors.items():
        out[name] = (out[name] * factor).astype(out[name].dtype)
    return out
```

```python
from contextlib import ExitStack

import numpy as np

import concourse.bass as bass
from concourse import mybir

F32 = mybir.dt.float32
F32R = mybir.dt.float32r
U32 = mybir.dt.uint32
I32 = mybir.dt.int32
ALU = mybir.AluOpType
ACT = mybir.ActivationFunctionType
X = mybir.AxisListType.X

P = 128
D, SEQ, DEPTH = 1024, 256, 2
TT = SEQ // P
KT = D // P
EPS = 1e-6
NEG = -1.0e30
LOWEST = -3.0e38

M_HEADS, M_DK, M_DV = 4, 128, 256
A_HEADS, A_KV, A_DH = 16, 4, 64
GROUP = A_HEADS // A_KV
WINDOW, N_BUCKETS, MAX_DISTANCE = 128, 32, 128
CONV_K = 4
D_FF = 4 * D
COL_MQK, COL_MV, COL_MO, COL_MI, COL_MF = 0, 1024, 2048, 3072, 3076
COL_AQ, COL_AK, COL_AV, COL_GA, COL_GB = 3080, 4104, 4360, 4616, 5640

H2, DH2 = 8, 64
W2 = H2 * DH2
P_HEADS, P_KEYS, P_TOP = 8, 128, 16
HP = 2 * P_HEADS
SLOTS = P_HEADS * P_TOP
N_EXPERTS = P_KEYS * P_KEYS

RING = 3
RAW_RING = 2
UNIT = 2048
GATE_F = 64
GATHER = 8
HALF = GATHER // 2
ROUNDS = SLOTS // GATHER


SIGNALS = {
    "consts": "a constant has been made", "x_loaded": "the tokens are here", "params_loaded": "a small parameter is here",
    "start_done": "the parameters stand in columns, in PSUM", "start_taken": "and in memory",
    "toep_ready": "the window's biases by distance are made", "toep_stored": "and in DRAM, once for each query",
    "bias_loaded": "the window's biases are here, shifted by one for each query",
    "hi_ready": "a unit's rounded part is made", "lo_ready": "and the rest of it: its raw slot is free",
    "unit_done": "TensorE is through with a unit", "emptied_act": "ScalarE has emptied a product's bank",
    "emptied_dve": "VectorE has emptied a product's bank",
    "ssq_ready": "a tile's sums of squares", "ms_ready": "those with eps", "rstd_ready": "one over their root",
    "hn_ready": "a tile is normed", "turned": "a tile of features is transposed, in PSUM",
    "x_hi": "its rounded part is made", "x_lo": "and the rest of it",
    "gate_loaded": "the gates' weights are here", "gate_hi": "their rounded part", "gate_lo": "and the rest",
    "gate_done": "their product", "gate_in": "with its bias", "gate_nabs": "minus |forget gate|", "gate_exp": "its exp",
    "gate_ln": "log(1 + exp)", "gate_row": "a step of the running sums", "gate_m": "the last one: -(B + M)",
    "gate_enm": "exp(-(B + M))", "columns_done": "a, -M and exp(-m) stand on columns, in PSUM", "acol_ready": "and in memory",
    "pads_ready": "ones beside the values, zeros before the first token", "conv_tap": "a tap of the convolution",
    "conv": "its last tap", "silu_sig": "the sigmoid of it", "silu": "its silu", "z_ready": "a - M of a head",
    "z_masked": "without the future", "w_ready": "the exp of it", "kq_done": "a head's keys times queries",
    "s_ready": "weighted", "num_done": "times the values", "num_ready": "and in memory", "num_ssq": "its sum of squares",
    "den_part": "a step of the denominators", "den_abs": "max(|den|, exp(-m))", "den_rec": "one over it",
    "num_norm": "a step of the heads' norm", "num_factor": "the factor of a head's numerators",
    "mo_sig": "the output gate", "hm_ready": "a head's output",
    "ak_part": "keys of a head are in place", "scores_done": "queries times keys", "lg_ready": "with their bias",
    "mx_ready": "their largest", "negm_part": "minus the maximum, for the first tile", "negm_ready": "and for the second",
    "sink_part": "the sink's exponent, for the first tile", "sink_diff": "and for the second", "sink_exp": "its exp",
    "probs_ready": "exp of the logits, with sums", "denom": "the sum with the sink", "rinv_ready": "one over it",
    "probs_turned": "the weights are transposed, in PSUM", "pT_ready": "and in memory", "pv_done": "times the values",
    "ha_ready": "a tile of the output",
    "g_sig": "a branch's gate", "y_ready": "the sum of the branches", "y_hi": "its rounded part", "y_lo": "and the rest",
    "x_added": "the mixer is on the residual stream", "ff_sq": "squares of the MLP's middle", "ff_hi": "their rounded part",
    "ff_lo": "and the rest", "mlp_added": "a part of the MLP is on the residual stream",
    "g_loaded": "a norm's weights are here", "g_scaled": "times the norm's sqrt(D)", "x_fin": "the first block's output",
    "dist": "a step of the distances", "alibi": "a head's slope times distance", "moba_bias": "without the future",
    "left_one": "nothing is broken off in front of the last key", "pair_scores": "queries times keys",
    "pair_lg": "with their bias", "pair_mx": "their largest", "pair_negm": "minus the maximum", "pair_part": "an exp",
    "pair_probs": "all weights of a pair", "pair_rinv": "one over their sums", "odds": "the odds to stop at a key or pass it",
    "odds_masked": "without the future", "left_ready": "what is left of the stick", "pair_turned": "weights transposed, in PSUM",
    "pair_pT": "and in memory", "pair_done": "times the values", "y_part": "the first of two steps into memory",
    "y_ready2": "a pair's output is in memory",
    "keys_loaded": "sub-keys are here", "keys_turned": "transposed, in PSUM", "keys_ready": "and in memory",
    "xn_ready": "a tile's normed tokens", "iota": "0 .. 15", "rank_done": "scores of a head's sub-keys", "rank_ready": "in memory",
    "top8": "the best eight", "top8_at": "where they are", "top8_out": "the scores without them", "next8": "the next eight",
    "next8_at": "where they are", "top_f": "places as floats", "cand": "sums of the best of both halves",
    "pos_i": "places in both halves", "pos_f": "as floats", "pick": "one-hot", "picked": "times the sub-keys' numbers",
    "both_f": "the sub-keys' numbers", "expert_f": "the experts' numbers", "expert_ready": "as indices",
    "best_diff": "scores less the largest", "best_exp": "their exp", "wsum": "its sum", "wrec": "one over it",
    "weight": "the softmax", "expert_now": "the numbers of the next rows", "rows_used": "a row of the ring has been used",
    "gelu_ready": "the experts' activations", "coef": "times the softmax",
    "g_last_loaded": "the last norm's weights are here", "final_ready": "a tile of the result", "out_stored": "and in DRAM",
}
SIGNALS |= {f"w_loaded{i}": "" for i in range(RAW_RING)} | {f"gathered{i}": "" for i in range(GATHER)}


def bucket_onehot():
    n = (WINDOW - 1) - np.arange(WINDOW)
    exact = N_BUCKETS // 2
    large = exact + (np.log(np.maximum(n, 1) / exact) / np.log(MAX_DISTANCE / exact)
                     * (N_BUCKETS - exact)).astype(np.int32)
    bucket = np.where(n < exact, n, np.minimum(large, N_BUCKETS - 1))
    return (np.arange(N_BUCKETS)[:, None] == bucket[None, :]).astype(np.float32)


def layer_units():
    u = [("mqk", i, "F") for i in range(4)] + [("mv", i, "T") for i in range(4)]
    u += [("aq", i, "F") for i in range(4)] + [("ak", 0, "F"), ("av", 0, "V")]
    u += [("mo", i, "T") for i in range(4)]
    u += [("ga", i, "F") for i in range(4)] + [("gb", i, "F") for i in range(4)]
    u += [("bm", i, "F") for i in range(4)] + [("ba", i, "F") for i in range(4)]
    u += [("wo", i, "T") for i in range(4)]
    pairs = D_FF // 512
    u += [("up", 0, "F"), ("up", 1, "F")]
    for p in range(pairs):
        if p + 1 < pairs:
            u += [("up", 2 * p + 2, "F"), ("up", 2 * p + 3, "F")]
        u += [("down", 2 * p, "T"), ("down", 2 * p + 1, "T")]
    return u


def second_units():
    u = [("qa", i, "F") for i in range(2)] + [("ka", i, "F") for i in range(2)] + [("va", i, "T") for i in range(2)]
    u += [("qb", i, "F") for i in range(2)] + [("kb", i, "F") for i in range(2)] + [("vb", i, "T") for i in range(2)]
    u += [("ga2", i, "F") for i in range(4)] + [("gb2", i, "F") for i in range(4)]
    u += [("yab", i, "Y") for i in range(4)]
    u += [("mix", i, "T") for i in range(4)] + [("pq", i, "F") for i in range(8)]
    return u


NU = len(layer_units())


class Counts:

    def __init__(self, known):
        self.known = known
        self.where = {}
        self.total = {}
        self.region = "pre"
        self.layer = None

    def mark(self, name, key=0, by=1):
        t = self.total.setdefault(name, {"pre": 0, "layer": 0, "post": 0})
        t[self.region] += by
        assert (name, self.region, key) not in self.where, (name, key)
        self.where[name, self.region, key] = t[self.region]
        return by

    def at(self, name, key=0, region=None):
        region = region or self.region
        if self.known is None:
            return 1
        t, n = self.known.total[name], self.known.where[name, region, key]
        if region == "pre":
            return n
        if region == "post":
            return t["pre"] + DEPTH * t["layer"] + n
        if self.region == "post":
            return t["pre"] + (DEPTH - 1) * t["layer"] + n
        return self.layer * t["layer"] + (t["pre"] + n)

    def at_layer_start(self, name):
        t = self.known.total[name] if self.known else {"pre": 1, "layer": 1}
        return (self.layer if self.region == "layer" else DEPTH) * t["layer"] + t["pre"]

    def free(self, u, ring, second):
        before = u - ring if u >= ring else max(v for v in range(NU) if v % ring == u) - NU
        return (DEPTH if second else self.layer) * NU + (ring + before + 1)


def build(nc, A, out, known):
    counts = Counts(known)
    ctx = ExitStack()
    at, mark = counts.at, counts.mark
    S = {name: ctx.enter_context(nc.semaphore(name)) for name in SIGNALS}

    with ctx:
        def sb(name, shape, dt=F32):
            return ctx.enter_context(nc.sbuf_tensor(name, shape, dt))

        xa_hi, xa_lo = sb("xa_hi", [P, KT, SEQ], F32R), sb("xa_lo", [P, KT, SEQ], F32R)
        xb_hi, xb_lo = sb("xb_hi", [P, KT, SEQ], F32R), sb("xb_lo", [P, KT, SEQ], F32R)
        w_hi, w_lo = sb("w_hi", [P, RING, UNIT], F32R), sb("w_lo", [P, RING, UNIT], F32R)
        GW = GATE_F + M_HEADS
        gate_hi, gate_lo = sb("gate_hi", [P, KT, GW], F32R), sb("gate_lo", [P, KT, GW], F32R)

        x_res = sb("x_res", [P, TT, D])
        ident = sb("ident", [P, P])
        params = sb("params", [P, P])
        params_m = sb("params_m", [P, 16])
        gate_b = sb("gate_b", [P, DEPTH])
        neg_sink = sb("neg_sink", [P, DEPTH, A_HEADS])
        minus_half = sb("minus_half", [P, 16])
        small = sb("small", [P, 256])
        gate_raw = sb("gate_raw", [P, KT, GW])
        scan_in = sb("scan_in", [M_HEADS, 2])
        ones_row, zero_row = (scan_in[:, i:i + 1].broadcast_to([M_HEADS, SEQ]) for i in range(2))
        ARENA = 27176
        arena = sb("arena", [P, ARENA])
        used = {}

        def view(name, at, size):
            assert at + size <= ARENA, (name, at + size)
            used[name] = (at, size)
            return arena[:, at:at + size]

        raw = [view(f"raw{s}", s * UNIT, UNIT) for s in range(RAW_RING)]
        o = RAW_RING * UNIT
        bias = view("bias", o, 16 * 256).rearrange("p (h c) -> p h c", h=A_HEADS)
        o += 16 * 256
        VW = M_DV + 1
        mv = view("mv", o, TT * M_HEADS * VW).rearrange("p (t h v) -> p t h v", t=TT, h=M_HEADS)
        ha = view("ha", o, TT * D).rearrange("p (t d) -> p t d", t=TT)
        o += TT * M_HEADS * VW
        num = view("num", o, TT * M_HEADS * VW).rearrange("p (t h v) -> p t h v", t=TT, h=M_HEADS)
        hn = view("hn", o, TT * D).rearrange("p (t d) -> p t d", t=TT)
        gates = view("gates", o, 8 * SEQ)[0:M_HEADS, :].rearrange("p (r t) -> p r t", r=8)
        o += TT * M_HEADS * VW
        CW = SEQ + CONV_K - 1
        mqk = view("mqk", o, KT * CW).rearrange("p (k t) -> p k t", k=KT)
        sig = mqk[:, :, 0:SEQ]
        pT = view("pT", o, 3 * 512).rearrange("p (c h k) -> p c h k", c=3, h=GROUP)
        o += KT * CW
        qk = view("qk", o, KT * SEQ).rearrange("p (k t) -> p k t", k=KT)
        lg = view("lg", o, GROUP * 384).rearrange("p (h c) -> p h c", h=GROUP)
        o += KT * SEQ
        mo = view("mo", o, TT * D).rearrange("p (t d) -> p t d", t=TT)
        o += TT * D
        ga = view("ga", o, KT * SEQ).rearrange("p (k t) -> p k t", k=KT)
        zw = view("zw", o, M_HEADS * 384).rearrange("p (h c) -> p h c", h=M_HEADS)
        sq = view("sq", o, 4 * 512).rearrange("p (b c) -> p b c", b=4)
        o += KT * SEQ
        gb = view("gb", o, KT * SEQ).rearrange("p (k t) -> p k t", k=KT)
        sm = view("sm", o, 2 * 384).rearrange("p (b c) -> p b c", b=2)
        o += KT * SEQ
        aq = view("aq", o, KT * SEQ).rearrange("p (k t) -> p k t", k=KT)
        o += KT * SEQ
        ak = view("ak", o, 2 * A_KV * SEQ).rearrange("p (e j t) -> p e j t", e=2, j=A_KV)
        o += 2 * A_KV * SEQ
        av = view("av", o, TT * 256).rearrange("p (t v) -> p t v", t=TT)
        o += TT * 256

        acc = [ctx.enter_context(nc.psum_tensor(f"acc{b}", [P, 512], F32)) for b in range(4)]
        att = [ctx.enter_context(nc.psum_tensor(f"att{b}", [P, 512], F32)) for b in range(4)]

        units, units2 = layer_units(), second_units()
        at_unit = {(n, i): k for k, (n, i, _) in enumerate(units)}
        at_unit2 = {(n, i): k for k, (n, i, _) in enumerate(units2)}

        def whi(s, kind):
            return w_hi[:, s, :].rearrange("p (k n) -> p k n", k=4 if kind == "T" else 8)

        def wlo(s, kind):
            return w_lo[:, s, :].rearrange("p (k n) -> p k n", k=4 if kind == "T" else 8)

        PARAM_ROWS = [("norm_mix_g", 16), ("norm_mlp_g", 16), ("norm1_g_2", 8), ("norm2_g_2", 8),
                      ("conv_w", 64), ("conv_b", 16)]
        COL = {}
        n = 0
        for name, rows in PARAM_ROWS:
            COL[name] = n
            n += rows
        assert n == P

        def col(name, l, k, tile=params):
            if isinstance(l, int):
                c = COL[name] + 8 * l + k if name != "conv_w" else COL[name] + 32 * l + k
                return tile[:, c:c + 1]
            step = 32 if name == "conv_w" else 8
            return tile[:, bass.ds(l * step + (COL[name] + k), 1)]

        rows_p = hn[:, 0, 0:P]
        rows_m = hn[:, 0, P:2 * P]
        onehot = hn[0:N_BUCKETS, 0, 2 * P:3 * P]
        rel_sb = hn[0:N_BUCKETS, 0, 3 * P:3 * P + A_HEADS]
        toep = hn[0:A_HEADS, 1, 0:384]

        def area(name, at, size):
            return arena[:, used[name][0] + at:used[name][0] + at + size]

        moba_bias = area("bias", 0, H2 * 384).rearrange("p (h c) -> p h c", h=H2)
        g_row = area("bias", H2 * 384, D)
        qa, ka = aq[:, 0:4, :], aq[:, 4:8, :]
        qb, kb = qk[:, 0:4, :], qk[:, 4:8, :]
        va, vb = (area("mv", i * TT * W2, TT * W2).rearrange("p (t v) -> p t v", t=TT) for i in range(2))
        ya, yb = (mo[:, i, :].rearrange("p (t v) -> p t v", t=TT) for i in range(2))
        lg2 = area("mqk", 0, 768).rearrange("p (h c) -> p h c", h=2)
        pT2 = area("mqk", 768, 768).rearrange("p (h c k) -> p h c k", h=2, c=3)
        dist_i, dist = area("mqk", 768, 384).bitcast(I32), area("mqk", 1536, 384)
        stay, stop, left = (area("ak", i * 768, 768).rearrange("p (h c) -> p h c", h=2) for i in range(3))
        raw_keys = mo.rearrange("p t d -> p (t d)").rearrange("p (h n) -> p h n", h=HP)
        keys = aq.rearrange("p k t -> p (k t)").rearrange("p (h n) -> p h n", h=HP)
        queries = area("ga", 0, HP * SEQ).rearrange("p (h t) -> p h t", h=HP)
        rank = [area(n_, 0, HP * P_KEYS).rearrange("p (h n) -> p h n", h=HP) for n_ in ("qk", "mqk")]
        g_last = area("mv", 0, D)
        expert = area("mv", D, TT * SLOTS).bitcast(U32)
        weight = area("mv", D + TT * SLOTS, TT * SLOTS)
        dots = area("mv", D + 2 * TT * SLOTS, TT * SLOTS)
        expert_now = area("mv", D + 3 * TT * SLOTS, GATHER).bitcast(U32)
        iota_i, iota16 = area("ak", 0, P_TOP).bitcast(I32), area("ak", P_TOP, P_TOP)
        top_s = area("ak", 32, 2 * P_TOP).rearrange("p (i k) -> p i k", i=2)
        top_i = area("ak", 64, 2 * P_TOP).bitcast(U32).rearrange("p (i k) -> p i k", i=2)
        top_f = area("ak", 96, 2 * P_TOP).rearrange("p (i k) -> p i k", i=2)
        pos = area("ak", 128, P_TOP).bitcast(U32)
        pos_i = area("ak", 144, 2 * P_TOP).bitcast(U32).rearrange("p (i k) -> p i k", i=2)
        pos_f = area("ak", 176, 2 * P_TOP).rearrange("p (i k) -> p i k", i=2)
        both_f = area("ak", 208, 2 * P_TOP).rearrange("p (i k) -> p i k", i=2)
        expert_f = area("ak", 240, P_TOP)
        cand = area("ak", 256, P_TOP * P_TOP).rearrange("p (a b) -> p a b", a=P_TOP)
        pick = area("ak", 512, 2 * P_TOP * P_TOP).rearrange("p (i k a) -> p i k a", i=2, k=P_TOP)
        best = area("ak", 1024, TT * SLOTS).rearrange("p (t h k) -> p t h k", t=TT, h=P_HEADS)
        wsum = area("ak", 1280, TT * P_HEADS).rearrange("p (t h) -> p t h", t=TT)
        rows_ring = [arena[:, i * D:(i + 1) * D] for i in range(GATHER)]

        def unit_dma(sp, unit, slot, l, second):
            name, i, kind = unit
            F = raw[slot].rearrange("p (k n) -> p k n", k=8)
            T = raw[slot].rearrange("p (k n) -> p k n", k=4)

            def f_src(w, c0):
                return w[:, c0 + 256 * i:c0 + 256 * (i + 1)].rearrange("(k p) n -> p k n", p=P)

            def t_src(w, c0):
                rows = w[512 * (i % 2):512 * (i % 2 + 1), c0 + 512 * (i // 2):c0 + 512 * (i // 2 + 1)]
                return rows.rearrange("(k p) n -> p k n", p=P)

            key = ("u2" if second else "u", at_unit2[name, i] if second else at_unit[name, i])
            f_cols = {"mqk": COL_MQK, "aq": COL_AQ, "ak": COL_AK, "av": COL_AV, "ga": COL_GA, "gb": COL_GB}
            f_cols2 = {"qa": 0, "ka": W2, "qb": 3 * W2, "kb": 4 * W2, "ga2": 6 * W2, "gb2": 6 * W2 + D}
            if second:
                if name in f_cols2:
                    sp.dma_start(F, f_src(A["w_in_2"][0], f_cols2[name])).then_inc(
                        S[f"w_loaded{slot}"], mark(f"w_loaded{slot}", key, 16))
                elif name in ("va", "vb"):
                    sp.dma_start(T, t_src(A["w_in_2"][0], {"va": 2 * W2, "vb": 5 * W2}[name])).then_inc(
                        S[f"w_loaded{slot}"], mark(f"w_loaded{slot}", key, 16))
                elif name == "yab":
                    sp.dma_start(F[:, 0:4, :], f_src(A["w_out_moba_2"][0], 0)).then_inc(
                        S[f"w_loaded{slot}"], mark(f"w_loaded{slot}", key + (0,), 16))
                    sp.dma_start(F[:, 4:8, :], f_src(A["w_out_sb_2"][0], 0)).then_inc(
                        S[f"w_loaded{slot}"], mark(f"w_loaded{slot}", key, 16))
                elif name == "mix":
                    sp.dma_start(T, t_src(A["w_mix_out_2"][0], 0)).then_inc(
                        S[f"w_loaded{slot}"], mark(f"w_loaded{slot}", key, 16))
                elif name == "pq":
                    sp.dma_start(F, f_src(A["peer_w_q_2"][0], 0)).then_inc(
                        S[f"w_loaded{slot}"], mark(f"w_loaded{slot}", key, 16))
                return

            def of(w):
                return A[w][bass.ds(l, 1)].rearrange("o k n -> (o k) n")

            if name in f_cols:
                src, dst = f_src(of("w_in"), f_cols[name]), F
            elif name in ("mv", "mo"):
                src, dst = t_src(of("w_in"), COL_MV if name == "mv" else COL_MO), T
            elif name in ("bm", "ba"):
                src, dst = f_src(of("w_branch_m" if name == "bm" else "w_branch_a"), 0), F
            elif name == "wo":
                src, dst = t_src(of("w_out"), 0), T
            elif name == "up":
                src, dst = f_src(of("w_up"), 0), F
            else:
                rows, half = 512 * (i // 2), 512 * (i % 2)
                src = of("w_down")[rows:rows + 512, half:half + 512].rearrange("(k p) n -> p k n", p=P)
                dst = T
            sp.dma_start(dst, src).then_inc(S[f"w_loaded{slot}"], mark(f"w_loaded{slot}", key, 16))

        def sync_program(sp):
            counts.region = "pre"
            sp.dma_start(x_res[:], A["x"][0].rearrange("(t p) d -> p t d", p=P)).then_inc(
                S["x_loaded"], mark("x_loaded", 0, 16))
            row = 0
            for name, rows in PARAM_ROWS:
                src = A[name]
                if name == "conv_w":
                    src = src.rearrange("l j (k p) -> (l j k) p", p=P)
                else:
                    src = src.rearrange("l (k p) -> (l k) p", p=P)
                sp.dma_start(rows_p[row:row + rows, :], src).then_inc(S["params_loaded"], mark("params_loaded", name, 16))
                row += rows
            sp.dma_start(rows_m[0:16, :], A["mlstm_norm_g"].rearrange("l (k p) -> (l k) p", p=P)).then_inc(
                S["params_loaded"], mark("params_loaded", "m", 16))
            sp.dma_start(onehot, A["onehot"]).then_inc(S["params_loaded"], mark("params_loaded", "onehot", 16))
            sp.dma_start(rel_sb, A["rel_bias"]).then_inc(S["params_loaded"], mark("params_loaded", "rel", 16))
            with nc.allow_non_contiguous_dma(reason="sixteen gate biases"):
                sp.dma_start(gate_b[0:M_HEADS, :], A["b_igate"].rearrange("l h -> h l")).then_inc(
                    S["params_loaded"], mark("params_loaded", "bi", 16))
                sp.dma_start(gate_b[GATE_F:GATE_F + M_HEADS, :], A["b_fgate"].rearrange("l h -> h l")).then_inc(
                    S["params_loaded"], mark("params_loaded", "bf", 16))
            sp.dma_start(neg_sink[:].rearrange("p l h -> p (l h)"),
                             A["attn_sinks"].rearrange("(o l) h -> o (l h)", o=1).broadcast_to([P, DEPTH * A_HEADS])).then_inc(
                S["params_loaded"], mark("params_loaded", "sink", 16))
            sp.wait_ge(S["toep_ready"], at("toep_ready", 1))
            sp.dma_start(A["toep"], toep.unsqueeze(1).broadcast_to([A_HEADS, P, 384])).then_inc(
                S["toep_stored"], mark("toep_stored", 0, 16))
            shifted = bass.AP(tensor=A["toep"].tensor, offset=WINDOW - 1, ap=[[383, P], [P * 384, A_HEADS], [1, 256]])

            counts.region = "layer"
            with sp.Fori(0, DEPTH) as l:
                counts.layer = l
                sp.wait_ge(S["lo_ready"], counts.free(0, RAW_RING, False))
                win = A["w_in"][bass.ds(l, 1)].rearrange("o k n -> (o k) n").rearrange("(k p) n -> p k n", p=P)
                with nc.allow_non_contiguous_dma(reason="eight columns"):
                    sp.wait_ge(S["consts"], at("consts", "gate_raw", "pre"))
                    sp.dma_start(gate_raw[:, :, 0:M_HEADS], win[:, :, COL_MI:COL_MI + M_HEADS]).then_inc(
                        S["gate_loaded"], mark("gate_loaded", 0, 16))
                    sp.dma_start(gate_raw[:, :, GATE_F:GATE_F + M_HEADS], win[:, :, COL_MF:COL_MF + M_HEADS]).then_inc(
                        S["gate_loaded"], mark("gate_loaded", 1, 16))
                for u, unit in enumerate(units):
                    if unit == ("mv", 0, "T"):
                        sp.wait_ge(S["toep_stored"], at("toep_stored", 0, "pre"))
                        sp.dma_start(bias, shifted).then_inc(S["bias_loaded"], mark("bias_loaded", 0, 16))
                    sp.wait_ge(S["consts"], at("consts", "gate_raw", "pre"))
                    sp.wait_ge(S["lo_ready"], counts.free(u, RAW_RING, False))
                    unit_dma(sp, unit, u % RAW_RING, l, False)

            counts.region = "post"
            counts.layer = None
            def rows_of(w):
                return w.broadcast_to([P, D])

            sp.wait_ge(S["lg_ready"], at("lg_ready", (A_KV - 1, 2), "layer"))
            sp.dma_start(g_row, rows_of(A["final_norm_g"].rearrange("(o d) -> o d", o=1))).then_inc(
                S["g_loaded"], mark("g_loaded", "fin", 16))
            for u, unit in enumerate(units2):
                if unit == ("ga2", 0, "F"):
                    sp.wait_ge(S["x_fin"], at("x_fin", TT - 1))
                    sp.dma_start(g_row, rows_of(A["norm2_g_2"])).then_inc(S["g_loaded"], mark("g_loaded", "n2", 16))
                elif unit == ("mix", 0, "T"):
                    sp.wait_ge(S["x_lo"], at("x_lo", ("y2", KT - 1)))
                    for h in range(HP):
                        sp.dma_start(raw_keys[:, h, :], A["peer_sub_keys_2"][0, h // 2, h % 2]).then_inc(
                            S["keys_loaded"], mark("keys_loaded", h, 16))
                elif unit == ("pq", 0, "F"):
                    sp.wait_ge(S["y_ready2"], at("y_ready2", ("s", 3)))
                    sp.dma_start(g_last, rows_of(A["final_norm_g_2"].rearrange("(o d) -> o d", o=1))).then_inc(
                        S["g_last_loaded"], mark("g_last_loaded", 0, 16))
                sp.wait_ge(S["lo_ready"], counts.free(u, RAW_RING, True))
                unit_dma(sp, unit, u % RAW_RING, None, True)
            dst = out[0].rearrange("(t p) d -> p t d", p=P)
            for t in range(TT):
                sp.wait_ge(S["final_ready"], at("final_ready", t))
                sp.dma_start(dst[:, t, :], x_res[:, t, :]).then_inc(S["out_stored"], mark("out_stored", t, 16))
            sp.wait_ge(S["out_stored"], at("out_stored", TT - 1))

        def split_hi(act, u, second):
            s, r = u % RING, u % RAW_RING
            act.wait_ge(S["unit_done"], counts.free(u, RING, second))
            act.wait_ge(S[f"w_loaded{r}"], at(f"w_loaded{r}", ("u2" if second else "u", u)))
            nc.scalar.copy(w_hi[:, s, :], raw[r]).then_inc(S["hi_ready"], mark("hi_ready", ("u2" if second else "u", u)))

        def split_lo(dve, u, second):
            s = u % RING
            dve.wait_ge(S["hi_ready"], at("hi_ready", ("u2" if second else "u", u)))
            nc.vector.tensor_tensor(w_lo[:, s, :], raw[u % RAW_RING], w_hi[:, s, :].bitcast(F32), ALU.subtract).then_inc(
                S["lo_ready"], mark("lo_ready", ("u2" if second else "u", u)))

        def passes(out_, lh, ll, rh, rl, first, last):
            nc.tensor.matmul(out_, lh, rh, start=first, stop=False)
            nc.tensor.matmul(out_, ll, rh, start=False, stop=False)
            return nc.tensor.matmul(out_, lh, rl, start=False, stop=last)

        def unit_f(banks, s, xh, xl, key):
            h, lw = whi(s, "F"), wlo(s, "F")
            for n_ in range(2):
                for k in range(8):
                    m = passes(banks[0][:, n_ * SEQ:(n_ + 1) * SEQ], h[:, k, n_ * P:(n_ + 1) * P],
                               lw[:, k, n_ * P:(n_ + 1) * P], xh[:, k, :], xl[:, k, :], k == 0, k == 7)
            m.then_inc(S["unit_done"], mark("unit_done", key))

        def unit_y(banks, s, xh, xl, key):
            h, lw = whi(s, "F"), wlo(s, "F")
            for b in range(2):
                for n_ in range(2):
                    for k in range(4):
                        kk = 4 * b + k
                        m = passes(banks[b][:, n_ * SEQ:(n_ + 1) * SEQ], h[:, kk, n_ * P:(n_ + 1) * P],
                                   lw[:, kk, n_ * P:(n_ + 1) * P], xh[:, kk, :], xl[:, kk, :], k == 0, k == 3)
            m.then_inc(S["unit_done"], mark("unit_done", key))

        def unit_v(banks, s, xh, xl, key):
            h, lw = whi(s, "F"), wlo(s, "F")
            for t in range(TT):
                for k in range(8):
                    tok = slice(t * P, (t + 1) * P)
                    m = passes(banks[0][:, t * 256:(t + 1) * 256], xh[:, k, tok], xl[:, k, tok],
                               h[:, k, :], lw[:, k, :], k == 0, k == 7)
            m.then_inc(S["unit_done"], mark("unit_done", key))

        def unit_t(banks, s, xh, xl, k0, first, last, key):
            h, lw = whi(s, "T"), wlo(s, "T")
            for t in range(TT):
                tok = slice(t * P, (t + 1) * P)
                for k in range(4):
                    m = passes(banks[t][:], xh[:, k0 + k, tok], xl[:, k0 + k, tok], h[:, k, :], lw[:, k, :],
                               first and k == 0, last and k == 3)
            m.then_inc(S["unit_done"], mark("unit_done", key))

        ssq, rstd = small[:, 0:2], small[:, 2:4]
        eps_d, eps_v, idle, zero_all = small[:, 240:242], small[:, 242:250], small[:, 251:252], small[:, 252:253]
        junk = hn

        def norm_act(act, tag):
            if tag in ("mix", "fin"):
                act.wait_ge(S["mlp_added"], counts.at_layer_start("mlp_added"))
            for t in range(TT):
                if tag == "n1":
                    act.wait_ge(S["x_fin"], at("x_fin", t))
                nc.scalar.activation(junk[:, t, :], x_res[:, t, :], ACT.Square, accum_out=ssq[:, t:t + 1]).then_inc(
                    S["ssq_ready"], mark("ssq_ready", (tag, t)))

        def norm_pool(pool, tag):
            pool.wait_ge(S["ssq_ready"], at("ssq_ready", (tag, 1)))
            nc.gpsimd.tensor_tensor(rstd, ssq, eps_d, ALU.add).then_inc(S["ms_ready"], mark("ms_ready", tag))
            pool.wait_ge(S["ms_ready"], at("ms_ready", tag))
            nc.gpsimd.tensor_tensor(rstd, rstd, minus_half[:, 0:2], ALU.pow).then_inc(S["rstd_ready"], mark("rstd_ready", tag))

        def norm_dve(dve, tag):
            dve.wait_ge(S["rstd_ready"], at("rstd_ready", tag))
            for t in range(TT):
                nc.vector.tensor_scalar(hn[:, t, :], x_res[:, t, :], rstd[:, t:t + 1], D ** 0.5, ALU.mult, ALU.mult).then_inc(
                    S["hn_ready"], mark("hn_ready", (tag, t)))

        def turn_pe(pe, src, tag, ready, kts=KT):
            for k in range(kts):
                for t in range(TT):
                    if k == 0:
                        pe.wait_ge(S[ready[t][0]], at(*ready[t]))
                    m = nc.tensor.transpose(att[k // 2][:, (k % 2) * SEQ + t * P:(k % 2) * SEQ + (t + 1) * P],
                                            src(k, t), ident[:])
                m.then_inc(S["turned"], mark("turned", (tag, k)))

        def turn_act(act, dst_hi, tag, scale, kts=KT):
            for k in range(kts):
                act.wait_ge(S["turned"], at("turned", (tag, k | 1)))
                ps = att[k // 2][:, (k % 2) * SEQ:(k % 2 + 1) * SEQ]
                nc.scalar.activation(dst_hi[:, k, :], ps, ACT.Copy, scale=scale(k)).then_inc(S["x_hi"], mark("x_hi", (tag, k)))

        def turn_dve(dve, dst_hi, dst_lo, tag, scale, kts=KT):
            for k in range(kts):
                dve.wait_ge(S["x_hi"], at("x_hi", (tag, k | 1)))
                ps = att[k // 2][:, (k % 2) * SEQ:(k % 2 + 1) * SEQ]
                nc.vector.scalar_tensor_tensor(dst_lo[:, k, :], ps, scale(k), dst_hi[:, k, :].bitcast(F32),
                                                   ALU.mult, ALU.subtract).then_inc(S["x_lo"], mark("x_lo", (tag, k)))

        g_i, g_f, g_n, g_e = gates[:, 0, :], gates[:, 1, :], gates[:, 2, :], gates[:, 3, :]
        g_B, g_a, g_M, g_m = gates[:, 4, :], gates[:, 5, :], gates[:, 6, :], gates[:, 7, :]
        acol = small[:, 4:20]
        n_ss, n_dn, n_ms, n_c = small[:, 20:28], small[:, 28:36], small[:, 36:44], small[:, 44:52]
        n_rec = small[:, 52:60]
        mx, negm, sums, esink, rinv = (small[:, 60 + 8 * i:68 + 8 * i] for i in range(5))

        BANKS = {}
        for i in range(4):
            BANKS["mqk", i] = [acc[i]]
            BANKS["aq", i] = [acc[i]]
            for name in ("ga", "gb", "bm", "ba"):
                BANKS[name, i] = [acc[(2 + i) % 4]]
            BANKS["mv", i] = [acc[2 * (i // 2)], acc[2 * (i // 2) + 1]]
            for name in ("mo", "wo"):
                BANKS[name, i] = [acc[(2 + 2 * (i // 2)) % 4], acc[(3 + 2 * (i // 2)) % 4]]
        BANKS["ak", 0], BANKS["av", 0] = [acc[0]], [acc[1]]
        for i in range(16):
            BANKS["up", i] = [att[i % 2]]
            BANKS["down", i] = [acc[i % 2], acc[2 + i % 2]]
        BEFORE = {("mv", 0): [("mqk", 0), ("mqk", 1)], ("mv", 2): [("mqk", 2), ("mqk", 3)],
                  ("aq", 0): [("mv", 1)], ("aq", 2): [("mv", 3)], ("ak", 0): [("aq", 0)], ("av", 0): [("aq", 1)],
                  ("mo", 0): [("aq", 2), ("aq", 3)], ("mo", 2): [("ak", 0), ("av", 0)],
                  ("ga", 0): [("mo", 1)], ("ga", 2): [("mo", 3)]}
        for i in range(4):
            BEFORE["gb", i], BEFORE["bm", i], BEFORE["ba", i] = [("ga", i)], [("gb", i)], [("bm", i)]
        BEFORE["wo", 0], BEFORE["wo", 2] = [("ba", 0), ("ba", 1)], [("ba", 2), ("ba", 3)]
        BEFORE["down", 0], BEFORE["down", 1] = [("wo", 1), ("wo", 3)], []
        for i in range(2, 16):
            BEFORE["up", i] = [("up", i - 2)]
        BY_ACT = {"mqk", "mv", "aq", "av"}

        def emptied(eng, name, i):
            eng.wait_ge(S["emptied_act" if name in BY_ACT else "emptied_dve"], at("emptied_act" if name in BY_ACT else "emptied_dve", (name, i)))

        def layer_pe(pe, l):
            def turn_norm(tag):
                turn_pe(pe, lambda k, t: hn[:, t, k * P:(k + 1) * P], tag,
                        [("hn_ready", (tag, 0)), ("hn_ready", (tag, 1))])

            def gate_products():
                pe.wait_ge(S["gate_lo"], at("gate_lo"))
                for k in range(KT):
                    m = passes(att[0][0:GW, 0:SEQ], gate_hi[:, k, :], gate_lo[:, k, :], xa_hi[:, k, :], xa_lo[:, k, :],
                               k == 0, k == KT - 1)
                m.then_inc(S["gate_done"], mark("gate_done"))

            def gate_columns():
                pe.wait_ge(S["gate_m"], at("gate_m"))
                for h in range(M_HEADS):
                    m = nc.tensor.matmul(att[h // 2][:, (h % 2) * SEQ:(h % 2 + 1) * SEQ], ident[0:M_HEADS, h:h + 1].broadcast_to([M_HEADS, P]), g_M,
                                         start=True, stop=True)
                pe.wait_ge(S["gate_enm"], at("gate_enm"))
                for n_, row in enumerate((g_a, g_m)):
                    for t in range(TT):
                        m = nc.tensor.matmul(att[2][:, (2 * n_ + t) * 4:(2 * n_ + t) * 4 + 4], row[:, t * P:(t + 1) * P],
                                             ident[0:4, 0:4], start=True, stop=True)
                m.then_inc(S["columns_done"], mark("columns_done"))

            def kq(h):
                b = att[2 + h % 2]
                if h == 0:
                    pe.wait_ge(S["acol_ready"], at("acol_ready"))
                pe.wait_ge(S["silu"], at("silu", h))
                pe.wait_ge(S["silu"], at("silu", 4 + h))
                if h >= 2:
                    pe.wait_ge(S["s_ready"], at("s_ready", h - 2))
                nc.tensor.matmul(b[:, 0:256], qk[:, 4 + h, 0:P], qk[:, h, :], start=True, stop=True)
                m = nc.tensor.matmul(b[:, 256:384], qk[:, 4 + h, P:2 * P], qk[:, h, P:2 * P], start=True, stop=True)
                m.then_inc(S["kq_done"], mark("kq_done", h))

            def num_product(h):
                pe.wait_ge(S["s_ready"], at("s_ready", h))
                if h >= 1:
                    pe.wait_ge(S["num_ready"], at("num_ready", (h - 1, 1)))
                s = sm[:, h % 2, :]
                nc.tensor.matmul(att[0][:, 0:VW], s[:, 0:P], mv[:, 0, h, :], start=True, stop=True).then_inc(
                    S["num_done"], mark("num_done", (h, 0)))
                nc.tensor.matmul(att[1][:, 0:VW], s[:, P:2 * P], mv[:, 0, h, :], start=True, stop=False)
                nc.tensor.matmul(att[1][:, 0:VW], s[:, 2 * P:3 * P], mv[:, 1, h, :], start=False, stop=True).then_inc(
                    S["num_done"], mark("num_done", (h, 1)))

            def scores(j):
                if j == 0:
                    pe.wait_ge(S["num_ready"], at("num_ready", (3, 1)))
                    emptied(pe, "ak", 0)
                    emptied(pe, "aq", 3)
                else:
                    pe.wait_ge(S["pT_ready"], at("pT_ready", (j - 1, 2)))
                for g in range(GROUP):
                    h = GROUP * j + g
                    q, k_ = aq[:, h // 2, :], ak[:, h % 2, j, :]
                    nc.tensor.matmul(att[0][:, g * P:(g + 1) * P], q[:, 0:P], k_[:, 0:P], start=True, stop=True)
                    m = nc.tensor.matmul(att[1 + g // 2][:, (g % 2) * SEQ:(g % 2 + 1) * SEQ], q[:, P:2 * P], k_[:, :],
                                         start=True, stop=True)
                m.then_inc(S["scores_done"], mark("scores_done", j))

            def turn_probs(j):
                pe.wait_ge(S["probs_ready"], at("probs_ready", (j, 7)))
                for c in range(3):
                    for g in range(GROUP):
                        m = nc.tensor.transpose(att[c][:, g * P:(g + 1) * P], lg[:, g, c * P:(c + 1) * P], ident[:])
                    m.then_inc(S["probs_turned"], mark("probs_turned", (j, c)))

            def pv(j):
                pe.wait_ge(S["pT_ready"], at("pT_ready", (j, 2)))
                if j >= 1:
                    pe.wait_ge(S["ha_ready"], at("ha_ready", (j - 1, 1)))
                else:
                    emptied(pe, "av", 0)
                v0, v1 = av[:, 0, j * A_DH:(j + 1) * A_DH], av[:, 1, j * A_DH:(j + 1) * A_DH]
                for g in range(GROUP):
                    nc.tensor.matmul(att[3][:, g * A_DH:(g + 1) * A_DH], pT[:, 0, g, :], v0, start=True, stop=True)
                for g in range(GROUP):
                    c = 256 + g * A_DH
                    nc.tensor.matmul(att[3][:, c:c + A_DH], pT[:, 1, g, :], v0, start=True, stop=False)
                    m = nc.tensor.matmul(att[3][:, c:c + A_DH], pT[:, 2, g, :], v1, start=False, stop=True)
                m.then_inc(S["pv_done"], mark("pv_done", j))

            def turn_hm():
                pe.wait_ge(S["ha_ready"], at("ha_ready", (3, 1)))
                turn_pe(pe, lambda k, t: mo[:, t, k * P:(k + 1) * P], "hm", [("hm_ready", (0, 3)), ("hm_ready", (1, 3))])

            def turn_ha():
                pe.wait_ge(S["x_lo"], at("x_lo", ("hm", KT - 1)))
                turn_pe(pe, lambda k, t: ha[:, t, k * P:(k + 1) * P], "ha", [("ha_ready", (3, 0)), ("ha_ready", (3, 1))])

            turn_norm("mix")
            for u, (name, i, kind) in enumerate(units):
                pe.wait_ge(S["lo_ready"], at("lo_ready", ("u", u)))
                for p in BEFORE.get((name, i), []):
                    emptied(pe, *p)
                if (name, i) == ("mqk", 0):
                    pe.wait_ge(S["x_lo"], at("x_lo", ("mix", KT - 1)))
                if (name, i) == ("bm", 0):
                    pe.wait_ge(S["x_lo"], at("x_lo", ("hm", KT - 1)))
                if (name, i) == ("ba", 0):
                    pe.wait_ge(S["x_lo"], at("x_lo", ("ha", KT - 1)))
                if (name, i) == ("wo", 0):
                    pe.wait_ge(S["y_lo"], at("y_lo", 3))
                if (name, i) == ("up", 0):
                    pe.wait_ge(S["x_lo"], at("x_lo", ("mlp", KT - 1)))
                if name == "down" and i % 2 == 0:
                    pe.wait_ge(S["ff_lo"], at("ff_lo", i + 1))
                xh, xl = (xb_hi, xb_lo) if name in ("bm", "wo", "down") else (xa_hi, xa_lo)
                b, s = BANKS[name, i], u % RING
                if kind == "F":
                    unit_f(b, s, xh, xl, ("u", u))
                elif kind == "V":
                    unit_v(b, s, xh, xl, ("u", u))
                elif name == "down":
                    unit_t(b, s, xh, xl, 4 * (i // 2 % 2), i < 2, i >= 14, ("u", u))
                else:
                    unit_t(b, s, xh, xl, 4 * (i % 2), i % 2 == 0, i % 2 == 1, ("u", u))
                if (name, i) == ("mqk", 3):
                    gate_products()
                elif (name, i) == ("aq", 0):
                    gate_columns()
                elif (name, i) == ("aq", 1):
                    kq(0)
                    kq(1)
                elif (name, i) == ("aq", 3):
                    num_product(0)
                    kq(2)
                elif (name, i) == ("ak", 0):
                    num_product(1)
                    kq(3)
                elif (name, i) == ("av", 0):
                    num_product(2)
                elif (name, i) == ("mo", 0):
                    num_product(3)
                elif (name, i) == ("mo", 1):
                    scores(0)
                elif (name, i) == ("mo", 2):
                    turn_probs(0)
                elif (name, i) == ("mo", 3):
                    pv(0)
                    scores(1)
                elif (name, i) == ("ga", 0):
                    turn_probs(1)
                elif (name, i) == ("ga", 1):
                    pv(1)
                    scores(2)
                elif (name, i) == ("ga", 2):
                    turn_probs(2)
                elif (name, i) == ("ga", 3):
                    pv(2)
                    scores(3)
                elif (name, i) == ("gb", 0):
                    turn_probs(3)
                elif (name, i) == ("gb", 1):
                    pv(3)
                elif (name, i) == ("gb", 3):
                    turn_hm()
                elif (name, i) == ("bm", 0):
                    turn_ha()
                elif (name, i) == ("wo", 3):
                    turn_norm("mlp")

        def layer_act(act, l):
            def unit(name, i):
                act.wait_ge(S["unit_done"], at("unit_done", ("u", at_unit[name, i])))

            def gate_split():
                act.wait_ge(S["gate_loaded"], at("gate_loaded", 1))
                nc.scalar.copy(gate_hi[:], gate_raw[:]).then_inc(S["gate_hi"], mark("gate_hi"))

            def gate_softplus():
                act.wait_ge(S["gate_nabs"], at("gate_nabs"))
                nc.scalar.activation(g_e, g_n, ACT.Exp).then_inc(S["gate_exp"], mark("gate_exp"))
                act.wait_ge(S["gate_exp"], at("gate_exp"))
                nc.scalar.activation(g_e, g_e, ACT.Ln, bias=1.0).then_inc(S["gate_ln"], mark("gate_ln"))

            def gate_enm():
                act.wait_ge(S["gate_m"], at("gate_m"))
                nc.scalar.activation(g_m, g_m, ACT.Exp).then_inc(S["gate_enm"], mark("gate_enm"))

            def silu_sigmoid():
                act.wait_ge(S["conv"], at("conv", 7))
                for k in range(4):
                    nc.scalar.activation(sig[:, 2 * k:2 * k + 2, :], qk[:, 2 * k:2 * k + 2, :], ACT.Sigmoid).then_inc(
                        S["silu_sig"], mark("silu_sig", k))

            def decay_exp():
                act.wait_ge(S["z_masked"], at("z_masked", 1))
                nc.scalar.activation(zw, zw, ACT.Exp).then_inc(S["w_ready"], mark("w_ready"))

            def num_take(h):
                for t in range(TT):
                    act.wait_ge(S["num_done"], at("num_done", (h, t)))
                    nc.scalar.copy(num[:, t, h, :], att[t][:, 0:VW]).then_inc(S["num_ready"], mark("num_ready", (h, t)))

            def num_squares():
                act.wait_ge(S["num_ready"], at("num_ready", (3, 1)))
                for t in range(TT):
                    for h in range(M_HEADS):
                        nc.scalar.activation(sm[:, t, 0:M_DV], num[:, t, h, 0:M_DV], ACT.Square,
                                                 accum_out=n_ss[:, 4 * t + h:4 * t + h + 1]).then_inc(
                            S["num_ssq"], mark("num_ssq", (t, h)))
                        act.wait_ge(S["num_ssq"], at("num_ssq", (t, h)))

            def probs(j):
                act.wait_ge(S["negm_ready"], at("negm_ready", j))
                for g in range(GROUP):
                    for t in range(TT):
                        piece = lg[:, g, 0:P] if t == 0 else lg[:, g, P:3 * P]
                        nc.scalar.activation(piece, piece, ACT.Exp, bias=negm[:, 4 * t + g:4 * t + g + 1],
                                                 accum_out=sums[:, 4 * t + g:4 * t + g + 1]).then_inc(
                            S["probs_ready"], mark("probs_ready", (j, 2 * g + t)))
                act.wait_ge(S["sink_diff"], at("sink_diff", j))
                nc.scalar.activation(esink, esink, ACT.Exp).then_inc(S["sink_exp"], mark("sink_exp", j))

            def probs_take(j):
                if j >= 1:
                    act.wait_ge(S["pv_done"], at("pv_done", j - 1))
                for c in range(3):
                    act.wait_ge(S["probs_turned"], at("probs_turned", (j, c)))
                    nc.scalar.copy(pT[:, c, :, :], att[c][:].rearrange("p (h k) -> p h k", h=GROUP)).then_inc(
                        S["pT_ready"], mark("pT_ready", (j, c)))

            def sigmoid(tile, name, sem_, key):
                act.wait_ge(S["emptied_dve"], at("emptied_dve", (name, 3)))
                nc.scalar.activation(tile, tile, ACT.Sigmoid).then_inc(S[sem_], mark(sem_, key))

            def take(name, i):
                b = BANKS[name, i]
                if name == "mqk":
                    unit(name, i)
                    nc.scalar.copy(mqk[:, 2 * i:2 * i + 2, CONV_K - 1:CW], b[0][:].rearrange("p (n t) -> p n t", n=2)).then_inc(
                        S["emptied_act"], mark("emptied_act", (name, i)))
                elif name == "aq":
                    unit(name, i)
                    nc.scalar.mul(aq[:, 2 * i:2 * i + 2, :], b[0][:].rearrange("p (n t) -> p n t", n=2), A_DH ** -0.5).then_inc(
                        S["emptied_act"], mark("emptied_act", (name, i)))
                elif name == "av":
                    unit(name, i)
                    nc.scalar.copy(av, b[0][:].rearrange("p (t v) -> p t v", t=TT)).then_inc(
                        S["emptied_act"], mark("emptied_act", (name, i)))
                elif name == "mv" and i % 2 == 1:
                    unit(name, i)
                    for t in range(TT):
                        nc.scalar.copy(mv[:, t, i - 1:i + 1, 0:M_DV], b[t][:].rearrange("p (h v) -> p h v", h=2)).then_inc(
                            S["emptied_act"], mark("emptied_act", (name, i - 1 + t)))
                elif name == "ba":
                    act.wait_ge(S["y_ready"], at("y_ready", i))
                    nc.scalar.copy(xb_hi[:, 2 * i:2 * i + 2, :], ga[:, 2 * i:2 * i + 2, :]).then_inc(S["y_hi"], mark("y_hi", i))
                elif name == "up":
                    k0 = 4 * (i // 2 % 2) + 2 * (i % 2)
                    act.wait_ge(S["emptied_dve"], at("emptied_dve", (name, i)))
                    nc.scalar.activation(sq[:, 2 + i % 2, :], sq[:, i % 2, :], ACT.Square).then_inc(
                        S["ff_sq"], mark("ff_sq", i))
                    act.wait_ge(S["ff_sq"], at("ff_sq", i))
                    if i >= 4:
                        act.wait_ge(S["unit_done"], at("unit_done", ("u", at_unit["down", 2 * (i // 2 - 2) + 1])))
                    nc.scalar.copy(xb_hi[:, k0:k0 + 2, :], sq[:, 2 + i % 2, :].rearrange("p (n t) -> p n t", n=2)).then_inc(
                        S["ff_hi"], mark("ff_hi", i))

            split_hi(act, 0, False)
            split_hi(act, 1, False)
            norm_act(act, "mix")
            turn_act(act, xa_hi, "mix", lambda k: col("norm_mix_g", l, k))
            for u, (name, i, kind) in enumerate(units):
                if u + 2 < NU:
                    split_hi(act, u + 2, False)
                take(name, i)
                if (name, i) == ("mqk", 0):
                    gate_split()
                elif (name, i) == ("mv", 0):
                    gate_softplus()
                elif (name, i) == ("mv", 1):
                    gate_enm()
                elif (name, i) == ("aq", 0):
                    silu_sigmoid()
                elif (name, i) == ("aq", 2):
                    decay_exp()
                elif (name, i) == ("aq", 3):
                    num_take(0)
                elif (name, i) == ("ak", 0):
                    num_take(1)
                elif (name, i) == ("av", 0):
                    num_take(2)
                elif (name, i) == ("mo", 0):
                    num_take(3)
                    num_squares()
                elif (name, i) == ("mo", 1):
                    probs(0)
                elif (name, i) == ("mo", 2):
                    probs_take(0)
                elif (name, i) == ("mo", 3):
                    probs(1)
                elif (name, i) == ("ga", 0):
                    probs_take(1)
                elif (name, i) == ("ga", 1):
                    probs(2)
                elif (name, i) == ("ga", 2):
                    probs_take(2)
                elif (name, i) == ("ga", 3):
                    probs(3)
                elif (name, i) == ("gb", 0):
                    probs_take(3)
                    sigmoid(mo, "mo", "mo_sig", 0)
                    sigmoid(ga, "ga", "g_sig", 0)
                elif (name, i) == ("gb", 3):
                    turn_act(act, xb_hi, "hm", lambda k: m_col(l, k))
                    sigmoid(gb, "gb", "g_sig", 1)
                elif (name, i) == ("bm", 0):
                    turn_act(act, xa_hi, "ha", lambda k: 1.0)
                elif (name, i) == ("wo", 3):
                    act.wait_ge(S["x_added"], at("x_added", "wo"))
                    norm_act(act, "mlp")
                    turn_act(act, xa_hi, "mlp", lambda k: col("norm_mlp_g", l, k))

        def m_col(l, k):
            return params_m[:, bass.ds(l * 8 + k, 1)]

        def layer_dve(dve, l):
            def unit(name, i):
                dve.wait_ge(S["unit_done"], at("unit_done", ("u", at_unit[name, i])))

            def gate_split():
                dve.wait_ge(S["gate_hi"], at("gate_hi"))
                nc.vector.tensor_tensor(gate_lo[:], gate_raw[:], gate_hi[:].bitcast(F32), ALU.subtract).then_inc(
                    S["gate_lo"], mark("gate_lo"))

            def gate_start():
                dve.wait_ge(S["gate_done"], at("gate_done"))
                bi, bf = gate_b[0:M_HEADS, bass.ds(l, 1)], gate_b[GATE_F:GATE_F + M_HEADS, bass.ds(l, 1)]
                nc.vector.tensor_scalar(g_i, att[0][0:M_HEADS, 0:SEQ], bi, None, ALU.add).then_inc(
                    S["gate_in"], mark("gate_in", 0))
                nc.vector.tensor_scalar(g_f, att[0][GATE_F:GATE_F + M_HEADS, 0:SEQ], bf, None, ALU.add).then_inc(
                    S["gate_in"], mark("gate_in", 1))
                dve.wait_ge(S["gate_in"], at("gate_in", 1))
                nc.vector.scalar_tensor_tensor(g_n, g_f, -1.0, g_f, ALU.mult, ALU.min).then_inc(
                    S["gate_nabs"], mark("gate_nabs"))

            def gate_rows():
                dve.wait_ge(S["gate_ln"], at("gate_ln"))
                nc.vector.scalar_tensor_tensor(g_n, g_f, 0.0, g_e, ALU.min, ALU.subtract).then_inc(
                    S["gate_row"], mark("gate_row", 0))
                dve.wait_ge(S["gate_row"], at("gate_row", 0))
                nc.vector.tensor_tensor_scan(g_B, ones_row, g_n, 0.0, ALU.mult, ALU.add).then_inc(
                    S["gate_row"], mark("gate_row", 1))
                dve.wait_ge(S["gate_row"], at("gate_row", 1))
                nc.vector.tensor_tensor(g_a, g_i, g_B, ALU.subtract).then_inc(S["gate_row"], mark("gate_row", 2))
                dve.wait_ge(S["gate_row"], at("gate_row", 2))
                nc.vector.tensor_tensor_scan(g_f, zero_row, g_a, 0.0, ALU.max, ALU.max).then_inc(
                    S["gate_row"], mark("gate_row", 3))
                dve.wait_ge(S["gate_row"], at("gate_row", 3))
                nc.vector.tensor_scalar(g_M, g_f, -1.0, None, ALU.mult).then_inc(S["gate_row"], mark("gate_row", 4))
                nc.vector.scalar_tensor_tensor(g_m, g_B, -1.0, g_f, ALU.mult, ALU.subtract).then_inc(
                    S["gate_m"], mark("gate_m"))

            def conv(tiles):
                dve.wait_ge(S["pads_ready"], at("pads_ready", 1))
                dve.wait_ge(S["emptied_act"], at("emptied_act", ("mqk", 3)))
                for k in tiles:
                    nc.vector.tensor_scalar(qk[:, k, :], mqk[:, k, 0:SEQ], col("conv_w", l, k), col("conv_b", l, k),
                                                ALU.mult, ALU.add).then_inc(S["conv_tap"], mark("conv_tap", (k, 0)))
                for j in range(1, CONV_K):
                    for k in tiles:
                        dve.wait_ge(S["conv_tap"], at("conv_tap", (k, j - 1)))
                        nc.vector.scalar_tensor_tensor(qk[:, k, :], mqk[:, k, j:j + SEQ], col("conv_w", l, 8 * j + k),
                                                           qk[:, k, :], ALU.mult, ALU.add).then_inc(
                            S["conv" if j == CONV_K - 1 else "conv_tap"], mark("conv" if j == CONV_K - 1 else "conv_tap", k if j == CONV_K - 1 else (k, j)))

            def decay():
                dve.wait_ge(S["columns_done"], at("columns_done"))
                nc.vector.tensor_copy(acol, att[2][:, 0:16]).then_inc(S["acol_ready"], mark("acol_ready"))
                dve.wait_ge(S["acol_ready"], at("acol_ready"))
                for h in range(M_HEADS):
                    row = att[h // 2][:, (h % 2) * SEQ:(h % 2 + 1) * SEQ]
                    nc.vector.tensor_scalar(zw[:, h, 0:SEQ], row, acol[:, h:h + 1], None, ALU.add).then_inc(
                        S["z_ready"], mark("z_ready", (h, 0)))
                    nc.vector.tensor_scalar(zw[:, h, SEQ:384], row[:, P:2 * P], acol[:, 4 + h:5 + h], None, ALU.add).then_inc(
                        S["z_ready"], mark("z_ready", (h, 1)))

            def s_take(h):
                dve.wait_ge(S["w_ready"], at("w_ready"))
                dve.wait_ge(S["kq_done"], at("kq_done", h))
                if h >= 2:
                    dve.wait_ge(S["num_done"], at("num_done", (h - 2, 1)))
                nc.vector.scalar_tensor_tensor(sm[:, h % 2, :], att[2 + h % 2][:, 0:384], M_DK ** -0.5, zw[:, h, :],
                                                   ALU.mult, ALU.mult).then_inc(S["s_ready"], mark("s_ready", h))

            def num_scale():
                for t in range(TT):
                    d = num[:, t, :, M_DV]
                    dve.wait_ge(S["num_ready"], at("num_ready", (3, t)))
                    nc.vector.scalar_tensor_tensor(n_dn[:, 4 * t:4 * t + 4], d, -1.0, acol[:, 8 + 4 * t:12 + 4 * t],
                                                       ALU.mult, ALU.max).then_inc(S["den_part"], mark("den_part", t))
                    dve.wait_ge(S["den_part"], at("den_part", t))
                    nc.vector.tensor_tensor(n_dn[:, 4 * t:4 * t + 4], n_dn[:, 4 * t:4 * t + 4], d, ALU.max).then_inc(
                        S["den_abs"], mark("den_abs", t))
                dve.wait_ge(S["den_abs"], at("den_abs", 1))
                nc.vector.reciprocal(n_rec, n_dn).then_inc(S["den_rec"], mark("den_rec"))

            def hm():
                dve.wait_ge(S["mo_sig"], at("mo_sig"))
                dve.wait_ge(S["num_norm"], at("num_norm", 3))
                nc.vector.scalar_tensor_tensor(n_c, n_ms, M_DV ** 0.5, n_rec, ALU.mult, ALU.mult).then_inc(
                    S["num_factor"], mark("num_factor"))
                dve.wait_ge(S["num_factor"], at("num_factor"))
                for t in range(TT):
                    for h in range(M_HEADS):
                        piece = mo[:, t, h * M_DV:(h + 1) * M_DV]
                        nc.vector.scalar_tensor_tensor(piece, num[:, t, h, 0:M_DV], n_c[:, 4 * t + h:4 * t + h + 1], piece,
                                                           ALU.mult, ALU.mult).then_inc(S["hm_ready"], mark("hm_ready", (t, h)))

            def logits(j):
                dve.wait_ge(S["scores_done"], at("scores_done", j))
                if j >= 1:
                    dve.wait_ge(S["probs_turned"], at("probs_turned", (j - 1, 2)))
                if j == 0:
                    dve.wait_ge(S["bias_loaded"], at("bias_loaded"))
                heads = slice(GROUP * j, GROUP * (j + 1))
                nc.vector.tensor_tensor(lg[:, :, 0:P], att[0][:].rearrange("p (h k) -> p h k", h=GROUP),
                                            bias[:, heads, P:2 * P], ALU.add).then_inc(S["lg_ready"], mark("lg_ready", (j, 0)))
                for i in range(2):
                    nc.vector.tensor_tensor(lg[:, 2 * i:2 * i + 2, P:3 * P], att[1 + i][:].rearrange("p (h k) -> p h k", h=2),
                                                bias[:, GROUP * j + 2 * i:GROUP * j + 2 * i + 2, :], ALU.add).then_inc(
                        S["lg_ready"], mark("lg_ready", (j, 1 + i)))
                dve.wait_ge(S["lg_ready"], at("lg_ready", (j, 2)))
                nc.vector.tensor_reduce(mx[:, 0:4], lg[:, :, 0:P], X, ALU.max).then_inc(S["mx_ready"], mark("mx_ready", (j, 0)))
                nc.vector.tensor_reduce(mx[:, 4:8], lg[:, :, P:3 * P], X, ALU.max).then_inc(
                    S["mx_ready"], mark("mx_ready", (j, 1)))
                dve.wait_ge(S["mx_ready"], at("mx_ready", (j, 1)))
                sink = neg_sink[:, bass.ds(l, 1), heads].rearrange("p o h -> p (o h)")
                for t in range(TT):
                    nc.vector.scalar_tensor_tensor(negm[:, 4 * t:4 * t + 4], mx[:, 4 * t:4 * t + 4], -1.0, sink,
                                                       ALU.mult, ALU.min).then_inc(
                        S["negm_part" if t == 0 else "negm_ready"], mark("negm_part" if t == 0 else "negm_ready", j))
                dve.wait_ge(S["negm_ready"], at("negm_ready", j))
                for t in range(TT):
                    nc.vector.tensor_tensor(esink[:, 4 * t:4 * t + 4], negm[:, 4 * t:4 * t + 4], sink, ALU.subtract).then_inc(
                        S["sink_part" if t == 0 else "sink_diff"], mark("sink_part" if t == 0 else "sink_diff", j))

            def denominators(j):
                dve.wait_ge(S["sink_exp"], at("sink_exp", j))
                nc.vector.tensor_tensor(rinv, sums, esink, ALU.add).then_inc(S["denom"], mark("denom", j))
                dve.wait_ge(S["denom"], at("denom", j))
                nc.vector.reciprocal(rinv, rinv).then_inc(S["rinv_ready"], mark("rinv_ready", j))

            def ha_take(j):
                dve.wait_ge(S["pv_done"], at("pv_done", j))
                dve.wait_ge(S["rinv_ready"], at("rinv_ready", j))
                for t in range(TT):
                    nc.vector.tensor_tensor(ha[:, t, j * 256:(j + 1) * 256].rearrange("p (h d) -> p h d", h=GROUP),
                                                att[3][:, t * 256:(t + 1) * 256].rearrange("p (h d) -> p h d", h=GROUP),
                                                rinv[:, 4 * t:4 * t + 4].unsqueeze(2).broadcast_to([P, GROUP, A_DH]), ALU.mult).then_inc(
                        S["ha_ready"], mark("ha_ready", (j, t)))

            def take(name, i):
                b = BANKS[name, i]
                if name == "ak":
                    unit(name, i)
                    for j in range(A_KV):
                        ps = b[0][64 * (j % 2):64 * (j % 2) + 64, (j // 2) * SEQ:(j // 2 + 1) * SEQ]
                        for half in range(2):
                            nc.vector.tensor_copy(ak[64 * half:64 * half + 64, half, j, :], ps).then_inc(
                                S["emptied_dve" if (j, half) == (3, 1) else "ak_part"], mark("emptied_dve" if (j, half) == (3, 1) else "ak_part", (name, i) if (j, half) == (3, 1) else (j, half)))
                elif name == "mo" and i % 2 == 1:
                    unit(name, i)
                    for t in range(TT):
                        nc.vector.tensor_copy(mo[:, t, 512 * (i // 2):512 * (i // 2 + 1)], b[t][:]).then_inc(
                            S["emptied_dve"], mark("emptied_dve", (name, i - 1 + t)))
                elif name in ("ga", "gb"):
                    unit(name, i)
                    tile = ga if name == "ga" else gb
                    nc.vector.tensor_copy(tile[:, 2 * i:2 * i + 2, :], b[0][:].rearrange("p (n t) -> p n t", n=2)).then_inc(
                        S["emptied_dve"], mark("emptied_dve", (name, i)))
                elif name in ("bm", "ba"):
                    tile = ga if name == "bm" else gb
                    piece = tile[:, 2 * i:2 * i + 2, :]
                    dve.wait_ge(S["g_sig"], at("g_sig", 0 if name == "bm" else 1))
                    unit(name, i)
                    nc.vector.tensor_tensor(piece, b[0][:].rearrange("p (n t) -> p n t", n=2), piece, ALU.mult).then_inc(
                        S["emptied_dve"], mark("emptied_dve", (name, i)))
                    if name == "ba":
                        y = ga[:, 2 * i:2 * i + 2, :]
                        dve.wait_ge(S["emptied_dve"], at("emptied_dve", (name, i)))
                        nc.vector.tensor_tensor(y, y, piece, ALU.add).then_inc(S["y_ready"], mark("y_ready", i))
                        dve.wait_ge(S["y_hi"], at("y_hi", i))
                        nc.vector.tensor_tensor(xb_lo[:, 2 * i:2 * i + 2, :], y, xb_hi[:, 2 * i:2 * i + 2, :].bitcast(F32),
                                                    ALU.subtract).then_inc(S["y_lo"], mark("y_lo", i))
                elif name == "wo" and i % 2 == 1:
                    unit(name, i)
                    for t in range(TT):
                        piece = x_res[:, t, 512 * (i // 2):512 * (i // 2 + 1)]
                        nc.vector.tensor_tensor(piece, b[t][:], piece, ALU.add).then_inc(
                            S["emptied_dve"], mark("emptied_dve", (name, i - 1 + t)))
                    if i == 3:
                        dve.wait_ge(S["emptied_dve"], at("emptied_dve", ("wo", 3)))
                        nc.vector.memset(small[:, 250:251], 0.0).then_inc(S["x_added"], mark("x_added", "wo"))
                elif name == "up":
                    k0 = 4 * (i // 2 % 2) + 2 * (i % 2)
                    unit(name, i)
                    if i >= 2:
                        dve.wait_ge(S["ff_sq"], at("ff_sq", i - 2))
                    nc.vector.tensor_scalar(sq[:, i % 2, :], b[0][:], 0.0, None, ALU.max).then_inc(
                        S["emptied_dve"], mark("emptied_dve", (name, i)))
                    dve.wait_ge(S["ff_hi"], at("ff_hi", i))
                    nc.vector.tensor_tensor(xb_lo[:, k0:k0 + 2, :], sq[:, 2 + i % 2, :].rearrange("p (n t) -> p n t", n=2),
                                                xb_hi[:, k0:k0 + 2, :].bitcast(F32), ALU.subtract).then_inc(
                        S["ff_lo"], mark("ff_lo", i))
                elif (name, i) == ("down", 15):
                    unit(name, i)
                    for half in range(2):
                        for t in range(TT):
                            piece = x_res[:, t, 512 * half:512 * half + 512]
                            nc.vector.tensor_tensor(piece, BANKS["down", half][t][:], piece, ALU.add).then_inc(
                                S["mlp_added"], mark("mlp_added", (half, t)))
                    dve.wait_ge(S["mlp_added"], at("mlp_added", (1, 1)))

            split_lo(dve, 0, False)
            split_lo(dve, 1, False)
            norm_dve(dve, "mix")
            turn_dve(dve, xa_hi, xa_lo, "mix", lambda k: col("norm_mix_g", l, k))
            for u, (name, i, kind) in enumerate(units):
                if u + 2 < NU:
                    split_lo(dve, u + 2, False)
                take(name, i)
                if (name, i) == ("mqk", 0):
                    gate_split()
                elif (name, i) == ("mv", 0):
                    gate_start()
                    conv((0, 1, 2, 3))
                elif (name, i) == ("mv", 1):
                    gate_rows()
                    conv((4, 5, 6, 7))
                elif (name, i) == ("aq", 1):
                    decay()
                elif (name, i) == ("aq", 2):
                    s_take(0)
                    s_take(1)
                elif (name, i) == ("aq", 3):
                    s_take(2)
                elif (name, i) == ("ak", 0):
                    s_take(3)
                elif (name, i) == ("mo", 1):
                    logits(0)
                    num_scale()
                elif (name, i) == ("mo", 2):
                    denominators(0)
                elif (name, i) == ("mo", 3):
                    ha_take(0)
                    logits(1)
                elif (name, i) == ("ga", 0):
                    denominators(1)
                elif (name, i) == ("ga", 1):
                    ha_take(1)
                    logits(2)
                elif (name, i) == ("ga", 2):
                    denominators(2)
                elif (name, i) == ("ga", 3):
                    ha_take(2)
                    logits(3)
                elif (name, i) == ("gb", 0):
                    denominators(3)
                elif (name, i) == ("gb", 1):
                    ha_take(3)
                    hm()
                elif (name, i) == ("gb", 3):
                    turn_dve(dve, xb_hi, xb_lo, "hm", lambda k: m_col(l, k))
                elif (name, i) == ("bm", 0):
                    turn_dve(dve, xa_hi, xa_lo, "ha", lambda k: 1.0)
                elif (name, i) == ("wo", 3):
                    norm_dve(dve, "mlp")
                    turn_dve(dve, xa_hi, xa_lo, "mlp", lambda k: col("norm_mlp_g", l, k))

        def layer_pool(pool, l):
            norm_pool(pool, "mix")
            nc.gpsimd.memset(mv[:, :, :, M_DV:VW], 1.0).then_inc(S["pads_ready"], mark("pads_ready", 0))
            nc.gpsimd.memset(mqk[:, :, 0:CONV_K - 1], 0.0).then_inc(S["pads_ready"], mark("pads_ready", 1))
            for k in range(4):
                pool.wait_ge(S["silu_sig"], at("silu_sig", k))
                for kk in (2 * k, 2 * k + 1):
                    nc.gpsimd.tensor_tensor(qk[:, kk, :], qk[:, kk, :], sig[:, kk, :], ALU.mult).then_inc(
                        S["silu"], mark("silu", kk))
            pool.wait_ge(S["z_ready"], at("z_ready", (3, 1)))
            nc.gpsimd.tensor_tensor(idle, eps_d[:, 0:1], eps_d[:, 0:1], ALU.add)
            for t in range(TT):
                pool.wait_ge(S["consts"], at("consts", "ident", "pre"))
                d = zw[:, :, 0:P] if t == 0 else zw[:, :, SEQ:384]
                nc.gpsimd.affine_select(out=d, in_=d, compare_op=ALU.is_ge, fill=NEG, base=0,
                                            pattern=[[0, M_HEADS], [1, P]], channel_multiplier=-1).then_inc(
                    S["z_masked"], mark("z_masked", t))
            pool.wait_ge(S["num_ssq"], at("num_ssq", (1, 3)))
            pool.wait_ge(S["den_rec"], at("den_rec"))
            nc.gpsimd.tensor_tensor(n_ms, n_rec, n_rec, ALU.mult).then_inc(S["num_norm"], mark("num_norm", 0))
            pool.wait_ge(S["num_norm"], at("num_norm", 0))
            nc.gpsimd.tensor_tensor(n_ms, n_ms, n_ss, ALU.mult).then_inc(S["num_norm"], mark("num_norm", 1))
            pool.wait_ge(S["num_norm"], at("num_norm", 1))
            nc.gpsimd.tensor_tensor(n_ms, n_ms, eps_v, ALU.add).then_inc(S["num_norm"], mark("num_norm", 2))
            pool.wait_ge(S["num_norm"], at("num_norm", 2))
            nc.gpsimd.tensor_tensor(n_ms, n_ms, minus_half[:, 0:8], ALU.pow).then_inc(S["num_norm"], mark("num_norm", 3))
            norm_pool(pool, "mlp")

        def start_pool(pool):
            counts.region = "pre"
            nc.gpsimd.memset(ident[:], 0.0).then_inc(S["consts"], mark("consts", "zero"))
            nc.gpsimd.memset(minus_half[:], -0.5).then_inc(S["unit_done"], mark("unit_done", "free", RING))
            nc.gpsimd.memset(eps_d, D * EPS).then_inc(S["consts"], mark("consts", "eps_d"))
            nc.gpsimd.memset(zero_all, 0.0).then_inc(S["rows_used"], mark("rows_used", "free", GATHER))
            nc.gpsimd.memset(eps_v, M_DV * EPS).then_inc(S["consts"], mark("consts", "eps_v"))
            nc.gpsimd.memset(gate_raw[:], 0.0).then_inc(S["consts"], mark("consts", "gate_raw"))
            pool.wait_ge(S["consts"], at("consts", "gate_raw"))
            nc.gpsimd.affine_select(out=ident[:], in_=ident[:], compare_op=ALU.not_equal, fill=1.0, base=0,
                                        pattern=[[-1, P]], channel_multiplier=1).then_inc(S["consts"], mark("consts", "ident"))
            nc.gpsimd.memset(scan_in[:, 0:1], 1.0).then_inc(S["consts"], mark("consts", "ones"))
            nc.gpsimd.memset(scan_in[:, 1:2], 0.0).then_inc(S["consts"], mark("consts", "zeros"))
            nc.gpsimd.memset(ak, 0.0).then_inc(S["consts"], mark("consts", "ak"))
            pool.wait_ge(S["params_loaded"], at("params_loaded", "sink"))
            nc.gpsimd.tensor_scalar(neg_sink[:], neg_sink[:], -1.0, None, ALU.mult).then_inc(
                S["consts"], mark("consts", "sink"))

        def start_pe(pe):
            counts.region = "pre"
            pe.wait_ge(S["params_loaded"], at("params_loaded", "sink"))
            pe.wait_ge(S["consts"], at("consts", "ident"))
            nc.tensor.transpose(att[0][:, 0:P], rows_p, ident[:])
            nc.tensor.transpose(att[1][:, 0:16], rows_m[0:16, :], ident[0:16, 0:16])
            nc.tensor.matmul(att[2][0:A_HEADS, 0:WINDOW], rel_sb, onehot, start=True, stop=True).then_inc(
                S["start_done"], mark("start_done"))

        def start_act(act):
            counts.region = "pre"
            act.wait_ge(S["x_loaded"], at("x_loaded"))
            act.wait_ge(S["start_taken"], at("start_taken", 1))
            act.wait_ge(S["consts"], at("consts", "sink"))

        def start_dve(dve):
            counts.region = "pre"
            nc.vector.memset(toep, NEG).then_inc(S["lo_ready"], mark("lo_ready", "free", RAW_RING))
            nc.vector.memset(small[:, 250:251], 0.0).then_inc(S["mlp_added"], mark("mlp_added", "start"))
            dve.wait_ge(S["start_done"], at("start_done"))
            nc.vector.tensor_copy(params[:], att[0][:, 0:P]).then_inc(S["start_taken"], mark("start_taken", 0))
            nc.vector.tensor_copy(params_m[:], att[1][:, 0:16]).then_inc(S["start_taken"], mark("start_taken", 1))
            dve.wait_ge(S["lo_ready"], at("lo_ready", "free"))
            nc.vector.tensor_copy(toep[:, P:2 * P], att[2][0:A_HEADS, 0:WINDOW]).then_inc(
                S["toep_ready"], mark("toep_ready", 1))

        for i in range(2):
            BANKS["qa", i], BANKS["ka", i], BANKS["qb", i], BANKS["kb", i] = [acc[i]], [acc[2 + i]], [acc[2 + i]], [acc[i]]
            BANKS["va", i], BANKS["vb", i] = acc[0:2], acc[2:4]
        for i in range(4):
            BANKS["ga2", i] = BANKS["gb2", i] = [acc[i]]
            BANKS["yab", i] = acc[2 * (i % 2):2 * (i % 2) + 2]
            BANKS["mix", i] = acc[2 * (i // 2):2 * (i // 2) + 2]
        for i in range(8):
            BANKS["pq", i] = [acc[i % 4]]
        BEFORE2 = {("va", 0): [("qa", 0), ("qa", 1)], ("qb", 0): [("ka", 0)], ("qb", 1): [("ka", 1)],
                   ("kb", 0): [("va", 0)], ("kb", 1): [("va", 1)], ("vb", 0): [("qb", 0), ("qb", 1)],
                   ("ga2", 0): [("kb", 0)], ("ga2", 1): [("kb", 1)], ("ga2", 2): [("vb", 0)], ("ga2", 3): [("vb", 1)],
                   ("yab", 0): [("gb2", 0), ("gb2", 1)], ("yab", 1): [("gb2", 2), ("gb2", 3)],
                   ("yab", 2): [("yab", 0)], ("yab", 3): [("yab", 1)], ("mix", 0): [("yab", 2)], ("mix", 2): [("yab", 3)],
                   ("pq", 0): [("mix", 0)], ("pq", 1): [("mix", 1)], ("pq", 2): [("mix", 2)], ("pq", 3): [("mix", 3)]}
        for i in range(4):
            BEFORE2["gb2", i] = [("ga2", i)]
            BEFORE2["pq", 4 + i] = [("pq", i)]
        BY_DVE2 = {"yab", "mix"}

        def emptied2(eng, name, i):
            eng.wait_ge(S["emptied_dve" if name in BY_DVE2 else "emptied_act"], at("emptied_dve" if name in BY_DVE2 else "emptied_act", (name, i)))

        PAIRS = H2 // 2
        FIRST_ATT = 4
        STEPS = [(tag, p) for tag in "ms" for p in range(PAIRS)]
        mx2, negm2, sums2, rinv2 = (small[:, 100 + 4 * i:104 + 4 * i] for i in range(4))

        def pair_at(u):
            n_, odd = divmod(u - FIRST_ATT, 2)
            if not 0 <= n_ < len(STEPS):
                return False, None, None
            return odd == 0, STEPS[n_], STEPS[n_ - 1] if n_ else None

        def second_pe(pe):
            def turn_norm(tag):
                turn_pe(pe, lambda k, t: hn[:, t, k * P:(k + 1) * P], tag, [("hn_ready", (tag, 0)), ("hn_ready", (tag, 1))])

            def scores(tag, p):
                q, k_ = (qa, ka) if tag == "m" else (qb, kb)
                emptied2(pe, "ka" if tag == "m" else "kb", 1)
                if (tag, p) == ("m", 0):
                    pe.wait_ge(S["x_lo"], at("x_lo", ("n1", KT - 1)))
                else:
                    before = STEPS[STEPS.index((tag, p)) - 1]
                    pe.wait_ge(S["y_ready2"], at("y_ready2", before))
                for e in range(2):
                    rows = slice(64 * e, 64 * e + 64)
                    nc.tensor.matmul(att[e][:, 0:P], q[rows, p, 0:P], k_[rows, p, 0:P], start=True, stop=True)
                    m = nc.tensor.matmul(att[e][:, P:3 * P], q[rows, p, P:2 * P], k_[rows, p, :], start=True, stop=True)
                m.then_inc(S["pair_scores"], mark("pair_scores", (tag, p)))

            def turned(tag, p):
                pe.wait_ge(S["pair_probs"], at("pair_probs", (tag, p)))
                for e in range(2):
                    for c in range(3):
                        m = nc.tensor.transpose(att[2 + e][:, c * P:(c + 1) * P], lg2[:, e, c * P:(c + 1) * P], ident[:])
                    m.then_inc(S["pair_turned"], mark("pair_turned", (tag, p, e)))

            def product(tag, p):
                v = va if tag == "m" else vb
                emptied2(pe, "va" if tag == "m" else "vb", 1)
                pe.wait_ge(S["pair_pT"], at("pair_pT", (tag, p, 1)))
                for e in range(2):
                    h = 2 * p + e
                    v0, v1 = v[:, 0, h * DH2:(h + 1) * DH2], v[:, 1, h * DH2:(h + 1) * DH2]
                    nc.tensor.matmul(att[0][:, e * DH2:(e + 1) * DH2], pT2[:, e, 0, :], v0, start=True, stop=True)
                    second = att[0][:, P + e * DH2:P + (e + 1) * DH2]
                    nc.tensor.matmul(second, pT2[:, e, 1, :], v0, start=True, stop=False)
                    m = nc.tensor.matmul(second, pT2[:, e, 2, :], v1, start=False, stop=True)
                m.then_inc(S["pair_done"], mark("pair_done", (tag, p)))

            def turn_y():
                pe.wait_ge(S["pair_pT"], at("pair_pT", ("s", PAIRS - 1, 1)))
                ready = ("y_ready2", ("s", PAIRS - 1))
                turn_pe(pe, lambda k, t: (ya if k < 4 else yb)[:, t, (k % 4) * P:(k % 4 + 1) * P], "y2", [ready, ready])

            def turn_keys():
                pe.wait_ge(S["keys_loaded"], at("keys_loaded", HP - 1))
                for b in range(4):
                    for i in range(4):
                        m = nc.tensor.transpose(att[b][:, i * P:(i + 1) * P], raw_keys[:, 4 * b + i, :], ident[:])
                    m.then_inc(S["keys_turned"], mark("keys_turned", b))

            def rank_keys(h):
                emptied2(pe, "pq", h)
                if h >= 2:
                    pe.wait_ge(S["rank_ready"], at("rank_ready", (h - 2, TT - 1)))
                else:
                    pe.wait_ge(S["x_lo"], at("x_lo", ("n2", KT - 1)))
                for t in range(TT):
                    for i in range(2):
                        m = nc.tensor.matmul(att[2 * t + h % 2][:, i * P:(i + 1) * P], queries[:, 2 * h + i, t * P:(t + 1) * P],
                                             keys[:, 2 * h + i, :], start=True, stop=True)
                    m.then_inc(S["rank_done"], mark("rank_done", (h, t)))

            operand_ready = {("qa", 0): ("x_lo", ("n1", KT - 1)), ("yab", 0): ("x_lo", ("y2", KT - 1)),
                             ("mix", 0): ("y_lo", 3), ("pq", 0): ("x_lo", ("n2", KT - 1))}
            turn_norm("n1")
            for u, (name, i, kind) in enumerate(units2):
                pe.wait_ge(S["lo_ready"], at("lo_ready", ("u2", u)))
                for p in BEFORE2.get((name, i), []):
                    emptied2(pe, *p)
                if (name, i) in operand_ready:
                    pe.wait_ge(S[operand_ready[name, i][0]], at(*operand_ready[name, i]))
                xh, xl = (xb_hi, xb_lo) if name in ("yab", "pq") else (xa_hi, xa_lo)
                b, s = BANKS[name, i], u % RING
                if kind == "F":
                    unit_f(b, s, xh, xl, ("u2", u))
                elif kind == "Y":
                    unit_y(b, s, xh, xl, ("u2", u))
                else:
                    unit_t(b, s, xh, xl, 4 * (i % 2), i % 2 == 0, i % 2 == 1, ("u2", u))
                scored, pair, before = pair_at(u)
                if pair and scored:
                    if before:
                        product(*before)
                    scores(*pair)
                elif pair:
                    turned(*pair)
                if (name, i) == ("gb2", 3):
                    product(*STEPS[-1])
                    turn_y()
                elif (name, i) == ("mix", 0):
                    turn_keys()
                elif (name, i) == ("mix", 3):
                    pe.wait_ge(S["keys_ready"], at("keys_ready", 3))
                    turn_norm("n2")
                if name == "pq" and i >= 1:
                    rank_keys(i - 1)
            rank_keys(P_HEADS - 1)

        def second_act(act):
            def unit(name, i):
                act.wait_ge(S["unit_done"], at("unit_done", ("u2", at_unit2[name, i])))

            def weights(tag, p):
                if tag == "m":
                    act.wait_ge(S["pair_negm"], at("pair_negm", p))
                    for e in range(2):
                        for t in range(TT):
                            piece = lg2[:, e, 0:P] if t == 0 else lg2[:, e, P:3 * P]
                            last = (e, t) == (1, 1)
                            nc.scalar.activation(piece, piece, ACT.Exp, bias=negm2[:, 2 * t + e:2 * t + e + 1],
                                                     accum_out=sums2[:, 2 * t + e:2 * t + e + 1]).then_inc(
                                S["pair_probs" if last else "pair_part"], mark("pair_probs" if last else "pair_part", (tag, p) if last else (p, e, t)))
                else:
                    act.wait_ge(S["pair_scores"], at("pair_scores", (tag, p)))
                    if p >= 1:
                        act.wait_ge(S["pair_probs"], at("pair_probs", (tag, p - 1)))
                    for e in range(2):
                        nc.scalar.activation(stay[:, e, :], att[e][:, 0:384], ACT.Sigmoid, scale=-1.0).then_inc(
                            S["odds"], mark("odds", (p, e, 0)))
                        nc.scalar.activation(stop[:, e, :], att[e][:, 0:384], ACT.Sigmoid).then_inc(
                            S["odds"], mark("odds", (p, e, 1)))

            def probs_take(tag, p):
                n_ = STEPS.index((tag, p))
                if n_ >= 1:
                    act.wait_ge(S["pair_done"], at("pair_done", STEPS[n_ - 1]))
                for e in range(2):
                    act.wait_ge(S["pair_turned"], at("pair_turned", (tag, p, e)))
                    nc.scalar.copy(pT2[:, e, :, :], att[2 + e][:, 0:384].rearrange("p (c k) -> p c k", c=3)).then_inc(
                        S["pair_pT"], mark("pair_pT", (tag, p, e)))

            def keys_take():
                for b in range(4):
                    act.wait_ge(S["keys_turned"], at("keys_turned", b))
                    nc.scalar.copy(keys[:, 4 * b:4 * b + 4, :], att[b][:].rearrange("p (h n) -> p h n", h=4)).then_inc(
                        S["keys_ready"], mark("keys_ready", b))

            def rank_take(h):
                for t in range(TT):
                    act.wait_ge(S["rank_done"], at("rank_done", (h, t)))
                    nc.scalar.copy(rank[t][:, 2 * h:2 * h + 2, :],
                                       att[2 * t + h % 2][:, 0:2 * P].rearrange("p (i n) -> p i n", i=2)).then_inc(
                        S["rank_ready"], mark("rank_ready", (h, t)))

            def take(name, i):
                b = BANKS[name, i]
                two = b[0][:].rearrange("p (n t) -> p n t", n=2)
                if name in ("qa", "qb"):
                    unit(name, i)
                    q = qa if name == "qa" else qb
                    nc.scalar.mul(q[:, 2 * i:2 * i + 2, :], two, DH2 ** -0.5).then_inc(
                        S["emptied_act"], mark("emptied_act", (name, i)))
                elif name in ("ka", "kb"):
                    unit(name, i)
                    k_ = ka if name == "ka" else kb
                    nc.scalar.copy(k_[:, 2 * i:2 * i + 2, :], two).then_inc(S["emptied_act"], mark("emptied_act", (name, i)))
                elif name in ("va", "vb") and i == 1:
                    unit(name, i)
                    v = va if name == "va" else vb
                    for t in range(TT):
                        nc.scalar.copy(v[:, t, :], b[t][:]).then_inc(S["emptied_act"], mark("emptied_act", (name, t)))
                elif name in ("ga2", "gb2"):
                    unit(name, i)
                    g = ga if name == "ga2" else gb
                    nc.scalar.activation(g[:, 2 * i:2 * i + 2, :], two, ACT.Sigmoid).then_inc(
                        S["emptied_act"], mark("emptied_act", (name, i)))
                elif name == "yab":
                    act.wait_ge(S["y_ready"], at("y_ready", i))
                    nc.scalar.copy(xa_hi[:, 2 * i:2 * i + 2, :], ga[:, 2 * i:2 * i + 2, :]).then_inc(S["y_hi"], mark("y_hi", i))
                elif name == "pq":
                    unit(name, i)
                    nc.scalar.copy(queries[:, 2 * i:2 * i + 2, :], two).then_inc(
                        S["emptied_act"], mark("emptied_act", (name, i)))

            split_hi(act, 0, True)
            split_hi(act, 1, True)
            norm_act(act, "fin")
            norm_act(act, "n1")
            turn_act(act, xa_hi, "n1", lambda k: col("norm1_g_2", 0, k))
            for u, (name, i, kind) in enumerate(units2):
                if u + 2 < len(units2):
                    split_hi(act, u + 2, True)
                take(name, i)
                scored, pair, _ = pair_at(u)
                if pair and scored:
                    weights(*pair)
                elif pair:
                    probs_take(*pair)
                if (name, i) == ("gb2", 3):
                    turn_act(act, xb_hi, "y2", lambda k: 1.0)
                elif (name, i) == ("mix", 0):
                    keys_take()
                elif (name, i) == ("mix", 3):
                    act.wait_ge(S["emptied_dve"], at("emptied_dve", ("mix", 3)))
                    norm_act(act, "n2")
                    turn_act(act, xb_hi, "n2", lambda k: col("norm2_g_2", 0, k))
                if name == "pq" and i >= 1:
                    rank_take(i - 1)
            rank_take(P_HEADS - 1)
            for t in range(TT):
                act.wait_ge(S["best_diff"], at("best_diff", t))
                nc.scalar.activation(weight[:, t * SLOTS:(t + 1) * SLOTS], weight[:, t * SLOTS:(t + 1) * SLOTS], ACT.Exp).then_inc(
                    S["best_exp"], mark("best_exp", t))
            for t in range(TT):
                act.wait_ge(S["rows_used"], GATHER + (t + 1) * SLOTS)
                nc.scalar.activation(dots[:, t * SLOTS:(t + 1) * SLOTS], dots[:, t * SLOTS:(t + 1) * SLOTS], ACT.Gelu).then_inc(
                    S["gelu_ready"], mark("gelu_ready", t))
            act.wait_ge(S["rows_used"], GATHER + 4 * SLOTS)
            norm_act(act, "last")

        def second_dve(dve):
            def unit(name, i):
                dve.wait_ge(S["unit_done"], at("unit_done", ("u2", at_unit2[name, i])))

            def logits(p):
                dve.wait_ge(S["pair_scores"], at("pair_scores", ("m", p)))
                dve.wait_ge(S["moba_bias"], at("moba_bias", 1))
                if p >= 1:
                    dve.wait_ge(S["pair_turned"], at("pair_turned", ("m", p - 1, 1)))
                for e in range(2):
                    nc.vector.tensor_tensor(lg2[:, e, :], att[e][:, 0:384], moba_bias[:, 2 * p + e, :], ALU.add).then_inc(
                        S["pair_lg"], mark("pair_lg", (p, e)))
                dve.wait_ge(S["pair_lg"], at("pair_lg", (p, 1)))
                nc.vector.tensor_reduce(mx2[:, 0:2], lg2[:, :, 0:P], X, ALU.max).then_inc(S["pair_mx"], mark("pair_mx", (p, 0)))
                nc.vector.tensor_reduce(mx2[:, 2:4], lg2[:, :, P:3 * P], X, ALU.max).then_inc(
                    S["pair_mx"], mark("pair_mx", (p, 1)))
                dve.wait_ge(S["pair_mx"], at("pair_mx", (p, 1)))
                nc.vector.tensor_scalar(negm2, mx2, -1.0, None, ALU.mult).then_inc(S["pair_negm"], mark("pair_negm", p))

            def sticks(p):
                dve.wait_ge(S["odds_masked"], at("odds_masked", (p, 3)))
                for e in range(2):
                    for c0, c1 in ((0, P), (P, 3 * P)):
                        nc.vector.tensor_tensor_scan(left[:, e, c0:c1 - 1][:, ::-1], stay[:, e, c0 + 1:c1][:, ::-1],
                                                         zero_all[:, 0:1].broadcast_to([P, c1 - c0 - 1]), 1.0, ALU.mult, ALU.add).then_inc(
                            S["left_ready"], mark("left_ready", (p, e, c0)))
                dve.wait_ge(S["left_ready"], at("left_ready", (p, 1, P)))
                dve.wait_ge(S["pair_turned"], at("pair_turned", ("m", PAIRS - 1, 1) if p == 0 else ("s", p - 1, 1)))
                nc.vector.tensor_tensor(lg2[:, :, :], stop[:, :, :], left[:, :, :], ALU.mult).then_inc(
                    S["pair_probs"], mark("pair_probs", ("s", p)))

            def weights(tag, p):
                if tag == "m":
                    logits(p)
                else:
                    sticks(p)

            def y_take(tag, p):
                y = ya if tag == "m" else yb
                if tag == "m":
                    dve.wait_ge(S["pair_probs"], at("pair_probs", (tag, p)))
                    nc.vector.reciprocal(rinv2, sums2).then_inc(S["pair_rinv"], mark("pair_rinv", p))
                    dve.wait_ge(S["pair_rinv"], at("pair_rinv", p))
                dve.wait_ge(S["pair_done"], at("pair_done", (tag, p)))
                for t in range(TT):
                    dst = y[:, t, P * p:P * (p + 1)].rearrange("p (e d) -> p e d", e=2)
                    src = att[0][:, t * P:(t + 1) * P].rearrange("p (e d) -> p e d", e=2)
                    if tag == "m":
                        ins = nc.vector.tensor_tensor(dst, src, rinv2[:, 2 * t:2 * t + 2].unsqueeze(2).broadcast_to([P, 2, DH2]),
                                                      ALU.mult)
                    else:
                        ins = nc.vector.tensor_copy(dst, src)
                    ins.then_inc(S["y_part" if t == 0 else "y_ready2"], mark("y_part" if t == 0 else "y_ready2", (tag, p)))

            def take(name, i):
                b = BANKS[name, i]
                if name == "yab":
                    unit(name, i)
                    for n_, g in enumerate((ga, gb)):
                        piece = g[:, 2 * i:2 * i + 2, :]
                        if n_ == 0:
                            dve.wait_ge(S["emptied_act"], at("emptied_act", ("gb2", 3)))
                        nc.vector.tensor_tensor(piece, b[n_][:].rearrange("p (n t) -> p n t", n=2), piece, ALU.mult).then_inc(
                            S["emptied_dve" if n_ == 1 else "y_part"], mark("emptied_dve" if n_ == 1 else "y_part", (name, i)))
                    y = ga[:, 2 * i:2 * i + 2, :]
                    dve.wait_ge(S["emptied_dve"], at("emptied_dve", (name, i)))
                    nc.vector.tensor_tensor(y, y, gb[:, 2 * i:2 * i + 2, :], ALU.add).then_inc(S["y_ready"], mark("y_ready", i))
                    dve.wait_ge(S["y_hi"], at("y_hi", i))
                    nc.vector.tensor_tensor(xa_lo[:, 2 * i:2 * i + 2, :], y, xa_hi[:, 2 * i:2 * i + 2, :].bitcast(F32),
                                                ALU.subtract).then_inc(S["y_lo"], mark("y_lo", i))
                elif name == "mix" and i % 2 == 1:
                    unit(name, i)
                    for t in range(TT):
                        piece = x_res[:, t, 512 * (i // 2):512 * (i // 2 + 1)]
                        nc.vector.tensor_tensor(piece, b[t][:], piece, ALU.add).then_inc(
                            S["emptied_dve"], mark("emptied_dve", (name, i - 1 + t)))

            def route(t, h):
                def top16(values, val, idx, key):
                    nc.vector.max(val[:, 0:8], values).then_inc(S["top8"], mark("top8", (t, h, key)))
                    dve.wait_ge(S["top8"], at("top8", (t, h, key)))
                    nc.vector.max_index(idx[:, 0:8], val[:, 0:8], values).then_inc(S["top8_at"], mark("top8_at", (t, h, key)))
                    dve.wait_ge(S["top8_at"], at("top8_at", (t, h, key)))
                    nc.vector.match_replace(values, val[:, 0:8], values, LOWEST).then_inc(
                        S["top8_out"], mark("top8_out", (t, h, key)))
                    dve.wait_ge(S["top8_out"], at("top8_out", (t, h, key)))
                    nc.vector.max(val[:, 8:16], values).then_inc(S["next8"], mark("next8", (t, h, key)))
                    dve.wait_ge(S["next8"], at("next8", (t, h, key)))
                    nc.vector.max_index(idx[:, 8:16], val[:, 8:16], values).then_inc(
                        S["next8_at"], mark("next8_at", (t, h, key)))

                dve.wait_ge(S["iota"], at("iota", 1))
                dve.wait_ge(S["rank_ready"], at("rank_ready", (h, t)))
                for i in range(2):
                    top16(rank[t][:, 2 * h + i, :], top_s[:, i, :], top_i[:, i, :], i)
                dve.wait_ge(S["next8_at"], at("next8_at", (t, h, 1)))
                nc.vector.tensor_copy(top_f, top_i).then_inc(S["top_f"], mark("top_f", (t, h)))
                nc.vector.tensor_tensor(cand, top_s[:, 0, :].unsqueeze(2).broadcast_to([P, P_TOP, P_TOP]),
                                            top_s[:, 1, :].unsqueeze(1).broadcast_to([P, P_TOP, P_TOP]), ALU.add).then_inc(
                    S["cand"], mark("cand", (t, h)))
                dve.wait_ge(S["cand"], at("cand", (t, h)))
                top16(cand.rearrange("p a b -> p (a b)"), best[:, t, h, :], pos, 2)
                dve.wait_ge(S["next8_at"], at("next8_at", (t, h, 2)))
                nc.vector.tensor_scalar(pos_i[:, 0, :], pos, 4, None, ALU.logical_shift_right).then_inc(
                    S["pos_i"], mark("pos_i", (t, h, 0)))
                nc.vector.tensor_scalar(pos_i[:, 1, :], pos, P_TOP - 1, None, ALU.bitwise_and).then_inc(
                    S["pos_i"], mark("pos_i", (t, h, 1)))
                dve.wait_ge(S["pos_i"], at("pos_i", (t, h, 1)))
                nc.vector.tensor_copy(pos_f, pos_i).then_inc(S["pos_f"], mark("pos_f", (t, h)))
                dve.wait_ge(S["pos_f"], at("pos_f", (t, h)))
                for i in range(2):
                    nc.vector.tensor_tensor(pick[:, i], pos_f[:, i, :].unsqueeze(2).broadcast_to([P, P_TOP, P_TOP]),
                                                iota16.unsqueeze(1).broadcast_to([P, P_TOP, P_TOP]), ALU.is_equal).then_inc(
                        S["pick"], mark("pick", (t, h, i)))
                dve.wait_ge(S["pick"], at("pick", (t, h, 1)))
                for i in range(2):
                    nc.vector.tensor_tensor(pick[:, i], pick[:, i], top_f[:, i, :].unsqueeze(1).broadcast_to([P, P_TOP, P_TOP]),
                                                ALU.mult).then_inc(S["picked"], mark("picked", (t, h, i)))
                dve.wait_ge(S["picked"], at("picked", (t, h, 1)))
                nc.vector.tensor_reduce(both_f, pick, X, ALU.add).then_inc(S["both_f"], mark("both_f", (t, h)))
                dve.wait_ge(S["both_f"], at("both_f", (t, h)))
                nc.vector.scalar_tensor_tensor(expert_f, both_f[:, 0, :], float(P_KEYS), both_f[:, 1, :], ALU.mult, ALU.add).then_inc(
                    S["expert_f"], mark("expert_f", (t, h)))
                dve.wait_ge(S["expert_f"], at("expert_f", (t, h)))
                c = t * SLOTS + h * P_TOP
                nc.vector.tensor_copy(expert[:, c:c + P_TOP], expert_f).then_inc(
                    S["expert_ready"], mark("expert_ready", (t, h)))

            def diff(t):
                w = weight[:, t * SLOTS:(t + 1) * SLOTS].rearrange("p (h k) -> p h k", h=P_HEADS)
                dve.wait_ge(S["next8"], at("next8", (t, P_HEADS - 1, 2)))
                nc.vector.tensor_tensor(w, best[:, t], best[:, t, :, 0:1].broadcast_to([P, P_HEADS, P_TOP]), ALU.subtract).then_inc(
                    S["best_diff"], mark("best_diff", t))

            def coefficients(t):
                w = weight[:, t * SLOTS:(t + 1) * SLOTS].rearrange("p (h k) -> p h k", h=P_HEADS)
                dve.wait_ge(S["best_exp"], at("best_exp", t))
                nc.vector.tensor_reduce(wsum[:, t, :], w, X, ALU.add).then_inc(S["wsum"], mark("wsum", t))
                dve.wait_ge(S["wsum"], at("wsum", t))
                nc.vector.reciprocal(wsum[:, t, :], wsum[:, t, :]).then_inc(S["wrec"], mark("wrec", t))
                dve.wait_ge(S["wrec"], at("wrec", t))
                nc.vector.tensor_tensor(w, w, wsum[:, t, :].unsqueeze(2).broadcast_to([P, P_HEADS, P_TOP]), ALU.mult).then_inc(
                    S["weight"], mark("weight", t))
                dve.wait_ge(S["weight"], at("weight", t))
                dve.wait_ge(S["gelu_ready"], at("gelu_ready", t))
                d = dots[:, t * SLOTS:(t + 1) * SLOTS]
                nc.vector.tensor_tensor(d, d, weight[:, t * SLOTS:(t + 1) * SLOTS], ALU.mult).then_inc(
                    S["coef"], mark("coef", t))

            def u_rows(t, first, rounds):
                with dve.Fori(first, first + rounds) as r:
                    for j in range(GATHER):
                        dve.wait_ge(S[f"gathered{j}"], r * 16 + 16 * (t * ROUNDS + 1))
                        dot = dots[:, bass.ds(r * GATHER + (t * SLOTS + j), 1)]
                        nc.vector.scalar_tensor_tensor(rows_ring[j], rows_ring[j], 1.0, hn[:, t, :], ALU.mult, ALU.mult,
                                                       accum_out=dot).then_inc(S["rows_used"], 1)

            def v_rows(t):
                with dve.Fori(0, ROUNDS) as r:
                    for j in range(GATHER):
                        dve.wait_ge(S[f"gathered{j}"], r * 16 + 16 * ((TT + t) * ROUNDS + 1))
                        dve.wait_ge(S["rows_used"], r * GATHER + (GATHER + (TT + t) * SLOTS + j))
                        c = dots[:, bass.ds(r * GATHER + (t * SLOTS + j), 1)]
                        nc.vector.scalar_tensor_tensor(x_res[:, t, :], rows_ring[j], c, x_res[:, t, :], ALU.mult,
                                                       ALU.add).then_inc(S["rows_used"], 1)

            def peer_norm():
                norm_dve(dve, "n2")
                turn_dve(dve, xb_hi, xb_lo, "n2", lambda k: col("norm2_g_2", 0, k))
                dve.wait_ge(S["g_loaded"], at("g_loaded", "n2"))
                for t in range(TT):
                    nc.vector.tensor_tensor(hn[:, t, :], hn[:, t, :], g_row, ALU.mult).then_inc(
                        S["xn_ready"], mark("xn_ready", t))

            split_lo(dve, 0, True)
            split_lo(dve, 1, True)
            dve.wait_ge(S["rstd_ready"], at("rstd_ready", "fin"))
            dve.wait_ge(S["g_scaled"], at("g_scaled", "fin"))
            for t in range(TT):
                nc.vector.scalar_tensor_tensor(x_res[:, t, :], x_res[:, t, :], rstd[:, t:t + 1], g_row, ALU.mult, ALU.mult).then_inc(
                    S["x_fin"], mark("x_fin", t))
            norm_dve(dve, "n1")
            turn_dve(dve, xa_hi, xa_lo, "n1", lambda k: col("norm1_g_2", 0, k))
            for u, (name, i, kind) in enumerate(units2):
                if u + 2 < len(units2):
                    split_lo(dve, u + 2, True)
                take(name, i)
                scored, pair, before = pair_at(u)
                if pair and scored:
                    if before:
                        y_take(*before)
                    weights(*pair)
                if (name, i) == ("gb2", 3):
                    y_take(*STEPS[-1])
                    turn_dve(dve, xb_hi, xb_lo, "y2", lambda k: 1.0)
                elif (name, i) == ("mix", 3):
                    peer_norm()
                if name == "pq" and i >= 1:
                    route(0, i - 1)
            route(0, P_HEADS - 1)
            diff(0)
            dve.wait_ge(S["xn_ready"], at("xn_ready", TT - 1))
            for h in range(P_HEADS):
                route(1, h)
                u_rows(0, h * ROUNDS // P_HEADS, ROUNDS // P_HEADS)
            diff(1)
            u_rows(1, 0, ROUNDS)
            for t in range(TT):
                coefficients(t)
            dve.wait_ge(S["coef"], at("coef", TT - 1))
            for t in range(TT):
                v_rows(t)
            dve.wait_ge(S["rstd_ready"], at("rstd_ready", "last"))
            dve.wait_ge(S["g_scaled"], at("g_scaled", "last"))
            for t in range(TT):
                nc.vector.scalar_tensor_tensor(x_res[:, t, :], x_res[:, t, :], rstd[:, t:t + 1], g_last, ALU.mult, ALU.mult).then_inc(
                    S["final_ready"], mark("final_ready", t))

        def second_pool(pool):
            pool.wait_ge(S["g_loaded"], at("g_loaded", "fin"))
            nc.gpsimd.tensor_scalar(g_row, g_row, D ** 0.5, None, ALU.mult).then_inc(S["g_scaled"], mark("g_scaled", "fin"))
            norm_pool(pool, "fin")
            norm_pool(pool, "n1")
            for t in range(TT):
                dst = dist_i[:, 0:P] if t == 0 else dist_i[:, P:3 * P]
                nc.gpsimd.iota(dst, pattern=[[1, P * (t + 1)]], base=-P * t, channel_multiplier=-1).then_inc(
                    S["dist"], mark("dist", t))
            pool.wait_ge(S["dist"], at("dist", 1))
            nc.gpsimd.tensor_copy(dist, dist_i).then_inc(S["dist"], mark("dist", 2))
            pool.wait_ge(S["dist"], at("dist", 2))
            for h in range(H2):
                nc.gpsimd.tensor_scalar(moba_bias[:, h, :], dist, 2.0 ** (-8.0 * (h + 1) / H2), None, ALU.mult).then_inc(
                    S["alibi"], mark("alibi", h))
            pool.wait_ge(S["alibi"], at("alibi", H2 - 1))
            for t in range(TT):
                d = moba_bias[:, :, 0:P] if t == 0 else moba_bias[:, :, 2 * P:3 * P]
                nc.gpsimd.affine_select(out=d, in_=d, compare_op=ALU.is_ge, fill=NEG, base=0,
                                            pattern=[[0, H2], [-1, P]], channel_multiplier=1).then_inc(
                    S["moba_bias"], mark("moba_bias", t))
            for c in (P - 1, 3 * P - 1):
                nc.gpsimd.memset(left[:, :, c:c + 1], 1.0).then_inc(S["left_one"], mark("left_one", c))
            for p in range(PAIRS):
                pool.wait_ge(S["left_one"], at("left_one", 3 * P - 1))
                pool.wait_ge(S["odds"], at("odds", (p, 1, 1)))
                n_ = 0
                for tile, fill in ((stay, 1.0), (stop, 0.0)):
                    for t in range(TT):
                        d = tile[:, :, 0:P] if t == 0 else tile[:, :, 2 * P:3 * P]
                        nc.gpsimd.affine_select(out=d, in_=d, compare_op=ALU.is_ge, fill=fill, base=-1,
                                                    pattern=[[0, 2], [-1, P]], channel_multiplier=1).then_inc(
                            S["odds_masked"], mark("odds_masked", (p, n_)))
                        n_ += 1
            norm_pool(pool, "n2")
            nc.gpsimd.iota(iota_i, pattern=[[1, P_TOP]], base=0, channel_multiplier=0).then_inc(S["iota"], mark("iota", 0))
            pool.wait_ge(S["iota"], at("iota", 0))
            nc.gpsimd.tensor_copy(iota16, iota_i).then_inc(S["iota"], mark("iota", 1))
            pool.wait_ge(S["g_last_loaded"], at("g_last_loaded"))
            nc.gpsimd.tensor_scalar(g_last, g_last, D ** 0.5, None, ALU.mult).then_inc(S["g_scaled"], mark("g_scaled", "last"))
            for phase in range(2 * TT):
                t = phase % TT
                w = A["peer_u_2" if phase < TT else "peer_v_2"][0]
                pool.wait_ge(S["expert_ready"], at("expert_ready", (t, P_HEADS - 1)))
                with pool.Fori(0, ROUNDS) as r:
                    for j0 in range(0, GATHER, HALF):
                        pool.wait_ge(S["rows_used"], r * GATHER + (phase * SLOTS + j0 + HALF))
                        nc.gpsimd.tensor_copy(expert_now[:, j0:j0 + HALF],
                                              expert[:, bass.ds(r * GATHER + (t * SLOTS + j0), HALF)]).then_inc(S["expert_now"], 1)
                        pool.wait_ge(S["expert_now"], r * (GATHER // HALF) + (phase * ROUNDS * (GATHER // HALF) + j0 // HALF + 1))
                        nc.gpsimd.tensor_tensor(idle, eps_d[:, 0:1], eps_d[:, 0:1], ALU.add)
                        for j in range(j0, j0 + HALF):
                            nc.gpsimd.indirect_dma_start(
                                rows_ring[j], None, w, bass.IndirectOffsetOnAxis(ap=expert_now[:, j:j + 1], axis=0)
                            ).then_inc(S[f"gathered{j}"], 16)
            norm_pool(pool, "last")

        block = ctx.enter_context(nc.Block())

        @block.sync
        def _(sp):
            sync_program(sp)

        @block.gpsimd
        def _(pool):
            start_pool(pool)
            counts.region = "layer"
            with pool.Fori(0, DEPTH) as l:
                counts.layer = l
                layer_pool(pool, l)
            counts.region, counts.layer = "post", None
            second_pool(pool)

        @block.scalar
        def _(act):
            start_act(act)
            counts.region = "layer"
            with act.Fori(0, DEPTH) as l:
                counts.layer = l
                layer_act(act, l)
            counts.region, counts.layer = "post", None
            second_act(act)

        @block.vector
        def _(dve):
            start_dve(dve)
            counts.region = "layer"
            with dve.Fori(0, DEPTH) as l:
                counts.layer = l
                layer_dve(dve, l)
            counts.region, counts.layer = "post", None
            second_dve(dve)

        @block.tensor
        def _(pe):
            start_pe(pe)
            counts.region = "layer"
            with pe.Fori(0, DEPTH) as l:
                counts.layer = l
                layer_pe(pe, l)
            counts.region, counts.layer = "post", None
            second_pe(pe)
    return counts


INPUTS = ["x", "norm_mix_g", "w_in", "conv_w", "conv_b", "b_igate", "b_fgate", "mlstm_norm_g", "attn_sinks", "rel_bias",
          "w_branch_m", "w_branch_a", "w_out", "norm_mlp_g", "w_up", "w_down", "final_norm_g", "norm1_g_2", "w_in_2",
          "w_out_moba_2", "w_out_sb_2", "w_mix_out_2", "norm2_g_2", "peer_w_q_2", "peer_sub_keys_2", "peer_u_2", "peer_v_2",
          "final_norm_g_2"]


def kernel(**inputs):
    import concourse.bacc as bacc
    from concourse.bass_utils import run_bass_kernel_spmd

    arrays = {f"in_{n}": np.ascontiguousarray(inputs[n]) for n in INPUTS}
    arrays["in_onehot"] = bucket_onehot()
    known = None
    for _ in range(2):
        nc = bacc.Bacc("TRN2", target_bir_lowering=False, num_devices=1)
        A = {n[3:]: nc.dram_tensor(n, a.shape, F32, kind="ExternalInput").ap() for n, a in arrays.items()}
        A["toep"] = nc.dram_tensor("toep", [A_HEADS, P, 384], F32, kind="Internal").ap()
        out = nc.dram_tensor("out", inputs["x"].shape, F32, kind="ExternalOutput").ap()
        known = build(nc, A, out, known)
    r = run_bass_kernel_spmd(nc, [arrays], core_ids=[0])
    return r.results[0]["out"]
```

```python
from contextlib import ExitStack

import numpy as np

import concourse.bass as bass
from concourse import mybir

F32 = mybir.dt.float32
F32R = mybir.dt.float32r
U32 = mybir.dt.uint32
I32 = mybir.dt.int32
ALU = mybir.AluOpType
ACT = mybir.ActivationFunctionType
X = mybir.AxisListType.X

P = 128
D, SEQ, DEPTH = 1024, 256, 2
TT = SEQ // P
KT = D // P
EPS = 1e-6
NEG = -1.0e30
LOWEST = -3.0e38

M_HEADS, M_DK, M_DV = 4, 128, 256
A_HEADS, A_KV, A_DH = 16, 4, 64
GROUP = A_HEADS // A_KV
WINDOW, N_BUCKETS, MAX_DISTANCE = 128, 32, 128
CONV_K = 4
D_FF = 4 * D
COL_MQK, COL_MV, COL_MO, COL_MI, COL_MF = 0, 1024, 2048, 3072, 3076
COL_AQ, COL_AK, COL_AV, COL_GA, COL_GB = 3080, 4104, 4360, 4616, 5640

H2, DH2 = 8, 64
W2 = H2 * DH2
P_HEADS, P_KEYS, P_TOP = 8, 128, 16
HP = 2 * P_HEADS
SLOTS = P_HEADS * P_TOP
N_EXPERTS = P_KEYS * P_KEYS

RING = 3
RAW_RING = 2
UNIT = 2048
GATE_F = 64
GATHER = 8
ROUNDS = SLOTS // GATHER
HEAD_ROUNDS = P_TOP // GATHER
ALL_HEADS = TT * P_HEADS


def u_block(g):
    return max(0, 2 * g - 1)


def v_block(g):
    return min(2 * g + 2, 2 * ALL_HEADS - 1)


SIGNALS = {
    "consts": "a constant has been made", "x_loaded": "the tokens are here", "params_loaded": "a small parameter is here",
    "start_done": "the parameters stand in columns, in PSUM", "start_taken": "and in memory",
    "toep_ready": "the window's biases by distance are made", "toep_stored": "and in DRAM, once for each query",
    "bias_loaded": "the window's biases are here, shifted by one for each query",
    "hi_ready": "a unit's rounded part is made", "lo_ready": "and the rest of it: its raw slot is free",
    "unit_done": "TensorE is through with a unit", "tile_done": "and with its first tile of tokens", "emptied_act": "ScalarE has emptied a product's bank",
    "emptied_dve": "VectorE has emptied a product's bank",
    "ssq_ready": "a tile's sums of squares", "ms_ready": "those with eps", "rstd_ready": "one over their root",
    "hn_ready": "a tile is normed", "turned": "a tile of features is transposed, in PSUM",
    "x_hi": "its rounded part is made", "x_lo": "and the rest of it",
    "gate_loaded": "the gates' weights are here", "gate_hi": "their rounded part", "gate_lo": "and the rest",
    "gate_done": "their product", "gate_in": "with its bias", "gate_nabs": "minus |forget gate|", "gate_exp": "its exp",
    "gate_ln": "log(1 + exp)", "gate_row": "a step of the running sums", "gate_m": "the last one: -(B + M)",
    "gate_enm": "exp(-(B + M))", "columns_done": "a, -M and exp(-m) stand on columns, in PSUM", "acol_ready": "and in memory",
    "pads_ready": "ones beside the values, zeros before the first token", "conv_tap": "a tap of the convolution",
    "conv": "its last tap", "silu_sig": "the sigmoid of it", "silu": "its silu", "z_ready": "a - M of a head",
    "z_masked": "without the future", "w_ready": "the exp of it", "kq_done": "a head's keys times queries",
    "s_ready": "weighted", "num_done": "times the values", "num_ready": "and in memory", "num_ssq": "its sum of squares",
    "den_part": "a step of the denominators", "den_abs": "max(|den|, exp(-m))", "den_rec": "one over it",
    "num_norm": "a step of the heads' norm", "num_factor": "the factor of a head's numerators",
    "mo_sig": "the output gate", "hm_ready": "a head's output",
    "ak_part": "keys of a head are in place", "scores_done": "queries times keys", "mx_ready": "with their bias, and the largest",
    "negm_ready": "minus the maximum", "sink_diff": "the sink's exponent", "sink_exp": "its exp",
    "probs_ready": "exp of the logits, with sums", "denom": "the sum with the sink", "rinv_ready": "one over it",
    "probs_turned": "the weights are transposed, in PSUM", "pT_ready": "and in memory", "pv_done": "times the values",
    "ha_ready": "a tile of the output",
    "g_sig": "a branch's gate", "y_ready": "the sum of the branches", "y_hi": "its rounded part", "y_lo": "and the rest",
    "ff_sq": "squares of the MLP's middle", "ff_hi": "their rounded part",
    "ff_lo": "and the rest", "mlp_added": "a part of the MLP is on the residual stream",
    "g_loaded": "a norm's weights are here", "g_scaled": "times the norm's sqrt(D)", "x_fin": "the first block's output",
    "dist": "a step of the distances", "alibi": "a head's slope times distance", "moba_bias": "without the future",
    "left_one": "nothing is broken off in front of the last key", "pair_scores": "queries times keys",
    "pair_mx": "with their bias, and the largest", "pair_negm": "minus the maximum", "pair_part": "an exp",
    "pair_probs": "all weights of a pair", "pair_rinv": "one over their sums", "odds": "the odds to stop at a key or pass it",
    "odds_masked": "without the future", "left_ready": "what is left of the stick", "pair_turned": "weights transposed, in PSUM",
    "pair_pT": "and in memory", "pair_done": "times the values", "y_part": "the first of two steps into memory",
    "y_ready2": "a pair's output is in memory",
    "keys_loaded": "sub-keys are here", "keys_turned": "transposed, in PSUM", "keys_ready": "and in memory",
    "xn_ready": "a tile's normed tokens", "iota": "0 .. 15", "rank_done": "scores of a head's sub-keys", "rank_ready": "in memory",
    "top8": "the best eight", "top8_at": "where they are", "top8_out": "the scores without them", "next8": "the next eight",
    "next8_at": "where they are", "top_f": "places as floats", "cand": "sums of the best of both halves",
    "pos_i": "places in both halves", "pos_f": "as floats", "pick": "one-hot", "picked": "times the sub-keys' numbers",
    "both_f": "the sub-keys' numbers", "expert_f": "the experts' numbers", "expert_ready": "as indices",
    "best_diff": "scores less the largest", "best_exp": "their exp, with its sum", "wrec": "one over it",
    "weight": "the softmax", "rows_used": "a row of the ring has been used",
    "gelu_ready": "the experts' activations", "coef": "times the softmax",
    "diag_ready": "a slot's coefficients stand on a diagonal",
    "rows_multiplied": "TensorE has used a row", "x_peer": "its sum is on the residual stream",
    "g_last_loaded": "the last norm's weights are here", "final_ready": "a tile of the result", "out_stored": "and in DRAM",
}
SIGNALS |= {f"w_loaded{i}": "" for i in range(RAW_RING)} | {f"gathered{i}": "" for i in range(GATHER)}


def bucket_onehot():
    n = (WINDOW - 1) - np.arange(WINDOW)
    exact = N_BUCKETS // 2
    large = exact + (np.log(np.maximum(n, 1) / exact) / np.log(MAX_DISTANCE / exact)
                     * (N_BUCKETS - exact)).astype(np.int32)
    bucket = np.where(n < exact, n, np.minimum(large, N_BUCKETS - 1))
    return (np.arange(N_BUCKETS)[:, None] == bucket[None, :]).astype(np.float32)


def layer_units():
    u = [("mqk", i, "F") for i in range(4)] + [("mv", i, "T") for i in range(4)]
    u += [("aq", i, "F") for i in range(4)] + [("ak", 0, "F"), ("av", 0, "V")]
    u += [("mo", i, "T") for i in range(4)]
    u += [("ga", i, "F") for i in range(4)] + [("gb", i, "F") for i in range(4)]
    u += [("bm", i, "F") for i in range(4)] + [("ba", i, "F") for i in range(4)]
    u += [("wo", i, "T") for i in range(4)]
    pairs = D_FF // 512
    u += [("up", 0, "F"), ("up", 1, "F")]
    for p in range(pairs):
        if p + 1 < pairs:
            u += [("up", 2 * p + 2, "F"), ("up", 2 * p + 3, "F")]
        u += [("down", 2 * p, "T"), ("down", 2 * p + 1, "T")]
    return u


def second_units():
    u = [("qa", i, "F") for i in range(2)] + [("ka", i, "F") for i in range(2)] + [("va", i, "T") for i in range(2)]
    u += [("qb", i, "F") for i in range(2)] + [("kb", i, "F") for i in range(2)] + [("vb", i, "T") for i in range(2)]
    u += [("ga2", i, "F") for i in range(4)] + [("gb2", i, "F") for i in range(4)]
    u += [("yab", i, "Y") for i in range(4)]
    u += [("mix", i, "T") for i in range(4)] + [("pq", i, "F") for i in range(8)]
    return u


NU = len(layer_units())
START = {RING: RING + 1, RAW_RING: RAW_RING}


def ring_slot(u, second):
    return 1 if u == NU - 1 and not second else u % RING


class Counts:

    def __init__(self, known):
        self.known = known
        self.where = {}
        self.total = {}
        self.region = "pre"
        self.layer = None

    def mark(self, name, key=0, by=1):
        t = self.total.setdefault(name, {"pre": 0, "layer": 0, "post": 0})
        t[self.region] += by
        assert (name, self.region, key) not in self.where, (name, key)
        self.where[name, self.region, key] = t[self.region]
        return by

    def at(self, name, key=0, region=None):
        region = region or self.region
        if self.known is None:
            return 1
        t, n = self.known.total[name], self.known.where[name, region, key]
        if region == "pre":
            return n
        if region == "post":
            return t["pre"] + DEPTH * t["layer"] + n
        if self.region == "post":
            return t["pre"] + (DEPTH - 1) * t["layer"] + n
        return self.layer * t["layer"] + (t["pre"] + n)

    def at_layer_start(self, name):
        t = self.known.total[name] if self.known else {"pre": 9, "layer": 1}
        return (self.layer if self.region == "layer" else DEPTH) * t["layer"] + t["pre"]

    def free(self, u, ring, second):
        def slot(v, second):
            return ring_slot(v, second) if ring == RING else v % ring

        mine = [v for v in range(u) if slot(v, second) == slot(u, second)]
        before = mine[-1] if mine else max(v for v in range(NU) if slot(v, False) == slot(u, second)) - NU
        return (DEPTH if second else self.layer) * NU + (START[ring] + before + 1)


def build(nc, A, out, known):
    counts = Counts(known)
    ctx = ExitStack()
    at, mark = counts.at, counts.mark
    S = {name: ctx.enter_context(nc.semaphore(name)) for name in SIGNALS}

    with ctx:
        def sb(name, shape, dt=F32):
            return ctx.enter_context(nc.sbuf_tensor(name, shape, dt))

        xa_hi, xa_lo = sb("xa_hi", [P, KT, SEQ], F32R), sb("xa_lo", [P, KT, SEQ], F32R)
        xb_hi, xb_lo = sb("xb_hi", [P, KT, SEQ], F32R), sb("xb_lo", [P, KT, SEQ], F32R)
        w_hi, w_lo = sb("w_hi", [P, RING, UNIT], F32R), sb("w_lo", [P, RING, UNIT], F32R)
        GW = GATE_F + M_HEADS
        gate_hi, gate_lo = sb("gate_hi", [P, KT, GW], F32R), sb("gate_lo", [P, KT, GW], F32R)

        x_res = sb("x_res", [P, TT, D])
        ident = sb("ident", [P, P])
        params = sb("params", [P, P])
        params_m = sb("params_m", [P, 16])
        gate_b = sb("gate_b", [P, DEPTH])
        neg_sink = sb("neg_sink", [P, DEPTH, A_HEADS])
        minus_half = sb("minus_half", [P, 16])
        small = sb("small", [P, 256])
        gate_raw = sb("gate_raw", [P, KT, GW])
        scan_in = sb("scan_in", [M_HEADS, 2])
        ones_row, zero_row = (scan_in[:, i:i + 1].broadcast_to([M_HEADS, SEQ]) for i in range(2))
        ARENA = 27176
        arena = sb("arena", [P, ARENA])
        used = {}

        def view(name, at, size):
            assert at + size <= ARENA, (name, at + size)
            used[name] = (at, size)
            return arena[:, at:at + size]

        raw = [view(f"raw{s}", s * UNIT, UNIT) for s in range(RAW_RING)]
        o = RAW_RING * UNIT
        bias = view("bias", o, 16 * 256).rearrange("p (h c) -> p h c", h=A_HEADS)
        o += 16 * 256
        VW = M_DV + 1
        mv = view("mv", o, TT * M_HEADS * VW).rearrange("p (t h v) -> p t h v", t=TT, h=M_HEADS)
        ha = view("ha", o, TT * D).rearrange("p (t d) -> p t d", t=TT)
        o += TT * M_HEADS * VW
        num = view("num", o, TT * M_HEADS * VW).rearrange("p (t h v) -> p t h v", t=TT, h=M_HEADS)
        hn = view("hn", o, TT * D).rearrange("p (t d) -> p t d", t=TT)
        gates = view("gates", o, 8 * SEQ)[0:M_HEADS, :].rearrange("p (r t) -> p r t", r=8)
        o += TT * M_HEADS * VW
        CW = SEQ + CONV_K - 1
        mqk = view("mqk", o, KT * CW).rearrange("p (k t) -> p k t", k=KT)
        sig = mqk[:, :, 0:SEQ]
        pT = view("pT", o, 3 * 512).rearrange("p (c h k) -> p c h k", c=3, h=GROUP)
        o += KT * CW
        qk = view("qk", o, KT * SEQ).rearrange("p (k t) -> p k t", k=KT)
        lg = view("lg", o, GROUP * 384).rearrange("p (h c) -> p h c", h=GROUP)
        o += KT * SEQ
        mo = view("mo", o, TT * D).rearrange("p (t d) -> p t d", t=TT)
        o += TT * D
        ga = view("ga", o, KT * SEQ).rearrange("p (k t) -> p k t", k=KT)
        zw = view("zw", o, M_HEADS * 384).rearrange("p (h c) -> p h c", h=M_HEADS)
        sq = view("sq", o, 4 * 512).rearrange("p (b c) -> p b c", b=4)
        o += KT * SEQ
        gb = view("gb", o, KT * SEQ).rearrange("p (k t) -> p k t", k=KT)
        sm = view("sm", o, 2 * 384).rearrange("p (b c) -> p b c", b=2)
        o += KT * SEQ
        aq = view("aq", o, KT * SEQ).rearrange("p (k t) -> p k t", k=KT)
        o += KT * SEQ
        ak = view("ak", o, 2 * A_KV * SEQ).rearrange("p (e j t) -> p e j t", e=2, j=A_KV)
        o += 2 * A_KV * SEQ
        av = view("av", o, TT * 256).rearrange("p (t v) -> p t v", t=TT)
        o += TT * 256

        acc = [ctx.enter_context(nc.psum_tensor(f"acc{b}", [P, 512], F32)) for b in range(4)]
        att = [ctx.enter_context(nc.psum_tensor(f"att{b}", [P, 512], F32)) for b in range(4)]

        units, units2 = layer_units(), second_units()
        at_unit = {(n, i): k for k, (n, i, _) in enumerate(units)}
        at_unit2 = {(n, i): k for k, (n, i, _) in enumerate(units2)}

        def whi(s, kind):
            return w_hi[:, s, :].rearrange("p (k n) -> p k n", k=4 if kind == "T" else 8)

        def wlo(s, kind):
            return w_lo[:, s, :].rearrange("p (k n) -> p k n", k=4 if kind == "T" else 8)

        PARAM_ROWS = [("norm_mix_g", 16), ("norm_mlp_g", 16), ("norm1_g_2", 8), ("norm2_g_2", 8),
                      ("conv_w", 64), ("conv_b", 16)]
        COL = {}
        n = 0
        for name, rows in PARAM_ROWS:
            COL[name] = n
            n += rows
        assert n == P

        def col(name, l, k, tile=params):
            if isinstance(l, int):
                c = COL[name] + 8 * l + k if name != "conv_w" else COL[name] + 32 * l + k
                return tile[:, c:c + 1]
            step = 32 if name == "conv_w" else 8
            return tile[:, bass.ds(l * step + (COL[name] + k), 1)]

        scratch = qk.rearrange("p k t -> p (k t)")
        rows_p = scratch[:, 0:P]
        rows_m = scratch[:, P:2 * P]
        onehot = scratch[0:N_BUCKETS, 2 * P:3 * P]
        rel_sb = scratch[0:N_BUCKETS, 3 * P:3 * P + A_HEADS]
        toep = scratch[0:A_HEADS, 4 * P:7 * P]

        def area(name, at, size):
            return arena[:, used[name][0] + at:used[name][0] + at + size]

        moba_bias = area("bias", 0, H2 * 384).rearrange("p (h c) -> p h c", h=H2)
        g_row = area("bias", H2 * 384, D)
        qa, ka = aq[:, 0:4, :], aq[:, 4:8, :]
        qb, kb = qk[:, 0:4, :], qk[:, 4:8, :]
        va, vb = (area("mv", i * TT * W2, TT * W2).rearrange("p (t v) -> p t v", t=TT) for i in range(2))
        ya, yb = (mo[:, i, :].rearrange("p (t v) -> p t v", t=TT) for i in range(2))
        lg2 = area("mqk", 0, 768).rearrange("p (h c) -> p h c", h=2)
        pT2 = area("mqk", 768, 768).rearrange("p (h c k) -> p h c k", h=2, c=3)
        dist_i, dist = area("mqk", 768, 384).bitcast(I32), area("mqk", 1536, 384)
        stay, stop, left = (area("ak", i * 768, 768).rearrange("p (h c) -> p h c", h=2) for i in range(3))
        raw_keys = mo.rearrange("p t d -> p (t d)").rearrange("p (h n) -> p h n", h=HP)
        keys = aq.rearrange("p k t -> p (k t)").rearrange("p (h n) -> p h n", h=HP)
        queries = area("ga", 0, HP * SEQ).rearrange("p (h t) -> p h t", h=HP)
        rank = [area(n_, 0, HP * P_KEYS).rearrange("p (h n) -> p h n", h=HP) for n_ in ("qk", "mqk")]
        g_last = area("raw0", 0, D)
        expert = area("mv", D, TT * SLOTS).bitcast(U32)
        weight = area("mv", D + TT * SLOTS, TT * SLOTS)
        dots = area("mv", D + 2 * TT * SLOTS, TT * SLOTS)
        iota_i, iota16 = area("ak", 0, P_TOP).bitcast(I32), area("ak", P_TOP, P_TOP)
        top_s = area("ak", 32, 2 * P_TOP).rearrange("p (i k) -> p i k", i=2)
        top_i = area("ak", 64, 2 * P_TOP).bitcast(U32).rearrange("p (i k) -> p i k", i=2)
        top_f = area("ak", 96, 2 * P_TOP).rearrange("p (i k) -> p i k", i=2)
        pos = area("ak", 128, P_TOP).bitcast(U32)
        pos_i = area("ak", 144, 2 * P_TOP).bitcast(U32).rearrange("p (i k) -> p i k", i=2)
        pos_f = area("ak", 176, 2 * P_TOP).rearrange("p (i k) -> p i k", i=2)
        both_f = area("ak", 208, 2 * P_TOP).rearrange("p (i k) -> p i k", i=2)
        expert_f = area("ak", 240, P_TOP)
        cand = area("ak", 256, P_TOP * P_TOP).rearrange("p (a b) -> p a b", a=P_TOP)
        pick = area("ak", 512, 2 * P_TOP * P_TOP).rearrange("p (i k a) -> p i k a", i=2, k=P_TOP)
        best = area("ak", 1024, TT * SLOTS).rearrange("p (h k) -> p h k", h=ALL_HEADS)
        wsum = area("ak", 1280, ALL_HEADS)
        rows_ring = [area("bias", i * D, D) for i in range(4)] + [area("mo", i * D, D) for i in range(2)]
        rows_ring += [area("mv", 0, D), area("ak", 1296, D)]
        assert len(rows_ring) == GATHER
        gate_flat = gate_raw[:].rearrange("p k n -> p (k n)")
        diag = [gate_flat[:, i * P:(i + 1) * P] for i in range(2)]

        def unit_dma(sp, unit, slot, l, second):
            name, i, kind = unit
            F = raw[slot].rearrange("p (k n) -> p k n", k=8)
            T = raw[slot].rearrange("p (k n) -> p k n", k=4)

            def f_src(w, c0):
                return w[:, c0 + 256 * i:c0 + 256 * (i + 1)].rearrange("(k p) n -> p k n", p=P)

            def t_src(w, c0):
                rows = w[512 * (i % 2):512 * (i % 2 + 1), c0 + 512 * (i // 2):c0 + 512 * (i // 2 + 1)]
                return rows.rearrange("(k p) n -> p k n", p=P)

            key = ("u2" if second else "u", at_unit2[name, i] if second else at_unit[name, i])
            f_cols = {"mqk": COL_MQK, "aq": COL_AQ, "ak": COL_AK, "av": COL_AV, "ga": COL_GA, "gb": COL_GB}
            f_cols2 = {"qa": 0, "ka": W2, "qb": 3 * W2, "kb": 4 * W2, "ga2": 6 * W2, "gb2": 6 * W2 + D}
            if second:
                if name in f_cols2:
                    sp.dma_start(F, f_src(A["w_in_2"][0], f_cols2[name])).then_inc(
                        S[f"w_loaded{slot}"], mark(f"w_loaded{slot}", key, 16))
                elif name in ("va", "vb"):
                    sp.dma_start(T, t_src(A["w_in_2"][0], {"va": 2 * W2, "vb": 5 * W2}[name])).then_inc(
                        S[f"w_loaded{slot}"], mark(f"w_loaded{slot}", key, 16))
                elif name == "yab":
                    sp.dma_start(F[:, 0:4, :], f_src(A["w_out_moba_2"][0], 0)).then_inc(
                        S[f"w_loaded{slot}"], mark(f"w_loaded{slot}", key + (0,), 16))
                    sp.dma_start(F[:, 4:8, :], f_src(A["w_out_sb_2"][0], 0)).then_inc(
                        S[f"w_loaded{slot}"], mark(f"w_loaded{slot}", key, 16))
                elif name == "mix":
                    sp.dma_start(T, t_src(A["w_mix_out_2"][0], 0)).then_inc(
                        S[f"w_loaded{slot}"], mark(f"w_loaded{slot}", key, 16))
                elif name == "pq":
                    sp.dma_start(F, f_src(A["peer_w_q_2"][0], 0)).then_inc(
                        S[f"w_loaded{slot}"], mark(f"w_loaded{slot}", key, 16))
                return

            def of(w):
                return A[w][bass.ds(l, 1)].rearrange("o k n -> (o k) n")

            if name in f_cols:
                src, dst = f_src(of("w_in"), f_cols[name]), F
            elif name in ("mv", "mo"):
                src, dst = t_src(of("w_in"), COL_MV if name == "mv" else COL_MO), T
            elif name in ("bm", "ba"):
                src, dst = f_src(of("w_branch_m" if name == "bm" else "w_branch_a"), 0), F
            elif name == "wo":
                src, dst = t_src(of("w_out"), 0), T
            elif name == "up":
                src, dst = f_src(of("w_up"), 0), F
            else:
                rows, half = 512 * (i // 2), 512 * (i % 2)
                src = of("w_down")[rows:rows + 512, half:half + 512].rearrange("(k p) n -> p k n", p=P)
                dst = T
            sp.dma_start(dst, src).then_inc(S[f"w_loaded{slot}"], mark(f"w_loaded{slot}", key, 16))

        def sync_program(sp):
            counts.region = "pre"
            sp.dma_start(x_res[:], A["x"][0].rearrange("(t p) d -> p t d", p=P)).then_inc(
                S["x_loaded"], mark("x_loaded", 0, 16))
            row = 0
            for name, rows in PARAM_ROWS:
                src = A[name]
                if name == "conv_w":
                    src = src.rearrange("l j (k p) -> (l j k) p", p=P)
                else:
                    src = src.rearrange("l (k p) -> (l k) p", p=P)
                sp.dma_start(rows_p[row:row + rows, :], src).then_inc(S["params_loaded"], mark("params_loaded", name, 16))
                row += rows
            sp.dma_start(rows_m[0:16, :], A["mlstm_norm_g"].rearrange("l (k p) -> (l k) p", p=P)).then_inc(
                S["params_loaded"], mark("params_loaded", "m", 16))
            sp.dma_start(onehot, A["onehot"]).then_inc(S["params_loaded"], mark("params_loaded", "onehot", 16))
            sp.dma_start(rel_sb, A["rel_bias"]).then_inc(S["params_loaded"], mark("params_loaded", "rel", 16))
            with nc.allow_non_contiguous_dma(reason="sixteen gate biases"):
                sp.dma_start(gate_b[0:M_HEADS, :], A["b_igate"].rearrange("l h -> h l")).then_inc(
                    S["params_loaded"], mark("params_loaded", "bi", 16))
                sp.dma_start(gate_b[GATE_F:GATE_F + M_HEADS, :], A["b_fgate"].rearrange("l h -> h l")).then_inc(
                    S["params_loaded"], mark("params_loaded", "bf", 16))
            sp.dma_start(neg_sink[:].rearrange("p l h -> p (l h)"),
                             A["attn_sinks"].rearrange("(o l) h -> o (l h)", o=1).broadcast_to([P, DEPTH * A_HEADS])).then_inc(
                S["params_loaded"], mark("params_loaded", "sink", 16))
            shifted = bass.AP(tensor=A["toep"].tensor, offset=WINDOW - 1, ap=[[383, P], [P * 384, A_HEADS], [1, 256]])

            counts.region = "layer"
            with sp.Fori(0, DEPTH) as l:
                counts.layer = l
                sp.wait_ge(S["lo_ready"], counts.free(0, RAW_RING, False))
                win = A["w_in"][bass.ds(l, 1)].rearrange("o k n -> (o k) n").rearrange("(k p) n -> p k n", p=P)
                with nc.allow_non_contiguous_dma(reason="eight columns"):
                    sp.wait_ge(S["consts"], at("consts", "gate_raw", "pre"))
                    sp.dma_start(gate_raw[:, :, 0:M_HEADS], win[:, :, COL_MI:COL_MI + M_HEADS]).then_inc(
                        S["gate_loaded"], mark("gate_loaded", 0, 16))
                    sp.dma_start(gate_raw[:, :, GATE_F:GATE_F + M_HEADS], win[:, :, COL_MF:COL_MF + M_HEADS]).then_inc(
                        S["gate_loaded"], mark("gate_loaded", 1, 16))
                for u, unit in enumerate(units):
                    if unit == ("mv", 0, "T"):
                        sp.wait_ge(S["toep_stored"], at("toep_stored", 0, "pre"))
                        sp.dma_start(bias, shifted).then_inc(S["bias_loaded"], mark("bias_loaded", 0, 16))
                    sp.wait_ge(S["consts"], at("consts", "gate_raw", "pre"))
                    sp.wait_ge(S["lo_ready"], counts.free(u, RAW_RING, False))
                    unit_dma(sp, unit, u % RAW_RING, l, False)

            counts.region = "post"
            counts.layer = None
            def rows_of(w):
                return w.broadcast_to([P, D])

            sp.wait_ge(S["mx_ready"], at("mx_ready", (A_KV - 1, 1, GROUP - 1), "layer"))
            sp.dma_start(g_row, rows_of(A["final_norm_g"].rearrange("(o d) -> o d", o=1))).then_inc(
                S["g_loaded"], mark("g_loaded", "fin", 16))
            for u, unit in enumerate(units2):
                if unit == ("ga2", 0, "F"):
                    sp.wait_ge(S["x_fin"], at("x_fin", TT - 1))
                    sp.dma_start(g_row, rows_of(A["norm2_g_2"])).then_inc(S["g_loaded"], mark("g_loaded", "n2", 16))
                elif unit == ("mix", 0, "T"):
                    sp.wait_ge(S["x_lo"], at("x_lo", ("y2", KT - 1)))
                    for h in range(HP):
                        sp.dma_start(raw_keys[:, h, :], A["peer_sub_keys_2"][0, h // 2, h % 2]).then_inc(
                            S["keys_loaded"], mark("keys_loaded", h, 16))
                sp.wait_ge(S["lo_ready"], counts.free(u, RAW_RING, True))
                unit_dma(sp, unit, u % RAW_RING, None, True)
            sp.wait_ge(S["lo_ready"], at("lo_ready", ("u2", len(units2) - 1)))
            sp.dma_start(g_last, rows_of(A["final_norm_g_2"].rearrange("(o d) -> o d", o=1))).then_inc(
                S["g_last_loaded"], mark("g_last_loaded", 0, 16))
            dst = out[0].rearrange("(t p) d -> p t d", p=P)
            for t in range(TT):
                sp.wait_ge(S["final_ready"], at("final_ready", t))
                sp.dma_start(dst[:, t, :], x_res[:, t, :]).then_inc(S["out_stored"], mark("out_stored", t, 16))
            sp.wait_ge(S["out_stored"], at("out_stored", TT - 1))

        def split_hi(act, u, second):
            s, r = ring_slot(u, second), u % RAW_RING
            act.wait_ge(S["unit_done"], counts.free(u, RING, second))
            act.wait_ge(S[f"w_loaded{r}"], at(f"w_loaded{r}", ("u2" if second else "u", u)))
            nc.scalar.copy(w_hi[:, s, :], raw[r]).then_inc(S["hi_ready"], mark("hi_ready", ("u2" if second else "u", u)))

        def split_lo(dve, u, second):
            s = ring_slot(u, second)
            dve.wait_ge(S["hi_ready"], at("hi_ready", ("u2" if second else "u", u)))
            nc.vector.tensor_tensor(w_lo[:, s, :], raw[u % RAW_RING], w_hi[:, s, :].bitcast(F32), ALU.subtract).then_inc(
                S["lo_ready"], mark("lo_ready", ("u2" if second else "u", u)))

        def passes(out_, lh, ll, rh, rl, first, last):
            nc.tensor.matmul(out_, lh, rh, start=first, stop=False)
            nc.tensor.matmul(out_, ll, rh, start=False, stop=False)
            return nc.tensor.matmul(out_, lh, rl, start=False, stop=last)

        def unit_f(banks, s, xh, xl, key, turned=None):
            h, lw = whi(s, "F"), wlo(s, "F")
            for n_ in range(2):
                for k in range(8):
                    if turned and n_ == 0:
                        nc.tensor.wait_ge(S["x_lo"], at("x_lo", (turned, k | 1)))
                    m = passes(banks[0][:, n_ * SEQ:(n_ + 1) * SEQ], h[:, k, n_ * P:(n_ + 1) * P],
                               lw[:, k, n_ * P:(n_ + 1) * P], xh[:, k, :], xl[:, k, :], k == 0, k == 7)
            m.then_inc(S["unit_done"], mark("unit_done", key))

        def unit_y(banks, s, xh, xl, key, turned=None):
            h, lw = whi(s, "F"), wlo(s, "F")
            for b in range(2):
                for n_ in range(2):
                    for k in range(4):
                        kk = 4 * b + k
                        if turned and n_ == 0:
                            nc.tensor.wait_ge(S["x_lo"], at("x_lo", (turned, kk | 1)))
                        m = passes(banks[b][:, n_ * SEQ:(n_ + 1) * SEQ], h[:, kk, n_ * P:(n_ + 1) * P],
                                   lw[:, kk, n_ * P:(n_ + 1) * P], xh[:, kk, :], xl[:, kk, :], k == 0, k == 3)
            m.then_inc(S["unit_done"], mark("unit_done", key))

        def unit_v(banks, s, xh, xl, key):
            h, lw = whi(s, "F"), wlo(s, "F")
            for t in range(TT):
                for k in range(8):
                    tok = slice(t * P, (t + 1) * P)
                    m = passes(banks[0][:, t * 256:(t + 1) * 256], xh[:, k, tok], xl[:, k, tok],
                               h[:, k, :], lw[:, k, :], k == 0, k == 7)
            m.then_inc(S["unit_done"], mark("unit_done", key))

        def unit_t(banks, s, xh, xl, k0, first, last, key, tile_key=None):
            h, lw = whi(s, "T"), wlo(s, "T")
            for t in range(TT):
                tok = slice(t * P, (t + 1) * P)
                for k in range(4):
                    m = passes(banks[t][:], xh[:, k0 + k, tok], xl[:, k0 + k, tok], h[:, k, :], lw[:, k, :],
                               first and k == 0, last and k == 3)
                if tile_key and t == 0:
                    m.then_inc(S["tile_done"], mark("tile_done", tile_key))
            m.then_inc(S["unit_done"], mark("unit_done", key))

        ssq, rstd = small[:, 0:2], small[:, 2:4]
        eps_d, eps_v, idle, zero_all, idle_dve = small[:, 240:242], small[:, 242:250], small[:, 251:252], small[:, 252:253], small[:, 253:254]
        junk = hn

        def norm_act(act, tag):
            for t in range(TT):
                if tag in ("mix", "fin"):
                    act.wait_ge(S["mlp_added"], counts.at_layer_start("mlp_added") - (TT - 1 - t))
                elif tag == "n1":
                    act.wait_ge(S["x_fin"], at("x_fin", t))
                elif tag == "last":
                    act.wait_ge(S["x_peer"], at("x_peer", (t, 1)))
                else:
                    act.wait_ge(S["emptied_dve"], at("emptied_dve", ("wo" if tag == "mlp" else "mix", 2 + t)))
                nc.scalar.activation(junk[:, t, :], x_res[:, t, :], ACT.Square, accum_out=ssq[:, t:t + 1]).then_inc(
                    S["ssq_ready"], mark("ssq_ready", (tag, t)))

        def norm_pool(pool, tag):
            for t in range(TT):
                pool.wait_ge(S["ssq_ready"], at("ssq_ready", (tag, t)))
                nc.gpsimd.tensor_tensor(rstd[:, t:t + 1], ssq[:, t:t + 1], eps_d[:, 0:1], ALU.add).then_inc(
                    S["ms_ready"], mark("ms_ready", (tag, t)))
                pool.wait_ge(S["ms_ready"], at("ms_ready", (tag, t)))
                nc.gpsimd.tensor_tensor(rstd[:, t:t + 1], rstd[:, t:t + 1], minus_half[:, 0:1], ALU.pow).then_inc(
                    S["rstd_ready"], mark("rstd_ready", (tag, t)))

        def norm_dve(dve, tag):
            for t in range(TT):
                dve.wait_ge(S["rstd_ready"], at("rstd_ready", (tag, t)))
                nc.vector.tensor_scalar(hn[:, t, :], x_res[:, t, :], rstd[:, t:t + 1], D ** 0.5, ALU.mult, ALU.mult).then_inc(
                    S["hn_ready"], mark("hn_ready", (tag, t)))

        def last_norm_act(act, t):
            act.wait_ge(S["x_peer"], at("x_peer", (t, 1)))
            nc.scalar.activation(junk[:, t, :], x_res[:, t, :], ACT.Square, accum_out=ssq[:, t:t + 1]).then_inc(
                S["ssq_ready"], mark("ssq_ready", ("last", t)))

        def last_norm_pool(pool, t):
            pool.wait_ge(S["ssq_ready"], at("ssq_ready", ("last", t)))
            nc.gpsimd.tensor_tensor(rstd[:, t:t + 1], ssq[:, t:t + 1], eps_d[:, 0:1], ALU.add).then_inc(
                S["ms_ready"], mark("ms_ready", ("last", t)))
            pool.wait_ge(S["ms_ready"], at("ms_ready", ("last", t)))
            nc.gpsimd.tensor_tensor(rstd[:, t:t + 1], rstd[:, t:t + 1], minus_half[:, 0:1], ALU.pow).then_inc(
                S["rstd_ready"], mark("rstd_ready", ("last", t)))

        def turn_pe(pe, src, tag, ready, kts=KT):
            for t in range(TT):
                pe.wait_ge(S[ready[t][0]], at(*ready[t]))
                for k in range(kts):
                    m = nc.tensor.transpose(att[k // 2][:, (k % 2) * SEQ + t * P:(k % 2) * SEQ + (t + 1) * P],
                                            src(k, t), ident[:])
                    if t == TT - 1:
                        m.then_inc(S["turned"], mark("turned", (tag, k)))

        def turn_act(act, dst_hi, tag, scale, kts=KT):
            for k in range(kts):
                act.wait_ge(S["turned"], at("turned", (tag, k | 1)))
                ps = att[k // 2][:, (k % 2) * SEQ:(k % 2 + 1) * SEQ]
                nc.scalar.activation(dst_hi[:, k, :], ps, ACT.Copy, scale=scale(k)).then_inc(S["x_hi"], mark("x_hi", (tag, k)))

        def turn_dve(dve, dst_hi, dst_lo, tag, scale, kts=KT):
            for k in range(kts):
                dve.wait_ge(S["x_hi"], at("x_hi", (tag, k | 1)))
                ps = att[k // 2][:, (k % 2) * SEQ:(k % 2 + 1) * SEQ]
                nc.vector.scalar_tensor_tensor(dst_lo[:, k, :], ps, scale(k), dst_hi[:, k, :].bitcast(F32),
                                                   ALU.mult, ALU.subtract).then_inc(S["x_lo"], mark("x_lo", (tag, k)))

        g_i, g_f, g_n, g_e = gates[:, 0, :], gates[:, 1, :], gates[:, 2, :], gates[:, 3, :]
        g_B, g_a, g_M, g_m = gates[:, 4, :], gates[:, 5, :], gates[:, 6, :], gates[:, 7, :]
        acol = small[:, 4:20]
        n_ss, n_dn, n_ms, n_c = small[:, 20:28], small[:, 28:36], small[:, 36:44], small[:, 44:52]
        n_rec = small[:, 52:60]
        mx, negm, sums, esink, rinv = (small[:, 60 + 8 * i:68 + 8 * i] for i in range(5))

        BANKS = {}
        for i in range(4):
            BANKS["mqk", i] = [acc[i]]
            BANKS["aq", i] = [acc[i]]
            for name in ("ga", "gb", "bm", "ba"):
                BANKS[name, i] = [acc[(2 + i) % 4]]
            BANKS["mv", i] = [acc[2 * (i // 2)], acc[2 * (i // 2) + 1]]
            for name in ("mo", "wo"):
                BANKS[name, i] = [acc[(2 + 2 * (i // 2)) % 4], acc[(3 + 2 * (i // 2)) % 4]]
        BANKS["ak", 0], BANKS["av", 0] = [acc[0]], [acc[1]]
        for i in range(16):
            BANKS["up", i] = [att[i % 2]]
            BANKS["down", i] = [acc[i % 2], acc[2 + i % 2]]
        BEFORE = {("mv", 0): [("mqk", 0), ("mqk", 1)], ("mv", 2): [("mqk", 2), ("mqk", 3)],
                  ("aq", 0): [("mv", 1)], ("aq", 2): [("mv", 3)], ("ak", 0): [("aq", 0)], ("av", 0): [("aq", 1)],
                  ("mo", 0): [("aq", 2), ("aq", 3)], ("mo", 2): [("ak", 0), ("av", 0)],
                  ("ga", 0): [("mo", 1)], ("ga", 2): [("mo", 3)]}
        for i in range(4):
            BEFORE["gb", i], BEFORE["bm", i], BEFORE["ba", i] = [("ga", i)], [("gb", i)], [("bm", i)]
        BEFORE["wo", 0], BEFORE["wo", 2] = [("ba", 0), ("ba", 1)], [("ba", 2), ("ba", 3)]
        BEFORE["down", 0], BEFORE["down", 1] = [("wo", 1), ("wo", 3)], []
        for i in range(2, 16):
            BEFORE["up", i] = [("up", i - 2)]
        BY_ACT = {"mqk", "mv", "aq", "av"}

        def emptied(eng, name, i):
            eng.wait_ge(S["emptied_act" if name in BY_ACT else "emptied_dve"], at("emptied_act" if name in BY_ACT else "emptied_dve", (name, i)))

        def layer_pe(pe, l):
            def turn_norm(tag):
                turn_pe(pe, lambda k, t: hn[:, t, k * P:(k + 1) * P], tag,
                        [("hn_ready", (tag, 0)), ("hn_ready", (tag, 1))])

            def gate_products():
                pe.wait_ge(S["gate_lo"], at("gate_lo"))
                for k in range(KT):
                    m = passes(att[0][0:GW, 0:SEQ], gate_hi[:, k, :], gate_lo[:, k, :], xa_hi[:, k, :], xa_lo[:, k, :],
                               k == 0, k == KT - 1)
                m.then_inc(S["gate_done"], mark("gate_done"))

            def gate_columns():
                pe.wait_ge(S["gate_m"], at("gate_m"))
                for h in range(M_HEADS):
                    m = nc.tensor.matmul(att[h // 2][:, (h % 2) * SEQ:(h % 2 + 1) * SEQ], ident[0:M_HEADS, h:h + 1].broadcast_to([M_HEADS, P]), g_M,
                                         start=True, stop=True)
                pe.wait_ge(S["gate_enm"], at("gate_enm"))
                for n_, row in enumerate((g_a, g_m)):
                    for t in range(TT):
                        m = nc.tensor.matmul(att[2][:, (2 * n_ + t) * 4:(2 * n_ + t) * 4 + 4], row[:, t * P:(t + 1) * P],
                                             ident[0:4, 0:4], start=True, stop=True)
                m.then_inc(S["columns_done"], mark("columns_done"))

            def kq(h):
                b = att[2 + h % 2]
                if h == 0:
                    pe.wait_ge(S["acol_ready"], at("acol_ready"))
                pe.wait_ge(S["silu"], at("silu", h))
                pe.wait_ge(S["silu"], at("silu", 4 + h))
                if h >= 2:
                    pe.wait_ge(S["s_ready"], at("s_ready", h - 2))
                nc.tensor.matmul(b[:, 0:256], qk[:, 4 + h, 0:P], qk[:, h, :], start=True, stop=True)
                m = nc.tensor.matmul(b[:, 256:384], qk[:, 4 + h, P:2 * P], qk[:, h, P:2 * P], start=True, stop=True)
                m.then_inc(S["kq_done"], mark("kq_done", h))

            def num_product(h):
                pe.wait_ge(S["s_ready"], at("s_ready", h))
                if h >= 1:
                    pe.wait_ge(S["num_ready"], at("num_ready", (h - 1, 1)))
                s = sm[:, h % 2, :]
                nc.tensor.matmul(att[0][:, 0:VW], s[:, 0:P], mv[:, 0, h, :], start=True, stop=True).then_inc(
                    S["num_done"], mark("num_done", (h, 0)))
                nc.tensor.matmul(att[1][:, 0:VW], s[:, P:2 * P], mv[:, 0, h, :], start=True, stop=False)
                nc.tensor.matmul(att[1][:, 0:VW], s[:, 2 * P:3 * P], mv[:, 1, h, :], start=False, stop=True).then_inc(
                    S["num_done"], mark("num_done", (h, 1)))

            def scores(j):
                if j == 0:
                    pe.wait_ge(S["num_ready"], at("num_ready", (3, 1)))
                    emptied(pe, "ak", 0)
                    emptied(pe, "aq", 3)
                else:
                    pe.wait_ge(S["pT_ready"], at("pT_ready", (j - 1, 2)))
                for g in range(GROUP):
                    h = GROUP * j + g
                    q, k_ = aq[:, h // 2, :], ak[:, h % 2, j, :]
                    nc.tensor.matmul(att[0][:, g * P:(g + 1) * P], q[:, 0:P], k_[:, 0:P], start=True, stop=True)
                    m = nc.tensor.matmul(att[1 + g // 2][:, (g % 2) * SEQ:(g % 2 + 1) * SEQ], q[:, P:2 * P], k_[:, :],
                                         start=True, stop=True)
                m.then_inc(S["scores_done"], mark("scores_done", j))

            def turn_probs(j):
                pe.wait_ge(S["probs_ready"], at("probs_ready", (j, 7)))
                for c in range(3):
                    for g in range(GROUP):
                        m = nc.tensor.transpose(att[c][:, g * P:(g + 1) * P], lg[:, g, c * P:(c + 1) * P], ident[:])
                    m.then_inc(S["probs_turned"], mark("probs_turned", (j, c)))

            def pv(j):
                pe.wait_ge(S["pT_ready"], at("pT_ready", (j, 2)))
                if j >= 1:
                    pe.wait_ge(S["ha_ready"], at("ha_ready", (j - 1, 1)))
                else:
                    emptied(pe, "av", 0)
                v0, v1 = av[:, 0, j * A_DH:(j + 1) * A_DH], av[:, 1, j * A_DH:(j + 1) * A_DH]
                for g in range(GROUP):
                    nc.tensor.matmul(att[3][:, g * A_DH:(g + 1) * A_DH], pT[:, 0, g, :], v0, start=True, stop=True)
                for g in range(GROUP):
                    c = 256 + g * A_DH
                    nc.tensor.matmul(att[3][:, c:c + A_DH], pT[:, 1, g, :], v0, start=True, stop=False)
                    m = nc.tensor.matmul(att[3][:, c:c + A_DH], pT[:, 2, g, :], v1, start=False, stop=True)
                m.then_inc(S["pv_done"], mark("pv_done", j))

            def turn_hm():
                pe.wait_ge(S["ha_ready"], at("ha_ready", (3, 1)))
                turn_pe(pe, lambda k, t: mo[:, t, k * P:(k + 1) * P], "hm", [("hm_ready", (0, 3)), ("hm_ready", (1, 3))])

            def turn_ha():
                pe.wait_ge(S["x_lo"], at("x_lo", ("hm", KT - 1)))
                turn_pe(pe, lambda k, t: ha[:, t, k * P:(k + 1) * P], "ha", [("ha_ready", (3, 0)), ("ha_ready", (3, 1))])

            turn_norm("mix")
            for u, (name, i, kind) in enumerate(units):
                pe.wait_ge(S["lo_ready"], at("lo_ready", ("u", u)))
                for p in BEFORE.get((name, i), []):
                    emptied(pe, *p)
                if name == "wo" and i < 2:
                    pe.wait_ge(S["y_lo"], at("y_lo", 2 * i + 1))
                if name == "down" and i % 2 == 0:
                    pe.wait_ge(S["ff_lo"], at("ff_lo", i + 1))
                xh, xl = (xb_hi, xb_lo) if name in ("bm", "wo", "down") else (xa_hi, xa_lo)
                b, s = BANKS[name, i], ring_slot(u, False)
                if kind == "F":
                    first = {("mqk", 0): "mix", ("bm", 0): "hm", ("ba", 0): "ha", ("up", 0): "mlp"}
                    unit_f(b, s, xh, xl, ("u", u), first.get((name, i)))
                elif kind == "V":
                    unit_v(b, s, xh, xl, ("u", u))
                elif name == "down":
                    unit_t(b, s, xh, xl, 4 * (i // 2 % 2), i < 2, i >= 14, ("u", u), "down" if i == 15 else None)
                else:
                    unit_t(b, s, xh, xl, 4 * (i % 2), i % 2 == 0, i % 2 == 1, ("u", u),
                           "wo" if (name, i) == ("wo", 3) else None)
                if (name, i) == ("mqk", 3):
                    gate_products()
                elif (name, i) == ("aq", 0):
                    gate_columns()
                elif (name, i) == ("aq", 1):
                    kq(0)
                    kq(1)
                elif (name, i) == ("aq", 3):
                    num_product(0)
                    kq(2)
                elif (name, i) == ("ak", 0):
                    num_product(1)
                    kq(3)
                elif (name, i) == ("av", 0):
                    num_product(2)
                elif (name, i) == ("mo", 0):
                    num_product(3)
                elif (name, i) == ("mo", 1):
                    scores(0)
                elif (name, i) == ("mo", 2):
                    turn_probs(0)
                elif (name, i) == ("mo", 3):
                    pv(0)
                    scores(1)
                elif (name, i) == ("ga", 0):
                    turn_probs(1)
                elif (name, i) == ("ga", 1):
                    pv(1)
                    scores(2)
                elif (name, i) == ("ga", 2):
                    turn_probs(2)
                elif (name, i) == ("ga", 3):
                    pv(2)
                    scores(3)
                elif (name, i) == ("gb", 0):
                    turn_probs(3)
                elif (name, i) == ("gb", 1):
                    pv(3)
                elif (name, i) == ("gb", 3):
                    turn_hm()
                elif (name, i) == ("bm", 0):
                    turn_ha()
                elif (name, i) == ("wo", 3):
                    turn_norm("mlp")

        def layer_act(act, l):
            def unit(name, i):
                act.wait_ge(S["unit_done"], at("unit_done", ("u", at_unit[name, i])))

            def gate_split():
                act.wait_ge(S["gate_loaded"], at("gate_loaded", 1))
                nc.scalar.copy(gate_hi[:], gate_raw[:]).then_inc(S["gate_hi"], mark("gate_hi"))

            def gate_softplus():
                act.wait_ge(S["gate_nabs"], at("gate_nabs"))
                nc.scalar.activation(g_e, g_n, ACT.Exp).then_inc(S["gate_exp"], mark("gate_exp"))
                act.wait_ge(S["gate_exp"], at("gate_exp"))
                nc.scalar.activation(g_e, g_e, ACT.Ln, bias=1.0).then_inc(S["gate_ln"], mark("gate_ln"))

            def gate_enm():
                act.wait_ge(S["gate_m"], at("gate_m"))
                nc.scalar.activation(g_m, g_m, ACT.Exp).then_inc(S["gate_enm"], mark("gate_enm"))

            def silu_sigmoid():
                act.wait_ge(S["conv"], at("conv", 7))
                for k in range(4):
                    nc.scalar.activation(sig[:, 2 * k:2 * k + 2, :], qk[:, 2 * k:2 * k + 2, :], ACT.Sigmoid).then_inc(
                        S["silu_sig"], mark("silu_sig", k))

            def decay_exp():
                act.wait_ge(S["z_masked"], at("z_masked", 1))
                nc.scalar.activation(zw, zw, ACT.Exp).then_inc(S["w_ready"], mark("w_ready"))

            def num_take(h):
                for t in range(TT):
                    act.wait_ge(S["num_done"], at("num_done", (h, t)))
                    nc.scalar.copy(num[:, t, h, :], att[t][:, 0:VW]).then_inc(S["num_ready"], mark("num_ready", (h, t)))

            def num_squares():
                act.wait_ge(S["num_ready"], at("num_ready", (3, 1)))
                for t in range(TT):
                    for h in range(M_HEADS):
                        nc.scalar.activation(sm[:, t, 0:M_DV], num[:, t, h, 0:M_DV], ACT.Square,
                                                 accum_out=n_ss[:, 4 * t + h:4 * t + h + 1]).then_inc(
                            S["num_ssq"], mark("num_ssq", (t, h)))
                        act.wait_ge(S["num_ssq"], at("num_ssq", (t, h)))

            def probs(j):
                for t in range(TT):
                    act.wait_ge(S["negm_ready"], at("negm_ready", (j, t)))
                    for g in range(GROUP):
                        piece = lg[:, g, 0:P] if t == 0 else lg[:, g, P:3 * P]
                        nc.scalar.activation(piece, piece, ACT.Exp, bias=negm[:, 4 * t + g:4 * t + g + 1],
                                             accum_out=sums[:, 4 * t + g:4 * t + g + 1]).then_inc(
                            S["probs_ready"], mark("probs_ready", (j, GROUP * t + g)))
                act.wait_ge(S["sink_diff"], at("sink_diff", (j, 1)))
                nc.scalar.activation(esink, esink, ACT.Exp).then_inc(S["sink_exp"], mark("sink_exp", j))

            def probs_take(j):
                if j >= 1:
                    act.wait_ge(S["pv_done"], at("pv_done", j - 1))
                for c in range(3):
                    act.wait_ge(S["probs_turned"], at("probs_turned", (j, c)))
                    nc.scalar.copy(pT[:, c, :, :], att[c][:].rearrange("p (h k) -> p h k", h=GROUP)).then_inc(
                        S["pT_ready"], mark("pT_ready", (j, c)))

            def sigmoid(tile, name, sem_, key):
                act.wait_ge(S["emptied_dve"], at("emptied_dve", (name, 3)))
                nc.scalar.activation(tile, tile, ACT.Sigmoid).then_inc(S[sem_], mark(sem_, key))

            def take(name, i):
                b = BANKS[name, i]
                if name == "mqk":
                    unit(name, i)
                    nc.scalar.copy(mqk[:, 2 * i:2 * i + 2, CONV_K - 1:CW], b[0][:].rearrange("p (n t) -> p n t", n=2)).then_inc(
                        S["emptied_act"], mark("emptied_act", (name, i)))
                elif name == "aq":
                    unit(name, i)
                    nc.scalar.mul(aq[:, 2 * i:2 * i + 2, :], b[0][:].rearrange("p (n t) -> p n t", n=2), A_DH ** -0.5).then_inc(
                        S["emptied_act"], mark("emptied_act", (name, i)))
                elif name == "av":
                    unit(name, i)
                    nc.scalar.copy(av, b[0][:].rearrange("p (t v) -> p t v", t=TT)).then_inc(
                        S["emptied_act"], mark("emptied_act", (name, i)))
                elif name == "mv" and i % 2 == 1:
                    unit(name, i)
                    for t in range(TT):
                        nc.scalar.copy(mv[:, t, i - 1:i + 1, 0:M_DV], b[t][:].rearrange("p (h v) -> p h v", h=2)).then_inc(
                            S["emptied_act"], mark("emptied_act", (name, i - 1 + t)))
                elif name == "ba":
                    act.wait_ge(S["y_ready"], at("y_ready", i))
                    nc.scalar.copy(xb_hi[:, 2 * i:2 * i + 2, :], ga[:, 2 * i:2 * i + 2, :]).then_inc(S["y_hi"], mark("y_hi", i))
                elif name == "up":
                    k0 = 4 * (i // 2 % 2) + 2 * (i % 2)
                    act.wait_ge(S["emptied_dve"], at("emptied_dve", (name, i)))
                    nc.scalar.activation(sq[:, 2 + i % 2, :], sq[:, i % 2, :], ACT.Square).then_inc(
                        S["ff_sq"], mark("ff_sq", i))
                    act.wait_ge(S["ff_sq"], at("ff_sq", i))
                    if i >= 4:
                        act.wait_ge(S["unit_done"], at("unit_done", ("u", at_unit["down", 2 * (i // 2 - 2) + 1])))
                    nc.scalar.copy(xb_hi[:, k0:k0 + 2, :], sq[:, 2 + i % 2, :].rearrange("p (n t) -> p n t", n=2)).then_inc(
                        S["ff_hi"], mark("ff_hi", i))

            split_hi(act, 0, False)
            norm_act(act, "mix")
            act.wait_ge(S["start_taken"], at("start_taken", 1, "pre"))
            turn_act(act, xa_hi, "mix", lambda k: col("norm_mix_g", l, k))
            split_hi(act, 1, False)
            for u, (name, i, kind) in enumerate(units):
                if u + 2 < NU:
                    split_hi(act, u + 2, False)
                take(name, i)
                if (name, i) == ("mqk", 0):
                    gate_split()
                elif (name, i) == ("mv", 0):
                    gate_softplus()
                elif (name, i) == ("mv", 1):
                    gate_enm()
                elif (name, i) == ("aq", 0):
                    silu_sigmoid()
                elif (name, i) == ("aq", 2):
                    decay_exp()
                elif (name, i) == ("aq", 3):
                    num_take(0)
                elif (name, i) == ("ak", 0):
                    num_take(1)
                elif (name, i) == ("av", 0):
                    num_take(2)
                elif (name, i) == ("mo", 0):
                    num_take(3)
                    num_squares()
                elif (name, i) == ("mo", 1):
                    probs(0)
                elif (name, i) == ("mo", 2):
                    probs_take(0)
                elif (name, i) == ("mo", 3):
                    probs(1)
                elif (name, i) == ("ga", 0):
                    probs_take(1)
                elif (name, i) == ("ga", 1):
                    probs(2)
                elif (name, i) == ("ga", 2):
                    probs_take(2)
                elif (name, i) == ("ga", 3):
                    probs(3)
                elif (name, i) == ("gb", 0):
                    probs_take(3)
                    sigmoid(mo, "mo", "mo_sig", 0)
                    sigmoid(ga, "ga", "g_sig", 0)
                elif (name, i) == ("gb", 3):
                    turn_act(act, xb_hi, "hm", lambda k: m_col(l, k))
                    sigmoid(gb, "gb", "g_sig", 1)
                elif (name, i) == ("bm", 0):
                    turn_act(act, xa_hi, "ha", lambda k: 1.0)
                elif (name, i) == ("wo", 3):
                    norm_act(act, "mlp")
                    turn_act(act, xa_hi, "mlp", lambda k: col("norm_mlp_g", l, k))

        def m_col(l, k):
            return params_m[:, bass.ds(l * 8 + k, 1)]

        def layer_dve(dve, l):
            def unit(name, i):
                dve.wait_ge(S["unit_done"], at("unit_done", ("u", at_unit[name, i])))

            def gate_split():
                dve.wait_ge(S["gate_hi"], at("gate_hi"))
                nc.vector.tensor_tensor(gate_lo[:], gate_raw[:], gate_hi[:].bitcast(F32), ALU.subtract).then_inc(
                    S["gate_lo"], mark("gate_lo"))

            def gate_start():
                dve.wait_ge(S["gate_done"], at("gate_done"))
                bi, bf = gate_b[0:M_HEADS, bass.ds(l, 1)], gate_b[GATE_F:GATE_F + M_HEADS, bass.ds(l, 1)]
                nc.vector.tensor_scalar(g_i, att[0][0:M_HEADS, 0:SEQ], bi, None, ALU.add).then_inc(
                    S["gate_in"], mark("gate_in", 0))
                nc.vector.tensor_scalar(g_f, att[0][GATE_F:GATE_F + M_HEADS, 0:SEQ], bf, None, ALU.add).then_inc(
                    S["gate_in"], mark("gate_in", 1))
                dve.wait_ge(S["gate_in"], at("gate_in", 1))
                nc.vector.scalar_tensor_tensor(g_n, g_f, -1.0, g_f, ALU.mult, ALU.min).then_inc(
                    S["gate_nabs"], mark("gate_nabs"))

            def gate_rows():
                dve.wait_ge(S["gate_ln"], at("gate_ln"))
                nc.vector.scalar_tensor_tensor(g_n, g_f, 0.0, g_e, ALU.min, ALU.subtract).then_inc(
                    S["gate_row"], mark("gate_row", 0))
                dve.wait_ge(S["gate_row"], at("gate_row", 0))
                nc.vector.tensor_tensor_scan(g_B, ones_row, g_n, 0.0, ALU.mult, ALU.add).then_inc(
                    S["gate_row"], mark("gate_row", 1))
                dve.wait_ge(S["gate_row"], at("gate_row", 1))
                nc.vector.tensor_tensor(g_a, g_i, g_B, ALU.subtract).then_inc(S["gate_row"], mark("gate_row", 2))
                dve.wait_ge(S["gate_row"], at("gate_row", 2))
                nc.vector.tensor_tensor_scan(g_f, zero_row, g_a, 0.0, ALU.max, ALU.max).then_inc(
                    S["gate_row"], mark("gate_row", 3))
                dve.wait_ge(S["gate_row"], at("gate_row", 3))
                nc.vector.tensor_scalar(g_M, g_f, -1.0, None, ALU.mult).then_inc(S["gate_row"], mark("gate_row", 4))
                nc.vector.scalar_tensor_tensor(g_m, g_B, -1.0, g_f, ALU.mult, ALU.subtract).then_inc(
                    S["gate_m"], mark("gate_m"))

            def conv(tiles):
                dve.wait_ge(S["pads_ready"], at("pads_ready", 1))
                dve.wait_ge(S["emptied_act"], at("emptied_act", ("mqk", tiles[-1] // 2)))
                for k in tiles:
                    nc.vector.tensor_scalar(qk[:, k, :], mqk[:, k, 0:SEQ], col("conv_w", l, k), col("conv_b", l, k),
                                                ALU.mult, ALU.add).then_inc(S["conv_tap"], mark("conv_tap", (k, 0)))
                for j in range(1, CONV_K):
                    for k in tiles:
                        dve.wait_ge(S["conv_tap"], at("conv_tap", (k, j - 1)))
                        nc.vector.scalar_tensor_tensor(qk[:, k, :], mqk[:, k, j:j + SEQ], col("conv_w", l, 8 * j + k),
                                                           qk[:, k, :], ALU.mult, ALU.add).then_inc(
                            S["conv" if j == CONV_K - 1 else "conv_tap"], mark("conv" if j == CONV_K - 1 else "conv_tap", k if j == CONV_K - 1 else (k, j)))

            def decay():
                dve.wait_ge(S["columns_done"], at("columns_done"))
                nc.vector.tensor_copy(acol, att[2][:, 0:16]).then_inc(S["acol_ready"], mark("acol_ready"))
                dve.wait_ge(S["acol_ready"], at("acol_ready"))
                for h in range(M_HEADS):
                    row = att[h // 2][:, (h % 2) * SEQ:(h % 2 + 1) * SEQ]
                    nc.vector.tensor_scalar(zw[:, h, 0:SEQ], row, acol[:, h:h + 1], None, ALU.add).then_inc(
                        S["z_ready"], mark("z_ready", (h, 0)))
                    nc.vector.tensor_scalar(zw[:, h, SEQ:384], row[:, P:2 * P], acol[:, 4 + h:5 + h], None, ALU.add).then_inc(
                        S["z_ready"], mark("z_ready", (h, 1)))

            def s_take(h):
                dve.wait_ge(S["w_ready"], at("w_ready"))
                dve.wait_ge(S["kq_done"], at("kq_done", h))
                if h >= 2:
                    dve.wait_ge(S["num_done"], at("num_done", (h - 2, 1)))
                nc.vector.scalar_tensor_tensor(sm[:, h % 2, :], att[2 + h % 2][:, 0:384], M_DK ** -0.5, zw[:, h, :],
                                                   ALU.mult, ALU.mult).then_inc(S["s_ready"], mark("s_ready", h))

            def num_scale():
                for t in range(TT):
                    d = num[:, t, :, M_DV]
                    dve.wait_ge(S["num_ready"], at("num_ready", (3, t)))
                    nc.vector.scalar_tensor_tensor(n_dn[:, 4 * t:4 * t + 4], d, -1.0, acol[:, 8 + 4 * t:12 + 4 * t],
                                                       ALU.mult, ALU.max).then_inc(S["den_part"], mark("den_part", t))
                    dve.wait_ge(S["den_part"], at("den_part", t))
                    nc.vector.tensor_tensor(n_dn[:, 4 * t:4 * t + 4], n_dn[:, 4 * t:4 * t + 4], d, ALU.max).then_inc(
                        S["den_abs"], mark("den_abs", t))
                dve.wait_ge(S["den_abs"], at("den_abs", 1))
                nc.vector.reciprocal(n_rec, n_dn).then_inc(S["den_rec"], mark("den_rec"))

            def hm():
                dve.wait_ge(S["mo_sig"], at("mo_sig"))
                dve.wait_ge(S["num_norm"], at("num_norm", 3))
                nc.vector.scalar_tensor_tensor(n_c, n_ms, M_DV ** 0.5, n_rec, ALU.mult, ALU.mult).then_inc(
                    S["num_factor"], mark("num_factor"))
                dve.wait_ge(S["num_factor"], at("num_factor"))
                for t in range(TT):
                    for h in range(M_HEADS):
                        piece = mo[:, t, h * M_DV:(h + 1) * M_DV]
                        nc.vector.scalar_tensor_tensor(piece, num[:, t, h, 0:M_DV], n_c[:, 4 * t + h:4 * t + h + 1], piece,
                                                           ALU.mult, ALU.mult).then_inc(S["hm_ready"], mark("hm_ready", (t, h)))

            def logits(j):
                dve.wait_ge(S["scores_done"], at("scores_done", j))
                if j >= 1:
                    dve.wait_ge(S["probs_turned"], at("probs_turned", (j - 1, 2)))
                if j == 0:
                    dve.wait_ge(S["bias_loaded"], at("bias_loaded"))
                nc.vector.memset(idle_dve, 0.0)
                sink = neg_sink[:, bass.ds(l, 1), GROUP * j:GROUP * (j + 1)].rearrange("p o h -> p (o h)")
                for t in range(TT):
                    for g in range(GROUP):
                        h = GROUP * j + g
                        if t == 0:
                            dst, b, src = lg[:, g, 0:P], bias[:, h, P:2 * P], att[0][:, g * P:(g + 1) * P]
                        else:
                            dst, b = lg[:, g, P:3 * P], bias[:, h, :]
                            src = att[1 + g // 2][:, (g % 2) * SEQ:(g % 2 + 1) * SEQ]
                        nc.vector.tensor_tensor_reduce(out=dst, in0=src, in1=b, scale=1.0, scalar=LOWEST, op0=ALU.add,
                                                       op1=ALU.max, accum_out=mx[:, 4 * t + g:4 * t + g + 1]).then_inc(
                            S["mx_ready"], mark("mx_ready", (j, t, g)))
                    dve.wait_ge(S["mx_ready"], at("mx_ready", (j, t, GROUP - 1)))
                    nc.vector.scalar_tensor_tensor(negm[:, 4 * t:4 * t + 4], mx[:, 4 * t:4 * t + 4], -1.0, sink,
                                                   ALU.mult, ALU.min).then_inc(S["negm_ready"], mark("negm_ready", (j, t)))
                for t in range(TT):
                    dve.wait_ge(S["negm_ready"], at("negm_ready", (j, t)))
                    nc.vector.tensor_tensor(esink[:, 4 * t:4 * t + 4], negm[:, 4 * t:4 * t + 4], sink, ALU.subtract).then_inc(
                        S["sink_diff"], mark("sink_diff", (j, t)))

            def denominators(j):
                dve.wait_ge(S["sink_exp"], at("sink_exp", j))
                nc.vector.tensor_tensor(rinv, sums, esink, ALU.add).then_inc(S["denom"], mark("denom", j))
                dve.wait_ge(S["denom"], at("denom", j))
                nc.vector.reciprocal(rinv, rinv).then_inc(S["rinv_ready"], mark("rinv_ready", j))

            def ha_take(j):
                dve.wait_ge(S["pv_done"], at("pv_done", j))
                dve.wait_ge(S["rinv_ready"], at("rinv_ready", j))
                for t in range(TT):
                    nc.vector.tensor_tensor(ha[:, t, j * 256:(j + 1) * 256].rearrange("p (h d) -> p h d", h=GROUP),
                                                att[3][:, t * 256:(t + 1) * 256].rearrange("p (h d) -> p h d", h=GROUP),
                                                rinv[:, 4 * t:4 * t + 4].unsqueeze(2).broadcast_to([P, GROUP, A_DH]), ALU.mult).then_inc(
                        S["ha_ready"], mark("ha_ready", (j, t)))

            def take(name, i):
                b = BANKS[name, i]
                if name == "ak":
                    unit(name, i)
                    for j in range(A_KV):
                        ps = b[0][64 * (j % 2):64 * (j % 2) + 64, (j // 2) * SEQ:(j // 2 + 1) * SEQ]
                        for half in range(2):
                            nc.vector.tensor_copy(ak[64 * half:64 * half + 64, half, j, :], ps).then_inc(
                                S["emptied_dve" if (j, half) == (3, 1) else "ak_part"], mark("emptied_dve" if (j, half) == (3, 1) else "ak_part", (name, i) if (j, half) == (3, 1) else (j, half)))
                elif name == "mo" and i % 2 == 1:
                    unit(name, i)
                    for t in range(TT):
                        nc.vector.tensor_copy(mo[:, t, 512 * (i // 2):512 * (i // 2 + 1)], b[t][:]).then_inc(
                            S["emptied_dve"], mark("emptied_dve", (name, i - 1 + t)))
                elif name in ("ga", "gb"):
                    unit(name, i)
                    tile = ga if name == "ga" else gb
                    nc.vector.tensor_copy(tile[:, 2 * i:2 * i + 2, :], b[0][:].rearrange("p (n t) -> p n t", n=2)).then_inc(
                        S["emptied_dve"], mark("emptied_dve", (name, i)))
                elif name in ("bm", "ba"):
                    tile = ga if name == "bm" else gb
                    piece = tile[:, 2 * i:2 * i + 2, :]
                    dve.wait_ge(S["g_sig"], at("g_sig", 0 if name == "bm" else 1))
                    unit(name, i)
                    nc.vector.tensor_tensor(piece, b[0][:].rearrange("p (n t) -> p n t", n=2), piece, ALU.mult).then_inc(
                        S["emptied_dve"], mark("emptied_dve", (name, i)))
                    if name == "ba":
                        y = ga[:, 2 * i:2 * i + 2, :]
                        dve.wait_ge(S["emptied_dve"], at("emptied_dve", (name, i)))
                        nc.vector.tensor_tensor(y, y, piece, ALU.add).then_inc(S["y_ready"], mark("y_ready", i))
                        dve.wait_ge(S["y_hi"], at("y_hi", i))
                        nc.vector.tensor_tensor(xb_lo[:, 2 * i:2 * i + 2, :], y, xb_hi[:, 2 * i:2 * i + 2, :].bitcast(F32),
                                                    ALU.subtract).then_inc(S["y_lo"], mark("y_lo", i))
                elif name == "wo" and i % 2 == 1:
                    if i == 3:
                        dve.wait_ge(S["tile_done"], at("tile_done", "wo"))
                    else:
                        unit(name, i)
                    for t in range(TT):
                        if t == 1 and i == 3:
                            unit(name, i)
                        piece = x_res[:, t, 512 * (i // 2):512 * (i // 2 + 1)]
                        nc.vector.tensor_tensor(piece, b[t][:], piece, ALU.add).then_inc(
                            S["emptied_dve"], mark("emptied_dve", (name, i - 1 + t)))
                elif name == "up":
                    k0 = 4 * (i // 2 % 2) + 2 * (i % 2)
                    unit(name, i)
                    if i >= 2:
                        dve.wait_ge(S["ff_sq"], at("ff_sq", i - 2))
                    nc.vector.tensor_scalar(sq[:, i % 2, :], b[0][:], 0.0, None, ALU.max).then_inc(
                        S["emptied_dve"], mark("emptied_dve", (name, i)))
                    dve.wait_ge(S["ff_hi"], at("ff_hi", i))
                    nc.vector.tensor_tensor(xb_lo[:, k0:k0 + 2, :], sq[:, 2 + i % 2, :].rearrange("p (n t) -> p n t", n=2),
                                                xb_hi[:, k0:k0 + 2, :].bitcast(F32), ALU.subtract).then_inc(
                        S["ff_lo"], mark("ff_lo", i))
                elif name == "down" and i >= 14:
                    half = i - 14
                    for t in range(TT):
                        if half == 1 and t == 0:
                            dve.wait_ge(S["tile_done"], at("tile_done", "down"))
                        else:
                            unit(name, i)
                        piece = x_res[:, t, 512 * half:512 * half + 512]
                        nc.vector.tensor_tensor(piece, b[t][:], piece, ALU.add).then_inc(
                            S["mlp_added"], mark("mlp_added", (half, t)))

            split_lo(dve, 0, False)
            norm_dve(dve, "mix")
            turn_dve(dve, xa_hi, xa_lo, "mix", lambda k: col("norm_mix_g", l, k))
            split_lo(dve, 1, False)
            for u, (name, i, kind) in enumerate(units):
                if u + 2 < NU:
                    split_lo(dve, u + 2, False)
                take(name, i)
                if (name, i) == ("mqk", 0):
                    gate_split()
                elif (name, i) == ("mqk", 1):
                    conv((0, 1))
                elif (name, i) == ("mqk", 2):
                    conv((2, 3))
                elif (name, i) == ("mqk", 3):
                    conv((4, 5))
                elif (name, i) == ("mv", 0):
                    gate_start()
                    conv((6, 7))
                elif (name, i) == ("mv", 1):
                    gate_rows()
                elif (name, i) == ("aq", 1):
                    decay()
                elif (name, i) == ("aq", 2):
                    s_take(0)
                    s_take(1)
                elif (name, i) == ("aq", 3):
                    s_take(2)
                elif (name, i) == ("ak", 0):
                    s_take(3)
                elif (name, i) == ("mo", 1):
                    logits(0)
                    num_scale()
                elif (name, i) == ("mo", 2):
                    denominators(0)
                elif (name, i) == ("mo", 3):
                    ha_take(0)
                    logits(1)
                elif (name, i) == ("ga", 0):
                    denominators(1)
                elif (name, i) == ("ga", 1):
                    ha_take(1)
                    logits(2)
                elif (name, i) == ("ga", 2):
                    denominators(2)
                elif (name, i) == ("ga", 3):
                    ha_take(2)
                    logits(3)
                elif (name, i) == ("gb", 0):
                    denominators(3)
                elif (name, i) == ("gb", 1):
                    ha_take(3)
                    hm()
                elif (name, i) == ("gb", 3):
                    turn_dve(dve, xb_hi, xb_lo, "hm", lambda k: m_col(l, k))
                elif (name, i) == ("bm", 0):
                    turn_dve(dve, xa_hi, xa_lo, "ha", lambda k: 1.0)
                elif (name, i) == ("wo", 3):
                    norm_dve(dve, "mlp")
                    turn_dve(dve, xa_hi, xa_lo, "mlp", lambda k: col("norm_mlp_g", l, k))

        def layer_pool(pool, l):
            norm_pool(pool, "mix")
            nc.gpsimd.memset(mv[:, :, :, M_DV:VW], 1.0).then_inc(S["pads_ready"], mark("pads_ready", 0))
            nc.gpsimd.memset(mqk[:, :, 0:CONV_K - 1], 0.0).then_inc(S["pads_ready"], mark("pads_ready", 1))
            for k in range(4):
                pool.wait_ge(S["silu_sig"], at("silu_sig", k))
                for kk in (2 * k, 2 * k + 1):
                    nc.gpsimd.tensor_tensor(qk[:, kk, :], qk[:, kk, :], sig[:, kk, :], ALU.mult).then_inc(
                        S["silu"], mark("silu", kk))
            pool.wait_ge(S["z_ready"], at("z_ready", (3, 1)))
            nc.gpsimd.tensor_tensor(idle, eps_d[:, 0:1], eps_d[:, 0:1], ALU.add)
            for t in range(TT):
                pool.wait_ge(S["consts"], at("consts", "ident", "pre"))
                d = zw[:, :, 0:P] if t == 0 else zw[:, :, SEQ:384]
                nc.gpsimd.affine_select(out=d, in_=d, compare_op=ALU.is_ge, fill=NEG, base=0,
                                            pattern=[[0, M_HEADS], [1, P]], channel_multiplier=-1).then_inc(
                    S["z_masked"], mark("z_masked", t))
            pool.wait_ge(S["num_ssq"], at("num_ssq", (1, 3)))
            pool.wait_ge(S["den_rec"], at("den_rec"))
            nc.gpsimd.tensor_tensor(n_ms, n_rec, n_rec, ALU.mult).then_inc(S["num_norm"], mark("num_norm", 0))
            pool.wait_ge(S["num_norm"], at("num_norm", 0))
            nc.gpsimd.tensor_tensor(n_ms, n_ms, n_ss, ALU.mult).then_inc(S["num_norm"], mark("num_norm", 1))
            pool.wait_ge(S["num_norm"], at("num_norm", 1))
            nc.gpsimd.tensor_tensor(n_ms, n_ms, eps_v, ALU.add).then_inc(S["num_norm"], mark("num_norm", 2))
            pool.wait_ge(S["num_norm"], at("num_norm", 2))
            nc.gpsimd.tensor_tensor(n_ms, n_ms, minus_half[:, 0:8], ALU.pow).then_inc(S["num_norm"], mark("num_norm", 3))
            norm_pool(pool, "mlp")

        def start_pool(pool):
            counts.region = "pre"
            nc.gpsimd.memset(ident[:], 0.0).then_inc(S["consts"], mark("consts", "zero"))
            nc.gpsimd.memset(minus_half[:], -0.5).then_inc(S["unit_done"], mark("unit_done", "free", START[RING]))
            nc.gpsimd.memset(eps_d, D * EPS).then_inc(S["consts"], mark("consts", "eps_d"))
            nc.gpsimd.memset(zero_all, 0.0).then_inc(S["rows_used"], mark("rows_used", "free", GATHER))
            nc.gpsimd.memset(idle, 0.0).then_inc(S["rows_multiplied"], mark("rows_multiplied", "free", GATHER))
            nc.gpsimd.memset(eps_v, M_DV * EPS).then_inc(S["consts"], mark("consts", "eps_v"))
            nc.gpsimd.memset(gate_raw[:], 0.0).then_inc(S["consts"], mark("consts", "gate_raw"))
            pool.wait_ge(S["consts"], at("consts", "gate_raw"))
            nc.gpsimd.affine_select(out=ident[:], in_=ident[:], compare_op=ALU.not_equal, fill=1.0, base=0,
                                        pattern=[[-1, P]], channel_multiplier=1).then_inc(S["consts"], mark("consts", "ident"))
            nc.gpsimd.memset(scan_in[:, 0:1], 1.0).then_inc(S["consts"], mark("consts", "ones"))
            nc.gpsimd.memset(scan_in[:, 1:2], 0.0).then_inc(S["consts"], mark("consts", "zeros"))
            nc.gpsimd.memset(ak, 0.0).then_inc(S["consts"], mark("consts", "ak"))
            pool.wait_ge(S["params_loaded"], at("params_loaded", "sink"))
            nc.gpsimd.tensor_scalar(neg_sink[:], neg_sink[:], -1.0, None, ALU.mult).then_inc(
                S["consts"], mark("consts", "sink"))
            pool.wait_ge(S["toep_ready"], at("toep_ready", 1))
            nc.gpsimd.dma_start(A["toep"], toep.unsqueeze(1).broadcast_to([A_HEADS, P, 384])).then_inc(
                S["toep_stored"], mark("toep_stored", 0, 16))

        def start_pe(pe):
            counts.region = "pre"
            pe.wait_ge(S["params_loaded"], at("params_loaded", "sink"))
            pe.wait_ge(S["consts"], at("consts", "ident"))
            nc.tensor.transpose(att[0][:, 0:P], rows_p, ident[:])
            nc.tensor.transpose(att[1][:, 0:16], rows_m[0:16, :], ident[0:16, 0:16])
            nc.tensor.matmul(att[2][0:A_HEADS, 0:WINDOW], rel_sb, onehot, start=True, stop=True).then_inc(
                S["start_done"], mark("start_done"))

        def start_act(act):
            counts.region = "pre"
            act.wait_ge(S["x_loaded"], at("x_loaded"))

        def start_dve(dve):
            counts.region = "pre"
            nc.vector.memset(toep, NEG).then_inc(S["lo_ready"], mark("lo_ready", "free", RAW_RING))
            nc.vector.memset(small[:, 250:251], 0.0).then_inc(S["mlp_added"], mark("mlp_added", "start", 2 * TT))
            dve.wait_ge(S["start_done"], at("start_done"))
            nc.vector.tensor_copy(params[:], att[0][:, 0:P]).then_inc(S["start_taken"], mark("start_taken", 0))
            nc.vector.tensor_copy(params_m[:], att[1][:, 0:16]).then_inc(S["start_taken"], mark("start_taken", 1))
            dve.wait_ge(S["lo_ready"], at("lo_ready", "free"))
            dve.wait_ge(S["consts"], at("consts", "sink"))
            nc.vector.tensor_copy(toep[:, P:2 * P], att[2][0:A_HEADS, 0:WINDOW]).then_inc(
                S["toep_ready"], mark("toep_ready", 1))

        for i in range(2):
            BANKS["qa", i], BANKS["ka", i], BANKS["qb", i], BANKS["kb", i] = [acc[i]], [acc[2 + i]], [acc[2 + i]], [acc[i]]
            BANKS["va", i], BANKS["vb", i] = acc[0:2], acc[2:4]
        for i in range(4):
            BANKS["ga2", i] = BANKS["gb2", i] = [acc[i]]
            BANKS["yab", i] = acc[2 * (i % 2):2 * (i % 2) + 2]
            BANKS["mix", i] = acc[2 * (i // 2):2 * (i // 2) + 2]
        for i in range(8):
            BANKS["pq", i] = [acc[i % 2]]
        BEFORE2 = {("va", 0): [("qa", 0), ("qa", 1)], ("qb", 0): [("ka", 0)], ("qb", 1): [("ka", 1)],
                   ("kb", 0): [("va", 0)], ("kb", 1): [("va", 1)], ("vb", 0): [("qb", 0), ("qb", 1)],
                   ("ga2", 0): [("kb", 0)], ("ga2", 1): [("kb", 1)], ("ga2", 2): [("vb", 0)], ("ga2", 3): [("vb", 1)],
                   ("yab", 0): [("gb2", 0), ("gb2", 1)], ("yab", 1): [("gb2", 2), ("gb2", 3)],
                   ("yab", 2): [("yab", 0)], ("yab", 3): [("yab", 1)], ("mix", 0): [("yab", 2)], ("mix", 2): [("yab", 3)],
                   ("pq", 0): [("mix", 0)], ("pq", 1): [("mix", 1)]}
        for i in range(4):
            BEFORE2["gb2", i] = [("ga2", i)]
        for i in range(2, 8):
            BEFORE2["pq", i] = [("pq", i - 2)]
        odd_sums = [acc[2:4], acc[0:2]]
        BY_DVE2 = {"yab", "mix"}

        def emptied2(eng, name, i):
            eng.wait_ge(S["emptied_dve" if name in BY_DVE2 else "emptied_act"], at("emptied_dve" if name in BY_DVE2 else "emptied_act", (name, i)))

        PAIRS = H2 // 2
        FIRST_ATT = 3
        STEPS = [(tag, p) for tag in "ms" for p in range(PAIRS)]
        mx2, negm2, sums2, rinv2 = (small[:, 100 + 4 * i:104 + 4 * i] for i in range(4))

        def pair_at(u):
            n_, odd = divmod(u - FIRST_ATT, 2)
            if not 0 <= n_ < len(STEPS):
                return False, None, None
            return odd == 0, STEPS[n_], STEPS[n_ - 1] if n_ else None

        def second_pe(pe):
            def turn_norm(tag):
                turn_pe(pe, lambda k, t: hn[:, t, k * P:(k + 1) * P], tag, [("hn_ready", (tag, 0)), ("hn_ready", (tag, 1))])

            def scores(tag, p):
                q, k_ = (qa, ka) if tag == "m" else (qb, kb)
                emptied2(pe, "ka" if tag == "m" else "kb", 1)
                if (tag, p) == ("m", 0):
                    pe.wait_ge(S["x_lo"], at("x_lo", ("n1", KT - 1)))
                for e in range(2):
                    rows = slice(64 * e, 64 * e + 64)
                    nc.tensor.matmul(att[e][:, 0:P], q[rows, p, 0:P], k_[rows, p, 0:P], start=True, stop=True)
                    m = nc.tensor.matmul(att[e][:, P:3 * P], q[rows, p, P:2 * P], k_[rows, p, :], start=True, stop=True)
                m.then_inc(S["pair_scores"], mark("pair_scores", (tag, p)))

            def turned(tag, p):
                pe.wait_ge(S["pair_probs"], at("pair_probs", (tag, p)))
                if (tag, p) != STEPS[0]:
                    pe.wait_ge(S["y_ready2"], at("y_ready2", STEPS[STEPS.index((tag, p)) - 1]))
                for e in range(2):
                    for c in range(3):
                        m = nc.tensor.transpose(att[2 + e][:, c * P:(c + 1) * P], lg2[:, e, c * P:(c + 1) * P], ident[:])
                    m.then_inc(S["pair_turned"], mark("pair_turned", (tag, p, e)))

            def product(tag, p):
                v = va if tag == "m" else vb
                emptied2(pe, "va" if tag == "m" else "vb", 1)
                pe.wait_ge(S["pair_pT"], at("pair_pT", (tag, p, 1)))
                for e in range(2):
                    h = 2 * p + e
                    v0, v1 = v[:, 0, h * DH2:(h + 1) * DH2], v[:, 1, h * DH2:(h + 1) * DH2]
                    c0 = 3 * P + e * DH2
                    nc.tensor.matmul(att[2][:, c0:c0 + DH2], pT2[:, e, 0, :], v0, start=True, stop=True)
                    second = att[3][:, c0:c0 + DH2]
                    nc.tensor.matmul(second, pT2[:, e, 1, :], v0, start=True, stop=False)
                    m = nc.tensor.matmul(second, pT2[:, e, 2, :], v1, start=False, stop=True)
                m.then_inc(S["pair_done"], mark("pair_done", (tag, p)))

            def turn_y():
                pe.wait_ge(S["pair_pT"], at("pair_pT", ("s", PAIRS - 1, 1)))
                ready = ("y_ready2", ("s", PAIRS - 1))
                turn_pe(pe, lambda k, t: (ya if k < 4 else yb)[:, t, (k % 4) * P:(k % 4 + 1) * P], "y2", [ready, ready])

            def turn_keys():
                pe.wait_ge(S["keys_loaded"], at("keys_loaded", HP - 1))
                for b in range(4):
                    for i in range(4):
                        m = nc.tensor.transpose(att[b][:, i * P:(i + 1) * P], raw_keys[:, 4 * b + i, :], ident[:])
                    m.then_inc(S["keys_turned"], mark("keys_turned", b))

            def rank_keys(h):
                emptied2(pe, "pq", h)
                if h >= 2:
                    pe.wait_ge(S["rank_ready"], at("rank_ready", (h - 2, TT - 1)))
                else:
                    pe.wait_ge(S["x_lo"], at("x_lo", ("n2", KT - 1)))
                for t in range(TT):
                    for i in range(2):
                        m = nc.tensor.matmul(att[2 * t + h % 2][:, i * P:(i + 1) * P], queries[:, 2 * h + i, t * P:(t + 1) * P],
                                             keys[:, 2 * h + i, :], start=True, stop=True)
                    m.then_inc(S["rank_done"], mark("rank_done", (h, t)))

            def odd_rows(step):
                g = step - 2
                if g < 0:
                    return
                t = g // P_HEADS
                sums = odd_sums[t]
                if g % P_HEADS == 0:
                    if t == 0:
                        emptied2(pe, "mix", 3)
                    else:
                        emptied2(pe, "pq", P_HEADS - 1)
                for r in range(HEAD_ROUNDS):
                    for j in range(1, GATHER, 2):
                        pe.wait_ge(S[f"gathered{j}"], r * 16 + 16 * (v_block(g) * HEAD_ROUNDS + 1))
                        pe.wait_ge(S["diag_ready"], r * (GATHER // 2) + (g * P_TOP // 2 + j // 2 + 1))
                        first = (g % P_HEADS, r, j) == (0, 0, 1)
                        last = (g % P_HEADS, r, j) == (P_HEADS - 1, HEAD_ROUNDS - 1, GATHER - 1)
                        nc.tensor.matmul(sums[0][:], diag[j // 2 % 2], rows_ring[j][:, 0:512], start=first, stop=last)
                        nc.tensor.matmul(sums[1][:], diag[j // 2 % 2], rows_ring[j][:, 512:D], start=first,
                                         stop=last).then_inc(S["rows_multiplied"], 2)

            operand_ready = {("mix", 0): ("y_lo", 1), ("mix", 1): ("y_lo", 3)}
            turn_norm("n1")
            for u, (name, i, kind) in enumerate(units2):
                pe.wait_ge(S["lo_ready"], at("lo_ready", ("u2", u)))
                for p in BEFORE2.get((name, i), []):
                    emptied2(pe, *p)
                if (name, i) in operand_ready:
                    pe.wait_ge(S[operand_ready[name, i][0]], at(*operand_ready[name, i]))
                xh, xl = (xb_hi, xb_lo) if name in ("yab", "pq") else (xa_hi, xa_lo)
                b, s = BANKS[name, i], ring_slot(u, True)
                if kind == "F":
                    unit_f(b, s, xh, xl, ("u2", u), {("qa", 0): "n1", ("pq", 0): "n2"}.get((name, i)))
                elif kind == "Y":
                    unit_y(b, s, xh, xl, ("u2", u), "y2" if i == 0 else None)
                else:
                    unit_t(b, s, xh, xl, 4 * (i % 2), i % 2 == 0, i % 2 == 1, ("u2", u),
                           "mix" if (name, i) == ("mix", 3) else None)
                scored, pair, before = pair_at(u)
                if pair and scored:
                    if before:
                        product(*before)
                    scores(*pair)
                elif pair:
                    turned(*pair)
                if (name, i) == ("gb2", 3):
                    product(*STEPS[-1])
                    turn_y()
                elif (name, i) == ("mix", 0):
                    turn_keys()
                elif (name, i) == ("mix", 3):
                    pe.wait_ge(S["keys_ready"], at("keys_ready", 3))
                    turn_norm("n2")
                if (name, i) == ("pq", 0):
                    rank_keys(0)
                elif name == "pq" and i >= 2:
                    rank_keys(i - 1)
                    odd_rows(i - 2)
            rank_keys(P_HEADS - 1)
            for step in range(P_HEADS - 2, ALL_HEADS + 2):
                odd_rows(step)

        def second_act(act):
            def unit(name, i):
                act.wait_ge(S["unit_done"], at("unit_done", ("u2", at_unit2[name, i])))

            def weights(tag, p):
                if tag == "m":
                    act.wait_ge(S["pair_negm"], at("pair_negm", p))
                    for e in range(2):
                        for t in range(TT):
                            piece = lg2[:, e, 0:P] if t == 0 else lg2[:, e, P:3 * P]
                            last = (e, t) == (1, 1)
                            nc.scalar.activation(piece, piece, ACT.Exp, bias=negm2[:, 2 * t + e:2 * t + e + 1],
                                                     accum_out=sums2[:, 2 * t + e:2 * t + e + 1]).then_inc(
                                S["pair_probs" if last else "pair_part"], mark("pair_probs" if last else "pair_part", (tag, p) if last else (p, e, t)))
                else:
                    act.wait_ge(S["pair_scores"], at("pair_scores", (tag, p)))
                    if p >= 1:
                        act.wait_ge(S["pair_probs"], at("pair_probs", (tag, p - 1)))
                    for e in range(2):
                        nc.scalar.activation(stay[:, e, :], att[e][:, 0:384], ACT.Sigmoid, scale=-1.0).then_inc(
                            S["odds"], mark("odds", (p, e, 0)))
                        nc.scalar.activation(stop[:, e, :], att[e][:, 0:384], ACT.Sigmoid).then_inc(
                            S["odds"], mark("odds", (p, e, 1)))

            def probs_take(tag, p):
                n_ = STEPS.index((tag, p))
                if n_ >= 1:
                    act.wait_ge(S["pair_done"], at("pair_done", STEPS[n_ - 1]))
                for e in range(2):
                    act.wait_ge(S["pair_turned"], at("pair_turned", (tag, p, e)))
                    nc.scalar.copy(pT2[:, e, :, :], att[2 + e][:, 0:384].rearrange("p (c k) -> p c k", c=3)).then_inc(
                        S["pair_pT"], mark("pair_pT", (tag, p, e)))

            def keys_take():
                for b in range(4):
                    act.wait_ge(S["keys_turned"], at("keys_turned", b))
                    nc.scalar.copy(keys[:, 4 * b:4 * b + 4, :], att[b][:].rearrange("p (h n) -> p h n", h=4)).then_inc(
                        S["keys_ready"], mark("keys_ready", b))

            def rank_take(h):
                for t in range(TT):
                    act.wait_ge(S["rank_done"], at("rank_done", (h, t)))
                    nc.scalar.copy(rank[t][:, 2 * h:2 * h + 2, :],
                                       att[2 * t + h % 2][:, 0:2 * P].rearrange("p (i n) -> p i n", i=2)).then_inc(
                        S["rank_ready"], mark("rank_ready", (h, t)))

            def expert_weights(step):
                if step < ALL_HEADS:
                    w = weight[:, step * P_TOP:(step + 1) * P_TOP]
                    act.wait_ge(S["best_diff"], at("best_diff", step))
                    nc.scalar.activation(w, w, ACT.Exp, accum_out=wsum[:, step:step + 1]).then_inc(
                        S["best_exp"], mark("best_exp", step))
                g = step - 1
                if 0 <= g < ALL_HEADS:
                    d = dots[:, g * P_TOP:(g + 1) * P_TOP]
                    act.wait_ge(S["rows_used"], GATHER + (u_block(g) + 1) * P_TOP)
                    nc.scalar.activation(d, d, ACT.Gelu).then_inc(S["gelu_ready"], mark("gelu_ready", g))
                g = step - 2
                if g >= 0:
                    act.wait_ge(S["coef"], at("coef", g))
                    for r in range(HEAD_ROUNDS):
                        for j in range(1, GATHER, 2):
                            act.wait_ge(S["rows_multiplied"], r * GATHER + (GATHER + g * P_TOP + j - 3))
                            c = dots[:, g * P_TOP + r * GATHER + j:g * P_TOP + r * GATHER + j + 1]
                            nc.scalar.activation(diag[j // 2 % 2], ident[:], ACT.Copy, scale=c).then_inc(S["diag_ready"], 1)

            def take(name, i):
                b = BANKS[name, i]
                two = b[0][:].rearrange("p (n t) -> p n t", n=2)
                if name in ("qa", "qb"):
                    unit(name, i)
                    q = qa if name == "qa" else qb
                    nc.scalar.mul(q[:, 2 * i:2 * i + 2, :], two, DH2 ** -0.5).then_inc(
                        S["emptied_act"], mark("emptied_act", (name, i)))
                elif name in ("ka", "kb"):
                    unit(name, i)
                    k_ = ka if name == "ka" else kb
                    nc.scalar.copy(k_[:, 2 * i:2 * i + 2, :], two).then_inc(S["emptied_act"], mark("emptied_act", (name, i)))
                elif name in ("va", "vb") and i == 1:
                    unit(name, i)
                    v = va if name == "va" else vb
                    for t in range(TT):
                        nc.scalar.copy(v[:, t, :], b[t][:]).then_inc(S["emptied_act"], mark("emptied_act", (name, t)))
                elif name in ("ga2", "gb2"):
                    unit(name, i)
                    g = ga if name == "ga2" else gb
                    nc.scalar.activation(g[:, 2 * i:2 * i + 2, :], two, ACT.Sigmoid).then_inc(
                        S["emptied_act"], mark("emptied_act", (name, i)))
                elif name == "yab":
                    act.wait_ge(S["y_ready"], at("y_ready", i))
                    nc.scalar.copy(xa_hi[:, 2 * i:2 * i + 2, :], ga[:, 2 * i:2 * i + 2, :]).then_inc(S["y_hi"], mark("y_hi", i))
                elif name == "pq":
                    unit(name, i)
                    nc.scalar.copy(queries[:, 2 * i:2 * i + 2, :], two).then_inc(
                        S["emptied_act"], mark("emptied_act", (name, i)))

            split_hi(act, 0, True)
            norm_act(act, "fin")
            norm_act(act, "n1")
            turn_act(act, xa_hi, "n1", lambda k: col("norm1_g_2", 0, k))
            split_hi(act, 1, True)
            for u, (name, i, kind) in enumerate(units2):
                if u + 2 < len(units2) and (name, i) != ("pq", 0):
                    split_hi(act, u + 2, True)
                take(name, i)
                scored, pair, _ = pair_at(u)
                if pair and scored:
                    weights(*pair)
                elif pair:
                    probs_take(*pair)
                if (name, i) == ("gb2", 3):
                    turn_act(act, xb_hi, "y2", lambda k: 1.0)
                elif (name, i) == ("mix", 0):
                    keys_take()
                elif (name, i) == ("mix", 3):
                    norm_act(act, "n2")
                    split_hi(act, at_unit2["pq", 2], True)
                    turn_act(act, xb_hi, "n2", lambda k: col("norm2_g_2", 0, k))
                if (name, i) == ("pq", 0):
                    rank_take(0)
                elif name == "pq" and i >= 2:
                    rank_take(i - 1)
                    expert_weights(i - 2)
            rank_take(P_HEADS - 1)
            for step in range(P_HEADS - 2, ALL_HEADS + 2):
                expert_weights(step)
                if step == P_HEADS + 1:
                    act.wait_ge(S["g_last_loaded"], at("g_last_loaded"))
                    nc.scalar.mul(g_last, g_last, D ** 0.5).then_inc(S["g_scaled"], mark("g_scaled", "last"))
                if step == P_HEADS + 2:
                    last_norm_act(act, 0)
            last_norm_act(act, 1)

        def second_dve(dve):
            def unit(name, i):
                dve.wait_ge(S["unit_done"], at("unit_done", ("u2", at_unit2[name, i])))

            def logits(p):
                dve.wait_ge(S["pair_scores"], at("pair_scores", ("m", p)))
                dve.wait_ge(S["moba_bias"], at("moba_bias", 1))
                if p >= 1:
                    dve.wait_ge(S["pair_turned"], at("pair_turned", ("m", p - 1, 1)))
                for e in range(2):
                    for t, (c0, c1) in enumerate(((0, P), (P, 3 * P))):
                        nc.vector.tensor_tensor_reduce(out=lg2[:, e, c0:c1], in0=att[e][:, c0:c1], in1=moba_bias[:, 2 * p + e, c0:c1],
                                                       scale=1.0, scalar=LOWEST, op0=ALU.add, op1=ALU.max,
                                                       accum_out=mx2[:, 2 * t + e:2 * t + e + 1]).then_inc(
                            S["pair_mx"], mark("pair_mx", (p, e, t)))
                dve.wait_ge(S["pair_mx"], at("pair_mx", (p, 1, 1)))
                nc.vector.tensor_scalar(negm2, mx2, -1.0, None, ALU.mult).then_inc(S["pair_negm"], mark("pair_negm", p))

            def sticks(p):
                dve.wait_ge(S["odds_masked"], at("odds_masked", (p, 3)))
                for e in range(2):
                    for c0, c1 in ((0, P), (P, 3 * P)):
                        nc.vector.tensor_tensor_scan(left[:, e, c0:c1 - 1][:, ::-1], stay[:, e, c0 + 1:c1][:, ::-1],
                                                         zero_all[:, 0:1].broadcast_to([P, c1 - c0 - 1]), 1.0, ALU.mult, ALU.add).then_inc(
                            S["left_ready"], mark("left_ready", (p, e, c0)))
                dve.wait_ge(S["left_ready"], at("left_ready", (p, 1, P)))
                dve.wait_ge(S["pair_turned"], at("pair_turned", ("m", PAIRS - 1, 1) if p == 0 else ("s", p - 1, 1)))
                nc.vector.tensor_tensor(lg2[:, :, :], stop[:, :, :], left[:, :, :], ALU.mult).then_inc(
                    S["pair_probs"], mark("pair_probs", ("s", p)))

            def weights(tag, p):
                if tag == "m":
                    logits(p)
                else:
                    sticks(p)

            def y_take(tag, p):
                y = ya if tag == "m" else yb
                if tag == "m":
                    dve.wait_ge(S["pair_probs"], at("pair_probs", (tag, p)))
                    nc.vector.reciprocal(rinv2, sums2).then_inc(S["pair_rinv"], mark("pair_rinv", p))
                    dve.wait_ge(S["pair_rinv"], at("pair_rinv", p))
                dve.wait_ge(S["pair_done"], at("pair_done", (tag, p)))
                for t in range(TT):
                    dst = y[:, t, P * p:P * (p + 1)].rearrange("p (e d) -> p e d", e=2)
                    src = att[2 + t][:, 3 * P:4 * P].rearrange("p (e d) -> p e d", e=2)
                    if tag == "m":
                        ins = nc.vector.tensor_tensor(dst, src, rinv2[:, 2 * t:2 * t + 2].unsqueeze(2).broadcast_to([P, 2, DH2]),
                                                      ALU.mult)
                    else:
                        ins = nc.vector.tensor_copy(dst, src)
                    ins.then_inc(S["y_part" if t == 0 else "y_ready2"], mark("y_part" if t == 0 else "y_ready2", (tag, p)))

            def take(name, i):
                b = BANKS[name, i]
                if name == "yab":
                    unit(name, i)
                    for n_, g in enumerate((ga, gb)):
                        piece = g[:, 2 * i:2 * i + 2, :]
                        if n_ == 0:
                            dve.wait_ge(S["emptied_act"], at("emptied_act", ("gb2", 3)))
                        nc.vector.tensor_tensor(piece, b[n_][:].rearrange("p (n t) -> p n t", n=2), piece, ALU.mult).then_inc(
                            S["emptied_dve" if n_ == 1 else "y_part"], mark("emptied_dve" if n_ == 1 else "y_part", (name, i)))
                    y = ga[:, 2 * i:2 * i + 2, :]
                    dve.wait_ge(S["emptied_dve"], at("emptied_dve", (name, i)))
                    nc.vector.tensor_tensor(y, y, gb[:, 2 * i:2 * i + 2, :], ALU.add).then_inc(S["y_ready"], mark("y_ready", i))
                    dve.wait_ge(S["y_hi"], at("y_hi", i))
                    nc.vector.tensor_tensor(xa_lo[:, 2 * i:2 * i + 2, :], y, xa_hi[:, 2 * i:2 * i + 2, :].bitcast(F32),
                                                ALU.subtract).then_inc(S["y_lo"], mark("y_lo", i))
                elif name == "mix" and i % 2 == 1:
                    if i == 3:
                        dve.wait_ge(S["tile_done"], at("tile_done", "mix"))
                    else:
                        unit(name, i)
                    for t in range(TT):
                        if t == 1 and i == 3:
                            unit(name, i)
                        piece = x_res[:, t, 512 * (i // 2):512 * (i // 2 + 1)]
                        nc.vector.tensor_tensor(piece, b[t][:], piece, ALU.add).then_inc(
                            S["emptied_dve"], mark("emptied_dve", (name, i - 1 + t)))

            def route(t, h):
                def top16(lists):
                    for values, val, idx, key in lists:
                        nc.vector.max(val[:, 0:8], values).then_inc(S["top8"], mark("top8", (t, h, key)))
                    for values, val, idx, key in lists:
                        dve.wait_ge(S["top8"], at("top8", (t, h, key)))
                        nc.vector.max_index(idx[:, 0:8], val[:, 0:8], values).then_inc(S["top8_at"], mark("top8_at", (t, h, key)))
                    for values, val, idx, key in lists:
                        dve.wait_ge(S["top8_at"], at("top8_at", (t, h, key)))
                        nc.vector.match_replace(values, val[:, 0:8], values, LOWEST).then_inc(
                            S["top8_out"], mark("top8_out", (t, h, key)))
                    for values, val, idx, key in lists:
                        dve.wait_ge(S["top8_out"], at("top8_out", (t, h, key)))
                        nc.vector.max(val[:, 8:16], values).then_inc(S["next8"], mark("next8", (t, h, key)))
                    for values, val, idx, key in lists:
                        dve.wait_ge(S["next8"], at("next8", (t, h, key)))
                        nc.vector.max_index(idx[:, 8:16], val[:, 8:16], values).then_inc(
                            S["next8_at"], mark("next8_at", (t, h, key)))

                dve.wait_ge(S["iota"], at("iota", 1))
                dve.wait_ge(S["rank_ready"], at("rank_ready", (h, t)))
                top16([(rank[t][:, 2 * h + i, :], top_s[:, i, :], top_i[:, i, :], i) for i in range(2)])
                dve.wait_ge(S["next8_at"], at("next8_at", (t, h, 1)))
                nc.vector.tensor_copy(top_f, top_i).then_inc(S["top_f"], mark("top_f", (t, h)))
                nc.vector.tensor_tensor(cand, top_s[:, 0, :].unsqueeze(2).broadcast_to([P, P_TOP, P_TOP]),
                                            top_s[:, 1, :].unsqueeze(1).broadcast_to([P, P_TOP, P_TOP]), ALU.add).then_inc(
                    S["cand"], mark("cand", (t, h)))
                dve.wait_ge(S["cand"], at("cand", (t, h)))
                top16([(cand.rearrange("p a b -> p (a b)"), best[:, t * P_HEADS + h, :], pos, 2)])
                dve.wait_ge(S["next8_at"], at("next8_at", (t, h, 2)))
                nc.vector.tensor_scalar(pos_i[:, 0, :], pos, 4, None, ALU.logical_shift_right).then_inc(
                    S["pos_i"], mark("pos_i", (t, h, 0)))
                nc.vector.tensor_scalar(pos_i[:, 1, :], pos, P_TOP - 1, None, ALU.bitwise_and).then_inc(
                    S["pos_i"], mark("pos_i", (t, h, 1)))
                dve.wait_ge(S["pos_i"], at("pos_i", (t, h, 1)))
                nc.vector.tensor_copy(pos_f, pos_i).then_inc(S["pos_f"], mark("pos_f", (t, h)))
                dve.wait_ge(S["pos_f"], at("pos_f", (t, h)))
                for i in range(2):
                    nc.vector.tensor_tensor(pick[:, i], pos_f[:, i, :].unsqueeze(2).broadcast_to([P, P_TOP, P_TOP]),
                                                iota16.unsqueeze(1).broadcast_to([P, P_TOP, P_TOP]), ALU.is_equal).then_inc(
                        S["pick"], mark("pick", (t, h, i)))
                dve.wait_ge(S["pick"], at("pick", (t, h, 1)))
                for i in range(2):
                    nc.vector.tensor_tensor(pick[:, i], pick[:, i], top_f[:, i, :].unsqueeze(1).broadcast_to([P, P_TOP, P_TOP]),
                                                ALU.mult).then_inc(S["picked"], mark("picked", (t, h, i)))
                dve.wait_ge(S["picked"], at("picked", (t, h, 1)))
                nc.vector.tensor_reduce(both_f, pick, X, ALU.add).then_inc(S["both_f"], mark("both_f", (t, h)))
                dve.wait_ge(S["both_f"], at("both_f", (t, h)))
                nc.vector.scalar_tensor_tensor(expert_f, both_f[:, 0, :], float(P_KEYS), both_f[:, 1, :], ALU.mult, ALU.add).then_inc(
                    S["expert_f"], mark("expert_f", (t, h)))
                dve.wait_ge(S["expert_f"], at("expert_f", (t, h)))
                c = t * SLOTS + h * P_TOP
                nc.vector.tensor_copy(expert[:, c:c + P_TOP], expert_f).then_inc(
                    S["expert_ready"], mark("expert_ready", (t, h)))

            def diff(g):
                nc.vector.tensor_scalar(weight[:, g * P_TOP:(g + 1) * P_TOP], best[:, g, :], best[:, g, 0:1], None,
                                        ALU.subtract).then_inc(S["best_diff"], mark("best_diff", g))

            def coefficients(g):
                d, w = dots[:, g * P_TOP:(g + 1) * P_TOP], weight[:, g * P_TOP:(g + 1) * P_TOP]
                dve.wait_ge(S["best_exp"], at("best_exp", g))
                nc.vector.reciprocal(wsum[:, g:g + 1], wsum[:, g:g + 1]).then_inc(S["wrec"], mark("wrec", g))
                dve.wait_ge(S["wrec"], at("wrec", g))
                dve.wait_ge(S["gelu_ready"], at("gelu_ready", g))
                nc.vector.scalar_tensor_tensor(d, d, wsum[:, g:g + 1], w, ALU.mult, ALU.mult).then_inc(
                    S["coef"], mark("coef", g))

            def u_rows(g, unit_to_split):
                t = g // P_HEADS
                dve.wait_ge(S["xn_ready"], at("xn_ready", t))
                for r in range(HEAD_ROUNDS):
                    if r == HEAD_ROUNDS // 2 and unit_to_split is not None:
                        split_lo(dve, unit_to_split, True)
                    for j in range(GATHER):
                        dve.wait_ge(S[f"gathered{j}"], r * 16 + 16 * (u_block(g) * HEAD_ROUNDS + 1))
                        dot = dots[:, g * P_TOP + r * GATHER + j:g * P_TOP + r * GATHER + j + 1]
                        nc.vector.scalar_tensor_tensor(rows_ring[j], rows_ring[j], 1.0, hn[:, t, :], ALU.mult, ALU.mult,
                                                       accum_out=dot).then_inc(S["rows_used"], 1)

            def v_rows(g):
                t = g // P_HEADS
                dve.wait_ge(S["coef"], at("coef", g))
                for r in range(HEAD_ROUNDS):
                    for j in range(0, GATHER, 2):
                        dve.wait_ge(S[f"gathered{j}"], r * 16 + 16 * (v_block(g) * HEAD_ROUNDS + 1))
                        dve.wait_ge(S["rows_used"], r * GATHER + (GATHER + v_block(g) * P_TOP + j))
                        c = dots[:, g * P_TOP + r * GATHER + j:g * P_TOP + r * GATHER + j + 1]
                        nc.vector.scalar_tensor_tensor(x_res[:, t, :], rows_ring[j], c, x_res[:, t, :], ALU.mult,
                                                       ALU.add).then_inc(S["rows_used"], 2)

            def experts(step, unit_to_split=None):
                if step < ALL_HEADS:
                    route(step // P_HEADS, step % P_HEADS)
                    diff(step)
                if 1 <= step <= ALL_HEADS:
                    u_rows(step - 1, unit_to_split)
                if step >= 2:
                    coefficients(step - 2)
                    if step == P_HEADS + 2:
                        v_sum(0)
                    v_rows(step - 2)

            def last_norm_dve(t):
                dve.wait_ge(S["g_scaled"], at("g_scaled", "last"))
                dve.wait_ge(S["rstd_ready"], at("rstd_ready", ("last", t)))
                nc.vector.scalar_tensor_tensor(x_res[:, t, :], x_res[:, t, :], rstd[:, t:t + 1], g_last, ALU.mult, ALU.mult).then_inc(
                    S["final_ready"], mark("final_ready", t))

            def v_sum(t):
                dve.wait_ge(S["rows_multiplied"], GATHER + (t + 1) * SLOTS)
                dve.wait_ge(S["rows_used"], GATHER + (v_block((t + 1) * P_HEADS - 1) + 1) * P_TOP)
                for n_ in range(2):
                    piece = x_res[:, t, 512 * n_:512 * (n_ + 1)]
                    nc.vector.tensor_tensor(piece, odd_sums[t][n_][:], piece, ALU.add).then_inc(
                        S["x_peer"], mark("x_peer", (t, n_)))

            def peer_norm():
                norm_dve(dve, "n2")
                split_lo(dve, at_unit2["pq", 1], True)
                turn_dve(dve, xb_hi, xb_lo, "n2", lambda k: col("norm2_g_2", 0, k))
                split_lo(dve, at_unit2["pq", 2], True)
                dve.wait_ge(S["g_loaded"], at("g_loaded", "n2"))
                for t in range(TT):
                    nc.vector.tensor_tensor(hn[:, t, :], hn[:, t, :], g_row, ALU.mult).then_inc(
                        S["xn_ready"], mark("xn_ready", t))

            split_lo(dve, 0, True)
            dve.wait_ge(S["g_scaled"], at("g_scaled", "fin"))
            for t in range(TT):
                dve.wait_ge(S["rstd_ready"], at("rstd_ready", ("fin", t)))
                nc.vector.scalar_tensor_tensor(x_res[:, t, :], x_res[:, t, :], rstd[:, t:t + 1], g_row, ALU.mult, ALU.mult).then_inc(
                    S["x_fin"], mark("x_fin", t))
            norm_dve(dve, "n1")
            turn_dve(dve, xa_hi, xa_lo, "n1", lambda k: col("norm1_g_2", 0, k))
            split_lo(dve, 1, True)
            for u, (name, i, kind) in enumerate(units2):
                later = u + 2 if u + 2 < len(units2) else None
                if later and ((name, i) == ("pq", 1) or later <= at_unit2["pq", 0]):
                    split_lo(dve, later, True)
                take(name, i)
                scored, pair, before = pair_at(u)
                if pair and scored:
                    if before:
                        y_take(*before)
                    weights(*pair)
                if (name, i) == ("gb2", 3):
                    y_take(*STEPS[-1])
                    turn_dve(dve, xb_hi, xb_lo, "y2", lambda k: 1.0)
                elif (name, i) == ("mix", 3):
                    peer_norm()
                if (name, i) == ("pq", 0):
                    experts(0)
                elif name == "pq" and i >= 2:
                    experts(i - 1, later)
            for step in range(P_HEADS - 1, ALL_HEADS + 2):
                experts(step)
                if step == P_HEADS + 4:
                    last_norm_dve(0)
            v_sum(1)
            last_norm_dve(1)

        def second_pool(pool):
            pool.wait_ge(S["g_loaded"], at("g_loaded", "fin"))
            nc.gpsimd.tensor_scalar(g_row, g_row, D ** 0.5, None, ALU.mult).then_inc(S["g_scaled"], mark("g_scaled", "fin"))
            norm_pool(pool, "fin")
            norm_pool(pool, "n1")
            for t in range(TT):
                dst = dist_i[:, 0:P] if t == 0 else dist_i[:, P:3 * P]
                nc.gpsimd.iota(dst, pattern=[[1, P * (t + 1)]], base=-P * t, channel_multiplier=-1).then_inc(
                    S["dist"], mark("dist", t))
            pool.wait_ge(S["dist"], at("dist", 1))
            nc.gpsimd.tensor_copy(dist, dist_i).then_inc(S["dist"], mark("dist", 2))
            pool.wait_ge(S["dist"], at("dist", 2))
            for h in range(H2):
                nc.gpsimd.tensor_scalar(moba_bias[:, h, :], dist, 2.0 ** (-8.0 * (h + 1) / H2), None, ALU.mult).then_inc(
                    S["alibi"], mark("alibi", h))
            pool.wait_ge(S["alibi"], at("alibi", H2 - 1))
            for t in range(TT):
                d = moba_bias[:, :, 0:P] if t == 0 else moba_bias[:, :, 2 * P:3 * P]
                nc.gpsimd.affine_select(out=d, in_=d, compare_op=ALU.is_ge, fill=NEG, base=0,
                                            pattern=[[0, H2], [-1, P]], channel_multiplier=1).then_inc(
                    S["moba_bias"], mark("moba_bias", t))
            for c in (P - 1, 3 * P - 1):
                nc.gpsimd.memset(left[:, :, c:c + 1], 1.0).then_inc(S["left_one"], mark("left_one", c))
            for p in range(PAIRS):
                pool.wait_ge(S["left_one"], at("left_one", 3 * P - 1))
                pool.wait_ge(S["odds"], at("odds", (p, 1, 1)))
                n_ = 0
                for tile, fill in ((stay, 1.0), (stop, 0.0)):
                    for t in range(TT):
                        d = tile[:, :, 0:P] if t == 0 else tile[:, :, 2 * P:3 * P]
                        nc.gpsimd.affine_select(out=d, in_=d, compare_op=ALU.is_ge, fill=fill, base=-1,
                                                    pattern=[[0, 2], [-1, P]], channel_multiplier=1).then_inc(
                            S["odds_masked"], mark("odds_masked", (p, n_)))
                        n_ += 1
            norm_pool(pool, "n2")
            nc.gpsimd.iota(iota_i, pattern=[[1, P_TOP]], base=0, channel_multiplier=0).then_inc(S["iota"], mark("iota", 0))
            pool.wait_ge(S["iota"], at("iota", 0))
            nc.gpsimd.tensor_copy(iota16, iota_i).then_inc(S["iota"], mark("iota", 1))

            def gather(w, g, place, v_done):
                for n_ in range(P_TOP):
                    j = n_ % GATHER
                    pool.wait_ge(S["rows_used"], place * P_TOP + n_ + 1)
                    if w is peer_v and n_ >= GATHER:
                        pool.wait_ge(S["rows_multiplied"], v_done * P_TOP + n_ + 1)
                    elif n_ < GATHER:
                        pool.wait_ge(S["rows_multiplied"], v_done * P_TOP + n_ + 1)
                    c = g * P_TOP + n_
                    nc.gpsimd.indirect_dma_start(
                        rows_ring[j], None, w, bass.IndirectOffsetOnAxis(ap=expert[:, c:c + 1], axis=0)
                    ).then_inc(S[f"gathered{j}"], 16)

            peer_u, peer_v = A["peer_u_2"][0], A["peer_v_2"][0]
            for step in range(1, ALL_HEADS + 2):
                if step <= ALL_HEADS:
                    pool.wait_ge(S["expert_ready"], at("expert_ready", ((step - 1) // P_HEADS, (step - 1) % P_HEADS)))
                    gather(peer_u, step - 1, u_block(step - 1), max(0, step - 2))
                if step >= 2:
                    gather(peer_v, step - 2, v_block(step - 2), step - 2)
                if step == P_HEADS + 4:
                    last_norm_pool(pool, 0)
            last_norm_pool(pool, 1)

        block = ctx.enter_context(nc.Block())

        @block.sync
        def _(sp):
            sync_program(sp)

        @block.gpsimd
        def _(pool):
            start_pool(pool)
            counts.region = "layer"
            with pool.Fori(0, DEPTH) as l:
                counts.layer = l
                layer_pool(pool, l)
            counts.region, counts.layer = "post", None
            second_pool(pool)

        @block.scalar
        def _(act):
            start_act(act)
            counts.region = "layer"
            with act.Fori(0, DEPTH) as l:
                counts.layer = l
                layer_act(act, l)
            counts.region, counts.layer = "post", None
            second_act(act)

        @block.vector
        def _(dve):
            start_dve(dve)
            counts.region = "layer"
            with dve.Fori(0, DEPTH) as l:
                counts.layer = l
                layer_dve(dve, l)
            counts.region, counts.layer = "post", None
            second_dve(dve)

        @block.tensor
        def _(pe):
            start_pe(pe)
            counts.region = "layer"
            with pe.Fori(0, DEPTH) as l:
                counts.layer = l
                layer_pe(pe, l)
            counts.region, counts.layer = "post", None
            second_pe(pe)
    return counts


INPUTS = ["x", "norm_mix_g", "w_in", "conv_w", "conv_b", "b_igate", "b_fgate", "mlstm_norm_g", "attn_sinks", "rel_bias",
          "w_branch_m", "w_branch_a", "w_out", "norm_mlp_g", "w_up", "w_down", "final_norm_g", "norm1_g_2", "w_in_2",
          "w_out_moba_2", "w_out_sb_2", "w_mix_out_2", "norm2_g_2", "peer_w_q_2", "peer_sub_keys_2", "peer_u_2", "peer_v_2",
          "final_norm_g_2"]


def kernel(**inputs):
    import concourse.bacc as bacc
    from concourse.bass_utils import run_bass_kernel_spmd

    arrays = {f"in_{n}": np.ascontiguousarray(inputs[n]) for n in INPUTS}
    arrays["in_onehot"] = bucket_onehot()
    known = None
    for _ in range(2):
        nc = bacc.Bacc("TRN2", target_bir_lowering=False, num_devices=1)
        A = {n[3:]: nc.dram_tensor(n, a.shape, F32, kind="ExternalInput").ap() for n, a in arrays.items()}
        A["toep"] = nc.dram_tensor("toep", [A_HEADS, P, 384], F32, kind="Internal").ap()
        out = nc.dram_tensor("out", inputs["x"].shape, F32, kind="ExternalOutput").ap()
        known = build(nc, A, out, known)
    r = run_bass_kernel_spmd(nc, [arrays], core_ids=[0])
    return r.results[0]["out"]
```
